# Optimizing a Trainium2 kernel written in Bass

```python
import jax, jax.numpy as jnp
from jax import lax
import numpy as np

D_MODEL = 1024
BATCH = 1
SEQ = 128
DEPTH = 1
DEC_BATCH = 1
DEC_SEQ = 1024
PAST_LEN = 128

GRID_W = 64
D_RWKV = 512
HEAD_SIZE = 64
N_HEADS_RWKV = D_RWKV // HEAD_SIZE
D_DECAY_LORA = 64
D_ICLR_LORA = 64
D_GATE_LORA = 128
N_DIR = 2
GN_EPS = 64e-5
D_POOL = D_MODEL - D_RWKV
POOL_WINDOWS = (2, 4, 8, 16)
N_POOL_GROUPS = len(POOL_WINDOWS)
POOL_GROUP = D_POOL // N_POOL_GROUPS
N_EXPERTS = 16
CAPACITY_FACTOR = 2
D_EXPERT = 2 * D_MODEL
N_MOD = 6
RMS_EPS = 1e-6
OFF_K = D_RWKV
OFF_V = 2 * D_RWKV
OFF_G = 3 * D_RWKV
OFF_W = OFF_G + D_GATE_LORA
OFF_A = OFF_W + N_DIR * D_DECAY_LORA
OFF_POOL = OFF_A + N_DIR * D_ICLR_LORA
D_IN = OFF_POOL + D_POOL

kernel_name = 'hybrid_rwkv7_pool_ecmoe_diffusion_step'

def rms_norm(x, gain):
    x32 = x.astype(jnp.float32)
    y = x32 * lax.rsqrt(jnp.mean(x32 * x32, axis=-1, keepdims=True) + RMS_EPS)
    return (y * gain.astype(jnp.float32)).astype(x.dtype)

def centred_shift(z):
    prev = jnp.pad(z[:, :-1], ((0, 0), (1, 0), (0, 0)))
    nxt = jnp.pad(z[:, 1:], ((0, 0), (0, 1), (0, 0)))
    return 0.5 * (prev + nxt) - z

def box_sum(z, window, axis):
    n = z.shape[axis]
    pad = [(0, 0)] * z.ndim
    pad[axis] = (1, 0)
    cs = jnp.pad(jnp.cumsum(z, axis=axis), pad)
    lo = window // 2
    hi = window - 1 - lo
    pos = np.arange(n)
    start = np.clip(pos - lo, 0, n)
    end = np.clip(pos + hi + 1, 0, n)
    s = jnp.take(cs, end, axis=axis) - jnp.take(cs, start, axis=axis)
    return s, (end - start).astype(np.float32)

def multiscale_pool(z, pool_w, pool_scale, use_grid):
    b, t, _ = z.shape
    z32 = z.astype(jnp.float32).reshape(b, t, N_POOL_GROUPS, POOL_GROUP)
    outs = []
    for gi, win in enumerate(POOL_WINDOWS):
        zg = z32[:, :, gi]
        if use_grid:
            rows = t // GRID_W
            s, cnt_c = box_sum(zg.reshape(b, rows, GRID_W, POOL_GROUP), win, 2)
            s, cnt_r = box_sum(s, win, 1)
            cnt = (cnt_r[:, None] * cnt_c[None, :])[None, :, :, None]
            mean = (s / cnt).reshape(b, t, POOL_GROUP)
        else:
            s, cnt = box_sum(zg, win, 1)
            mean = s / cnt[None, :, None]
        outs.append(mean - zg)
    d = jnp.stack(outs, axis=2).astype(z.dtype)
    y = jnp.einsum('btgc,gcd->btgd', d, pool_w).reshape(b, t, D_POOL)
    return y * pool_scale

def wkv_scan(s0, r, w, k, v, kk, kka, reverse):
    xs = tuple(jnp.moveaxis(u, 1, 0) for u in (r, w, k, v, kk, kka))

    def step(s, inp):
        r_t, w_t, k_t, v_t, kk_t, b_t = inp
        sa = jnp.einsum('bhvk,bhk->bhv', s, kk_t)
        s = (s * w_t[:, :, None, :] - sa[..., None] * b_t[:, :, None, :]
             + v_t[..., None] * k_t[:, :, None, :])
        y = jnp.einsum('bhvk,bhk->bhv', s, r_t)
        return s, y

    s_fin, ys = lax.scan(step, s0.astype(jnp.float32), xs, reverse=reverse)
    return s_fin, jnp.moveaxis(ys, 0, 1)

def rwkv7_bidir(p, s0, mu_shift, w0, w_up, a0, a_up, g_up, k_k, k_a, r_k, ln_x_w, ln_x_b):
    b, t, _ = p.shape
    z = p[..., :OFF_POOL]
    z = (z + mu_shift * centred_shift(z)).astype(jnp.float32)
    r = z[..., :OFF_K]
    k = z[..., OFF_K:OFF_V]
    v = z[..., OFF_V:OFF_G]
    gd = z[..., OFF_G:OFF_W]
    wd = z[..., OFF_W:OFF_A].reshape(b, t, N_DIR, D_DECAY_LORA)
    ad = z[..., OFF_A:OFF_POOL].reshape(b, t, N_DIR, D_ICLR_LORA)
    w_log = -jax.nn.softplus(-(w0 + jnp.einsum('btdr,drc->btdc', jnp.tanh(wd), w_up))) - 0.5
    decay = jnp.exp(-jnp.exp(w_log))
    a = jax.nn.sigmoid(a0 + jnp.einsum('btdr,drc->btdc', ad, a_up))
    g = jnp.einsum('btr,rc->btc', jax.nn.sigmoid(gd), g_up)

    def heads(u):
        return u.reshape(u.shape[:-1] + (N_HEADS_RWKV, HEAD_SIZE))

    kk = heads(k * k_k)
    kk = kk / jnp.maximum(jnp.sqrt(jnp.sum(kk * kk, axis=-1, keepdims=True)), 1e-12)
    k_dir = heads(k[:, :, None, :] * (1.0 + (a - 1.0) * k_a))
    rh, vh, ah, wh = heads(r), heads(v), heads(a), heads(decay)
    s_f, y_f = wkv_scan(s0[:, 0], rh, wh[:, :, 0], k_dir[:, :, 0], vh, kk, kk * ah[:, :, 0], False)
    s_b, y_b = wkv_scan(s0[:, 1], rh, wh[:, :, 1], k_dir[:, :, 1], vh, kk, kk * ah[:, :, 1], True)
    y = y_f + y_b
    mu = jnp.mean(y, axis=-1, keepdims=True)
    var = jnp.mean(jnp.square(y - mu), axis=-1, keepdims=True)
    y = ((y - mu) * lax.rsqrt(var + GN_EPS)).reshape(b, t, D_RWKV) * ln_x_w + ln_x_b
    bonus = jnp.einsum('bthn,btdhn,hn->bth', rh, k_dir,
                       r_k.reshape(N_HEADS_RWKV, HEAD_SIZE).astype(jnp.float32))[..., None] * vh
    y = (y + bonus.reshape(b, t, D_RWKV)) * g
    return y.astype(p.dtype), jnp.stack([s_f, s_b], axis=1)

def expert_choice_ffn(h, w_router, w1, w3, w2):
    bn, t, d = h.shape
    hf = h.reshape(-1, d)
    n_tok = hf.shape[0]
    cap = CAPACITY_FACTOR * n_tok // N_EXPERTS
    probs = jax.nn.softmax((hf @ w_router).astype(jnp.float32), axis=-1)
    gate, idx = lax.top_k(probs.T, cap)
    xe = hf[idx]
    he = jax.nn.silu(jnp.einsum('ecd,edf->ecf', xe, w1)) * jnp.einsum('ecd,edf->ecf', xe, w3)
    ye = jnp.einsum('ecf,efd->ecd', he, w2) * gate[..., None].astype(h.dtype)
    out = jnp.zeros((n_tok, d), ye.dtype).at[idx.reshape(-1)].add(ye.reshape(-1, d))
    return out.reshape(bn, t, d).astype(h.dtype)

def trunk_layer(x, cvec, s0, use_grid, norm1, norm2, ada_w, ada_b, w_in, mu_shift, w0, w_up,
                a0, a_up, g_up, k_k, k_a, r_k, ln_x_w, ln_x_b, pool_w, pool_scale, w_out,
                w_router, w1, w3, w2):
    mod = jnp.einsum('bd,de->be', jax.nn.silu(cvec), ada_w) + ada_b
    sh1, sc1, gt1, sh2, sc2, gt2 = jnp.split(mod[:, None, :], N_MOD, axis=-1)
    h = rms_norm(x, norm1) * (1.0 + sc1) + sh1
    p = h @ w_in
    y_rwkv, s_fin = rwkv7_bidir(p, s0, mu_shift, w0, w_up, a0, a_up, g_up, k_k, k_a, r_k,
                                ln_x_w, ln_x_b)
    y_pool = multiscale_pool(p[..., OFF_POOL:], pool_w, pool_scale, use_grid)
    m = jnp.concatenate([y_rwkv, y_pool.astype(y_rwkv.dtype)], axis=-1) @ w_out
    x = x + gt1 * m
    h = rms_norm(x, norm2) * (1.0 + sc2) + sh2
    x = x + gt2 * expert_choice_ffn(h, w_router, w1, w3, w2)
    return x, s_fin

def setup_inputs(seed: int = 0) -> dict:
    key = jax.random.key(seed)
    ks = jax.random.split(key, 32)
    f32 = jnp.float32
    L = DEPTH
    D = D_MODEL

    def nrm(k, shape, s):
        return jax.random.normal(k, shape, f32) * s

    return {
        'x_prompt': nrm(ks[0], (BATCH, SEQ, D), 1.0),
        'x_sample': nrm(ks[1], (DEC_BATCH, DEC_SEQ, D), 1.0),
        'state_rwkv': nrm(ks[2], (DEC_BATCH, L, N_DIR, N_HEADS_RWKV, HEAD_SIZE, HEAD_SIZE), 0.3),
        'c': nrm(ks[3], (DEC_BATCH, D), 1.0),
        'c_ctx': nrm(ks[4], (D,), 1.0),
        'norm1': 1.0 + nrm(ks[5], (L, D), 0.05),
        'norm2': 1.0 + nrm(ks[6], (L, D), 0.05),
        'norm_f': 1.0 + nrm(ks[7], (D,), 0.05),
        'ada_w': nrm(ks[8], (L, D, N_MOD * D), 0.5 * D ** -0.5),
        'ada_b': nrm(ks[9], (L, N_MOD * D), 0.05),
        'w_in': nrm(ks[10], (L, D, D_IN), D ** -0.5),
        'mu_shift': 0.5 + nrm(ks[11], (L, OFF_POOL), 0.1),
        'w0': -1.0 + nrm(ks[12], (L, N_DIR, D_RWKV), 0.5),
        'w_up': nrm(ks[13], (L, N_DIR, D_DECAY_LORA, D_RWKV), 0.1 * D_DECAY_LORA ** -0.5),
        'a0': nrm(ks[14], (L, N_DIR, D_RWKV), 0.5),
        'a_up': nrm(ks[15], (L, N_DIR, D_ICLR_LORA, D_RWKV), 0.1 * D_ICLR_LORA ** -0.5),
        'g_up': nrm(ks[16], (L, D_GATE_LORA, D_RWKV), D_GATE_LORA ** -0.5),
        'k_k': 0.85 + nrm(ks[17], (L, D_RWKV), 0.05),
        'k_a': 1.0 + nrm(ks[18], (L, D_RWKV), 0.05),
        'r_k': nrm(ks[19], (L, D_RWKV), 0.1),
        'ln_x_w': 1.0 + nrm(ks[20], (L, D_RWKV), 0.05),
        'ln_x_b': nrm(ks[21], (L, D_RWKV), 0.02),
        'pool_w': nrm(ks[22], (L, N_POOL_GROUPS, POOL_GROUP, POOL_GROUP), POOL_GROUP ** -0.5),
        'pool_scale': 1.0 + nrm(ks[23], (L, D_POOL), 0.05),
        'w_out': nrm(ks[24], (L, D, D), D ** -0.5),
        'w_router': nrm(ks[25], (L, D, N_EXPERTS), D ** -0.5),
        'w1': nrm(ks[26], (L, N_EXPERTS, D, D_EXPERT), D ** -0.5),
        'w3': nrm(ks[27], (L, N_EXPERTS, D, D_EXPERT), D ** -0.5),
        'w2': nrm(ks[28], (L, N_EXPERTS, D_EXPERT, D), D_EXPERT ** -0.5),
    }

def reference(x_prompt, x_sample, state_rwkv, c, c_ctx, norm1, norm2, norm_f, ada_w, ada_b,
              w_in, mu_shift, w0, w_up, a0, a_up, g_up, k_k, k_a, r_k, ln_x_w, ln_x_b,
              pool_w, pool_scale, w_out, w_router, w1, w3, w2):
    def run_layer(x, cvec, s0, use_grid, l):
        return trunk_layer(x, cvec, s0, use_grid, norm1[l], norm2[l], ada_w[l], ada_b[l],
                           w_in[l], mu_shift[l], w0[l], w_up[l], a0[l], a_up[l], g_up[l],
                           k_k[l], k_a[l], r_k[l], ln_x_w[l], ln_x_b[l], pool_w[l],
                           pool_scale[l], w_out[l], w_router[l], w1[l], w3[l], w2[l])

    b_ctx = x_prompt.shape[0]
    zero_state = jnp.zeros((b_ctx, N_DIR, N_HEADS_RWKV, HEAD_SIZE, HEAD_SIZE), jnp.float32)
    x = x_prompt
    ctx_states = []
    for l in range(DEPTH):
        x, s_fin = run_layer(x, c_ctx[None, :], zero_state, False, l)
        ctx_states.append(s_fin)
    y_prompt = rms_norm(x, norm_f)
    new_state_rwkv = jnp.stack(ctx_states, axis=1)

    x = x_sample
    for l in range(DEPTH):
        x, _ = run_layer(x, c, state_rwkv[:, l], True, l)
    y_sample = rms_norm(x, norm_f)

    return (y_prompt, y_sample, new_state_rwkv)


_drawn_inputs = setup_inputs


def setup_inputs(seed=0):
    import zlib

    import numpy as np

    out = dict(_drawn_inputs(seed))
    spreads = {}
    factors = {'state_rwkv': 8.0,
     'norm2': 5.346,
     'w_up': 3.528,
     'ln_x_w': 8.0,
     'ln_x_b': 8.0,
     'pool_scale': 5.295}
    for name, (base, spread) in spreads.items():
        noise = np.random.default_rng([zlib.crc32(name.encode()), seed]).standard_normal(out[name].shape)
        drawn = base * np.exp(spread * noise) if base else spread * noise
        out[name] = __import__('jax').numpy.asarray(drawn.astype(out[name].dtype))
    for name, factor in factors.items():
        out[name] = (out[name] * factor).astype(out[name].dtype)
    return out
```

```python
from contextlib import ExitStack

import numpy as np

import concourse.bass as bass
from concourse import mybir

ALU = mybir.AluOpType
ACT = mybir.ActivationFunctionType
AXX = mybir.AxisListType.X
F32 = mybir.dt.float32
U32 = mybir.dt.uint32
ds = bass.ds

P = 128
D = 1024
KT = D // P
SEQ, DEC = 128, 1024
NTOK = SEQ + DEC
NT = NTOK // P
GRID_W = 64
ROWS = DEC // GRID_W
DR = 512
HS = 64
CT = DR // P
NPROJ = 19
NZ = 15
T_R, T_K, T_V, T_G, T_W, T_A, T_POOL = 0, 4, 8, 12, 13, 14, 15
CH = 128
NCH = NTOK // CH
LEVELS = 7
WINDOWS = (2, 4, 8, 16)
NE = 16
DE = 2 * D
CAP_S = 2 * DEC // NE
CAP_P = 2 * SEQ // NE
SLOTS = CAP_S + CAP_P
RMS_EPS = 1e-6
GN_EPS = 64e-5
DECAY_C = float(np.exp(-0.5))
PIECE = NTOK // 3

PCOLS = {}
_n = 0
for _name, _k in (("c", 16), ("norm1", 8), ("ada_b", 48), ("mu", NZ), ("pool_scale", 4), ("head", 4 * 10)):
    PCOLS[_name] = (_n, _n + _k)
    _n += _k
NPARAM = _n
HP = {n: i for i, n in enumerate(("w0f", "w0b", "a0f", "a0b", "k_k", "k_a", "r_k", "ln_w", "ln_b", "zero"))}

CCOLS = {}
_n = 0
for _name, _k in (("ident", P), ("blk", P), ("eye", HS), ("lvl", 2 * LEVELS * CH), ("mask", 2 * 3 * CH),
                  ("tie", P), ("slot", P), ("tokid", NT)):
    CCOLS[_name] = (_n, _n + _k)
    _n += _k
NCONST = _n


class Steps:

    def __init__(self, names):
        self.names = names
        self.n = {x: i + 1 for i, x in enumerate(names)}
        assert len(self.n) == len(names)

    def __len__(self):
        return len(self.names)

    def __getitem__(self, name):
        return self.n[name]


class Signals:

    def __init__(self, sem, steps):
        self.sem, self.steps, self.at = sem, steps, 0

    def done(self, name, ins):
        assert self.steps.names[self.at] == name, (self.steps.names[self.at], name)
        self.at += 1
        ins.then_inc(self.sem, 1)


class Chain:

    def __init__(self, eng, sem, base=0):
        self.eng, self.sem, self.base, self.n = eng, sem, base, 0

    def __call__(self, ins):
        ins.then_inc(self.sem, 1)
        self.n += 1
        self.eng.wait_ge(self.sem, self.base + self.n)


def project_phase(nc, st, io, keep):
    sb = lambda n, s, dt=F32: st.enter_context(nc.sbuf_tensor(n, s, dt))
    ps = lambda n, s: st.enter_context(nc.psum_tensor(n, s, F32))
    sem = lambda n: st.enter_context(nc.semaphore(n))
    cst, par, z, zpool, mod = (keep[n] for n in ("cst", "par", "z", "zpool", "mod"))

    hT = sb("hT", [P, KT, NTOK])
    ada = sb("ada", [P, 2, KT, 256])
    xt = sb("xt", [P, 2, D])
    win = sb("win", [P, 2, KT, P])
    pad = sb("pad", [P, 2, NTOK + 3])
    nsum = sb("nsum", [P, NTOK + 1])
    silu_c = sb("silu_c", [P, KT, 2])
    sig_c = sb("sig_c", [P, 16])
    sq = sb("sq", [P, D])
    ss = sb("ss", [P, 8])
    g1 = sb("g1", [P, KT, 2])
    mus = sb("mus", [P, 2, NZ])
    modT = sb("modT", [96, P])

    ps_mod = ps("ps_mod", [P, 512])
    ps_t = ps("ps_t", [P, 2, 512])
    ps_p = ps("ps_p", [P, 3, 512])

    const_in = sem("const_in")
    silu_done = sem("silu_done")
    ada_in = [sem(f"ada_in{b}") for b in range(2)]
    ada_used = sem("ada_used")
    mod_done = sem("mod_done")
    modT_out = sem("modT_out")
    mod_sb = sem("mod_sb")
    x_in = [sem(f"x_in{b}") for b in range(2)]
    x_scaled = sem("x_scaled")
    x_turned = sem("x_turned")
    x_stored = sem("x_stored")
    sq_done = sem("sq_done")
    rms_v = sem("rms_v")
    rms_s = sem("rms_s")
    h_done = sem("h_done")
    win_in = [sem(f"win_in{b}") for b in range(2)]
    win_used = sem("win_used")
    p_copied = sem("p_copied")
    pad_used = sem("pad_used")
    pad_zero = sem("pad_zero")
    modrow_out = sem("modrow_out")
    pool_copied = sem("pool_copied")
    pre_chain = sem("pre_chain")
    shift_chain = sem("shift_chain")

    NADA = 6 * D // 256
    NROUND = NADA // 2
    ada_v = io["ada_w"].rearrange("(k p) e -> p k e", p=P)
    win_v = io["w_in"].rearrange("(k p) e -> p k e", p=P)
    x_v = io["x_all"].rearrange("(t p) d -> t p d", p=P)

    block = st.enter_context(nc.Block())

    @block.sync
    def _(eng):
        eng.dma_start(cst[:], io["consts"]).then_inc(const_in, 16)
        eng.dma_start(par[:], io["params"]).then_inc(const_in, 16)
        for b in range(2):
            eng.dma_start(xt[:, b], x_v[b]).then_inc(x_in[b], 16)
        for b in range(2):
            eng.dma_start(win[:, b], win_v[:, :, b * P:(b + 1) * P]).then_inc(win_in[b], 16)
            eng.dma_start(ada[:, b], ada_v[:, :, b * 256:(b + 1) * 256]).then_inc(ada_in[b], 16)
        for t in range(2, NT):
            eng.wait_ge(x_turned, t - 1)
            eng.dma_start(xt[:, t % 2], x_v[t]).then_inc(x_in[t % 2], 16)
        with eng.Fori(1, NROUND) as i:
            for b in range(2):
                eng.wait_ge(ada_used, 2 * i - 1 + b)
                eng.dma_start(ada[:, b], ada_v[:, :, ds(i * 512 + b * 256, 256)]).then_inc(ada_in[b], 16)
        with eng.Fori(1, NPROJ // 2) as i:
            for b in range(2):
                eng.wait_ge(win_used, 2 * i - 1 + b)
                eng.dma_start(win[:, b], win_v[:, :, ds(i * 256 + b * P, P)]).then_inc(win_in[b], 16)
        eng.wait_ge(win_used, NPROJ - 2)
        eng.dma_start(win[:, 0], win_v[:, :, (NPROJ - 1) * P:NPROJ * P]).then_inc(win_in[0], 16)
        eng.wait_ge(modT_out, 1)
        eng.dma_start(io["modrow"], modT[:, :]).then_inc(modrow_out, 16)
        eng.wait_ge(modrow_out, 16)

    @block.gpsimd
    def _(eng):
        eng.memset(pad[:], 0.0).then_inc(pad_zero, 1)

    @block.scalar
    def _(eng):
        eng.wait_ge(const_in, 32)
        eng.activation(sig_c[:], par[:, 0:16], ACT.Sigmoid).then_inc(silu_done, 1)
        for t in range(NT):
            b = t % 2
            eng.wait_ge(x_in[b], 16 * (t // 2 + 1))
            if t >= 1:
                eng.wait_ge(rms_v, 3 * t)
            eng.activation(sq[:], xt[:, b], ACT.Square, accum_out=ss[:, 0:1]).then_inc(sq_done, 1)
            eng.wait_ge(rms_v, 3 * t + 1)
            eng.activation(ss[:, 2:3], ss[:, 1:2], ACT.Sqrt).then_inc(rms_s, 1)
            eng.wait_ge(x_turned, t + 1)
            eng.activation(hT[:, :, t * P:(t + 1) * P], ps_t[:].rearrange("p a (k c) -> p (a k) c", c=P),
                           ACT.Copy).then_inc(x_stored, 1)

        def project(m, b, first):
            eng.wait_ge(win_used, m + 1)
            if not first:
                eng.wait_ge(pad_used, m - 1)
            eng.activation(pad[:, b, 1:1 + SEQ], ps_p[:, 0, 0:SEQ], ACT.Copy).then_inc(p_copied, 1)
            eng.activation(pad[:, b, 2 + SEQ:2 + PIECE], ps_p[:, 0, SEQ:PIECE], ACT.Copy).then_inc(p_copied, 1)
            eng.activation(pad[:, b, 2 + PIECE:2 + NTOK].rearrange("p (a c) -> p a c", a=2),
                           ps_p[:, 1:3, 0:PIECE], ACT.Copy).then_inc(p_copied, 1)

        eng.wait_ge(pad_zero, 1)
        project(0, 0, True)
        project(1, 1, True)
        with eng.Fori(1, NPROJ // 2) as i:
            for b in range(2):
                project(2 * i + b, b, False)
        project(NPROJ - 1, 0, False)

    @block.vector
    def _(eng):
        ch = Chain(eng, pre_chain)
        eng.wait_ge(silu_done, 1)
        ch(eng.tensor_tensor(silu_c[:].rearrange("p k s -> p (k s)"), sig_c[:], par[:, 0:16], ALU.mult))
        m0, m1 = PCOLS["mu"]
        ch(eng.tensor_scalar(mus[:, 0], par[:, m0:m1], -1.0, 1.0, ALU.mult, ALU.add))
        ch(eng.tensor_scalar(mus[:, 1], par[:, m0:m1], 0.5, None, ALU.mult))
        for t in range(NT):
            b = t % 2
            eng.wait_ge(sq_done, t + 1)
            eng.tensor_scalar(ss[:, 1:2], ss[:, 0:1], 1.0 / D, RMS_EPS, ALU.mult, ALU.add).then_inc(rms_v, 1)
            eng.wait_ge(rms_s, t + 1)
            eng.reciprocal(ss[:, 3:4], ss[:, 2:3]).then_inc(rms_v, 1)
            eng.wait_ge(rms_v, 3 * t + 2)
            eng.tensor_scalar(xt[:, b], xt[:, b], ss[:, 3:4], None, ALU.mult).then_inc(rms_v, 1)
        eng.wait_ge(mod_done, 1)
        a0, a1 = PCOLS["ada_b"]
        ch(eng.tensor_tensor(mod[:], ps_mod[:, 0:96].rearrange("p (e s) -> p e s", s=2),
                             par[:, a0:a1].unsqueeze(2).to_broadcast([P, 48, 2]), ALU.add))
        n0, n1 = PCOLS["norm1"]
        ch(eng.tensor_scalar(g1[:], mod[:, KT:2 * KT], 1.0, None, ALU.add))
        ch(eng.tensor_tensor(g1[:], g1[:], par[:, n0:n1].unsqueeze(2).to_broadcast([P, KT, 2]), ALU.mult))
        eng.sem_inc(mod_sb, 1)
        eng.wait_ge(x_stored, NT)
        for k in range(KT):
            for s, (lo, hi) in enumerate(((0, SEQ), (SEQ, NTOK))):
                eng.tensor_scalar(hT[:, k, lo:hi], hT[:, k, lo:hi], g1[:, k, s:s + 1], mod[:, k, s:s + 1],
                                  ALU.mult, ALU.add).then_inc(h_done, 1)
        eng.wait_ge(mod_done, 2)
        eng.tensor_copy(modT[:, :], ps_mod[0:96, 128:256]).then_inc(modT_out, 1)

        def shift(m, b, sh):
            eng.wait_ge(p_copied, 3 * m + 3)
            sh(eng.tensor_tensor(nsum[:], pad[:, b, 0:NTOK + 1], pad[:, b, 2:NTOK + 3], ALU.add))
            for lo, hi, g in ((0, SEQ, 0), (SEQ, NTOK, 1)):
                eng.tensor_scalar(z[:, m, lo:hi] if isinstance(m, int) else z[:, ds(m, 1), lo:hi],
                                  pad[:, b, 1 + lo + g:1 + hi + g] if isinstance(m, int) else pad[:, b:b + 1, 1 + lo + g:1 + hi + g],
                                  mus[:, 0, m:m + 1] if isinstance(m, int) else mus[:, 0, ds(m, 1)],
                                  None, ALU.mult).then_inc(shift_chain, 1)
            sh.n += 2
            eng.wait_ge(shift_chain, sh.base + sh.n)
            eng.tensor_scalar(nsum[:], nsum[:], mus[:, 1, m:m + 1] if isinstance(m, int) else mus[:, 1, ds(m, 1)],
                              None, ALU.mult).then_inc(shift_chain, 1)
            sh.n += 1
            eng.wait_ge(shift_chain, sh.base + sh.n)
            for lo, hi, g in ((0, SEQ, 0), (SEQ, NTOK, 1)):
                zz = z[:, m, lo:hi] if isinstance(m, int) else z[:, ds(m, 1), lo:hi].rearrange("p a c -> p (a c)")
                eng.tensor_tensor(zz, zz, nsum[:, lo + g:hi + g], ALU.add).then_inc(shift_chain, 1)
            sh.n += 2
            eng.wait_ge(shift_chain, sh.base + sh.n)
            eng.sem_inc(pad_used, 1)

        PER = 6
        sh = Chain(eng, shift_chain)
        with eng.Fori(0, NZ // 2) as i:
            for b in range(2):
                sh = Chain(eng, shift_chain, (2 * i + b) * PER)
                shift(2 * i + b, b, sh)
        shift(NZ - 1, 0, Chain(eng, shift_chain, (NZ - 1) * PER))
        for m in range(NZ, NPROJ):
            eng.wait_ge(p_copied, 3 * m + 3)
            eng.tensor_copy(zpool[:, m - NZ, 0:SEQ], pad[:, m % 2, 1:1 + SEQ]).then_inc(pool_copied, 1)
            eng.tensor_copy(zpool[:, m - NZ, SEQ:NTOK], pad[:, m % 2, 2 + SEQ:2 + NTOK]).then_inc(pad_used, 1)

    @block.tensor
    def _(eng):
        ident = cst[:, 0:P]
        eng.wait_ge(const_in, 32)
        for t in range(NT):
            eng.wait_ge(rms_v, 3 * t + 3)
            if t >= 1:
                eng.wait_ge(x_stored, t)
            for k in range(KT):
                ins = eng.transpose(ps_t[:, k // 4, (k % 4) * P:(k % 4 + 1) * P], xt[:, t % 2, k * P:(k + 1) * P], ident)
            ins.then_inc(x_turned, 1)
        eng.wait_ge(pre_chain, 1)
        with eng.Fori(0, NROUND) as i:
            for b in range(2):
                eng.wait_ge(ada_in[b], 16 * i + 16)
                for e in range(2):
                    for k in range(KT):
                        ins = eng.matmul(ps_mod[:, ds(i * 8 + b * 4 + e * 2, 2)], ada[:, b, k, e * P:(e + 1) * P],
                                         silu_c[:, k], start=(k == 0), stop=(k == KT - 1))
                ins.then_inc(ada_used, 1)
        eng.wait_ge(ada_used, NADA)
        eng.sem_inc(mod_done, 1)
        eng.wait_ge(mod_sb, 1)
        eng.transpose(ps_mod[0:96, 128:256], mod[:].rearrange("p e s -> p (e s)"), ident).then_inc(mod_done, 1)
        eng.wait_ge(h_done, 2 * KT)

        def project(m, b, first):
            eng.wait_ge(win_in[b], 16 * (m // 2 + 1) if isinstance(m, int) else m * 8 - 8 * b + 16)
            if not first:
                eng.wait_ge(p_copied, 3 * m)
            for c in range(3):
                for k in range(KT):
                    ins = eng.matmul(ps_p[:, c, 0:PIECE], win[:, b, k], hT[:, k, c * PIECE:(c + 1) * PIECE],
                                     start=(k == 0), stop=(k == KT - 1))
            ins.then_inc(win_used, 1)

        project(0, 0, True)
        project(1, 1, False)
        with eng.Fori(1, NPROJ // 2) as i:
            for b in range(2):
                project(2 * i + b, b, False)
        project(NPROJ - 1, 0, False)


def pool_phase(nc, st, io, keep):
    sb = lambda n, s, dt=F32: st.enter_context(nc.sbuf_tensor(n, s, dt))
    sem = lambda n: st.enter_context(nc.semaphore(n))
    zpool, par = keep["zpool"], keep["par"]
    NG = len(WINDOWS)
    cnt = sb("cnt", [P, NG, NTOK])
    seq = sb("seq", [P, 2, SEQ + 16])
    col = sb("col", [P, 2, ROWS, GRID_W + 16])
    row = sb("row", [P, 2, ROWS + 16, GRID_W])
    diff = sb("diff", [P, NG, NTOK])
    pw = sb("pw", [P, NG, P])
    yp = sb("yp", [P, NG, NTOK])
    ps_y = st.enter_context(nc.psum_tensor("ps_y", [P, 2, 3, 512], F32))
    pool_in = sem("pool_in")
    pool_chain = sem("pool_chain")
    diff_done = sem("diff_done")
    y_ready = sem("y_ready")
    y_copied = sem("y_copied")
    y_out = sem("y_out")
    block = st.enter_context(nc.Block())

    @block.sync
    def _(eng):
        eng.dma_start(pw[:], io["pool_w"].rearrange("g c d -> c g d")).then_inc(pool_in, 16)
        eng.dma_start(cnt[:], io["inv_cnt"].unsqueeze(0).to_broadcast([P, NG, NTOK])).then_inc(pool_in, 16)
        eng.wait_ge(y_copied, NG)
        eng.dma_start(io["ypool"], yp[:]).then_inc(y_out, 16)
        eng.wait_ge(y_out, 16)

    @block.vector
    def _(eng):
        ch = Chain(eng, pool_chain)
        eng.wait_ge(pool_in, 32)
        for g, win in enumerate(WINDOWS):
            hi = win - 1 - win // 2
            zg = zpool[:, g]
            for t in (seq, col, row):
                ch(eng.memset(t[:], 0.0))
            ch(eng.tensor_copy(seq[:, 0, 0:SEQ], zg[:, 0:SEQ]))
            ch(eng.tensor_copy(col[:, 0, :, 0:GRID_W], zg[:, SEQ:NTOK].rearrange("p (r c) -> p r c", c=GRID_W)))

            def doubled(buf):
                step, cur = 1, 0
                while step < win:
                    ch(eng.tensor_tensor(buf(1 - cur, step, None), buf(cur, step, None), buf(cur, 0, -step), ALU.add))
                    ch(eng.tensor_copy(buf(1 - cur, 0, step), buf(cur, 0, step)))
                    step, cur = 2 * step, 1 - cur
                return cur

            n = doubled(lambda i, a, b: seq[:, i, a:b])
            ch(eng.tensor_tensor(diff[:, g, 0:SEQ], seq[:, n, hi:hi + SEQ], cnt[:, g, 0:SEQ], ALU.mult))
            n = doubled(lambda i, a, b: col[:, i, :, a:b])
            ch(eng.tensor_copy(row[:, 0, 0:ROWS], col[:, n, :, hi:hi + GRID_W]))
            n = doubled(lambda i, a, b: row[:, i, a:b])
            ch(eng.tensor_tensor(diff[:, g, SEQ:NTOK], row[:, n, hi:hi + ROWS].rearrange("p r c -> p (r c)"),
                                 cnt[:, g, SEQ:NTOK], ALU.mult))
            eng.tensor_tensor(diff[:, g], diff[:, g], zg, ALU.subtract).then_inc(diff_done, 1)

    @block.tensor
    def _(eng):
        for g in range(NG):
            eng.wait_ge(diff_done, g + 1)
            if g >= 2:
                eng.wait_ge(y_copied, g - 1)
            for c in range(3):
                ins = eng.matmul(ps_y[:, g % 2, c, 0:PIECE], pw[:, g], diff[:, g, c * PIECE:(c + 1) * PIECE],
                                 start=True, stop=True)
            ins.then_inc(y_ready, 1)

    @block.scalar
    def _(eng):
        s0 = PCOLS["pool_scale"][0]
        for g in range(NG):
            eng.wait_ge(y_ready, g + 1)
            eng.activation(yp[:, g].rearrange("p (a c) -> p a c", a=3), ps_y[:, g % 2, :, 0:PIECE], ACT.Copy,
                           scale=par[:, s0 + g:s0 + g + 1]).then_inc(y_copied, 1)


CHUNK_PE = ([f"AB{u}" for u in range(4)] + ["TOK0", "TOK1"] + [f"D{u}" for u in range(4)] + [f"X0_{u}" for u in range(4)]
            + [f"{k}{lv}_{u}" for lv in range(1, LEVELS) for k in "XT" for u in range(4)]
            + [f"WU{u}" for u in range(4)] + ["FIN0", "FIN1", "Y0"])
CHUNK_DVE = (["kr", "kh", "nb"] + [f"AB{u}" for u in range(4)] + [f"X0_{u}" for u in range(4)]
             + [f"T{lv}_{u}" for lv in range(1, LEVELS) for u in range(4)] + ["FIN0", "FIN1"])
CHUNK_ACT = (["EX", "V", "TOK0", "TOK1"] + [f"D{u}" for u in range(4)]
             + [f"X{lv}_{u}" for lv in range(1, LEVELS) for u in range(4)]
             + [f"WU{u}" for u in range(4)] + ["FIN0", "FIN1", "Y0"])
CHUNK_POOL = [f"L{lv}_{u}" for lv in range(2) for u in range(4)] + [f"TT{u}" for u in range(4)]
CHUNK_POOL += [f"L{lv}_{u}" for lv in range(2, LEVELS) for u in range(4)]
SPANS = ((0, 1), (1, 4), (5, 4))


def scan_phase(nc, st, io, keep):
    sb = lambda n, s, dt=F32: st.enter_context(nc.sbuf_tensor(n, s, dt))
    sem = lambda n: st.enter_context(nc.semaphore(n))
    cst, par, z = keep["cst"], keep["par"], keep["z"]

    def const(name):
        return cst[:, CCOLS[name][0]:CCOLS[name][1]]

    ident, blk, eye = const("ident"), const("blk"), const("eye")
    lvl = const("lvl").rearrange("p (d l c) -> p d l c", d=2, l=LEVELS)
    mask = const("mask").rearrange("p (d k c) -> p d k c", d=2, k=3)

    reset = sb("reset", [P, NTOK])
    hp = sb("hp", [P, 10])
    ka1 = sb("ka1", [P, 1])
    up_w = sb("up_w", [P, P])
    up_a = sb("up_a", [P, P])
    up_g = sb("up_g", [P, P])
    l_in = sb("l_in", [P, 2, NTOK])
    l_ex = sb("l_ex", [P, 2, NTOK])
    cen = sb("cen", [P, 2, NCH])
    ncen = sb("ncen", [P, 2, NCH])
    e_cen = sb("e_cen", [P, 2, NCH])
    kd = sb("kd", [P, 2, NTOK])
    nb = sb("nb", [P, 2, NTOK])
    kk = sb("kk", [P, NTOK])
    y = sb("y", [P, NTOK])
    m_all = sb("m_all", [P, 2, NTOK])
    r_all = sb("r_all", [P, 2, NTOK])
    n_all = sb("n_all", [P, 2, NTOK])
    eps = sb("eps", [P, 1])
    ex_w = sb("ex_w", [P, 3, 2, CH])
    kr_w = sb("kr_w", [P, 2, 2, 2, CH])
    kh_w = sb("kh_w", [P, 2, CH])
    nb_w = sb("nb_w", [P, 2, CH])
    v_w = sb("v_w", [P, CH])
    ab_w = sb("ab_w", [P, 4, 3, CH])
    np_w = sb("np_w", [P, 4, HS + CH])
    lm_w = sb("lm_w", [P, 4, 2, CH])
    kt_w = sb("kt_w", [P, 2, CH])
    tokv_w = sb("tokv_w", [P, CH])
    kd_w = sb("kd_w", [P, 4, 2, HS])
    x_w = sb("x_w", [P, 4, CH])
    t_w = sb("t_w", [P, 4, 2, CH])
    wu_w = sb("wu_w", [P, 4, 2, HS])
    mr_w = sb("mr_w", [P, 2, HS + CH])
    zst = sb("zst", [P, 2, 2, HS])
    z0s = sb("z0s", [P, 2, CT, HS])

    banks = [st.enter_context(nc.psum_tensor(f"bank{i}", [P, 512], F32)) for i in range(8)]
    T_BANK = [banks[i] for i in (4, 5, 0, 1)]
    X_BANK = [banks[i] for i in (2, 3, 6, 7)]
    TOK_BANK = banks[6:8]
    FIN_BANK = banks[2:4]
    V_BANK, Y_BANK = banks[2], banks[6]

    scan_in = sem("scan_in")
    up_in = sem("up_in")
    lora_act = sem("lora_act")
    pre_pe = sem("pre_pe")
    pre_act = sem("pre_act")
    chain_v = sem("chain_v")
    chunk_pe = sem("chunk_pe")
    chunk_dve = sem("chunk_dve")
    chunk_act = sem("chunk_act")
    chunk_pool = sem("chunk_pool")
    state_pe = sem("state_pe")
    state_dve = sem("state_dve")
    gn_pe = sem("gn_pe")
    gn_act = sem("gn_act")
    state_out = sem("state_out")
    pre_free = sem("pre_free")
    pe_began = sem("pe_began")
    kd_ready = sem("kd_ready")
    mean_off = sem("mean_off")
    bonus_v = sem("bonus_v")
    kr_zero = sem("kr_zero")
    fin_sum = sem("fin_sum")

    PE_N, DVE_N, ACT_N, POOL_N = (Steps(x) for x in (CHUNK_PE, CHUNK_DVE, CHUNK_ACT, CHUNK_POOL))
    PRE_PE = Steps(["w0", "w1", "a0", "a1", "kk"])
    PRE_ACT = Steps(["w0", "w1", "a0", "a1", "ksq", "kroot", "e_cen"])
    GN_PE = Steps(["mean", "var", "bonus", "gate"])
    GN_ACT = Steps(["sq", "root", "gate"])
    V_CEN = 8
    V_PRE = 11
    V_ALL = 25
    DV0 = 1
    NSPAN = 2 * len(SPANS)
    S_ALL = 2 * NCH + 4
    H = (slice(0, HS), slice(HS, P))
    FWD = list(range(NCH))
    BWD = [0] + list(range(NCH - 1, 0, -1))

    def three(bank0):
        return [banks[bank0 + i][:, 0:PIECE] for i in range(3)]

    def pieces(ap):
        return [ap[:, c * PIECE:(c + 1) * PIECE] for c in range(3)]

    block = st.enter_context(nc.Block())

    @block.sync
    def _(eng):
        eng.dma_start(reset[:], io["reset"].unsqueeze(0).to_broadcast([P, NTOK])).then_inc(scan_in, 16)
        eng.dma_start(z0s[:], io["state0"].rearrange("d t p v -> p d t v")).then_inc(scan_in, 16)
        with eng.Fori(0, CT) as t:
            eng.wait_ge(pre_free, t + 1)
            eng.dma_start(up_w[:], io["w_up"][:, ds(t * P, P)]).then_inc(up_in, 16)
            eng.dma_start(up_a[:], io["a_up"][:, ds(t * P, P)]).then_inc(up_in, 16)
            eng.dma_start(up_g[:], io["g_up"][:, ds(t * P, P)]).then_inc(up_in, 16)
            for d in range(2):
                eng.wait_ge(state_dve, t * S_ALL + 3 + d)
                eng.dma_start(io["state_out"][d, ds(t, 1)].rearrange("o p v -> (o p) v"), zst[:, d, 1]).then_inc(state_out, 16)
        eng.wait_ge(state_out, 32 * CT)

    @block.gpsimd
    def _(eng):
        eng.memset(eps[:], GN_EPS).then_inc(pre_free, 1)
        eng.memset(kr_w[:], 0.0).then_inc(kr_zero, 1)
        with eng.Fori(0, CT) as t:
            with eng.Fori(0, NCH) as i:
                it = t * NCH + i
                dve, pe, own = DV0 + it * len(DVE_N), it * len(PE_N), it * len(POOL_N)
                sg = Signals(chunk_pool, POOL_N)

                def level(lv, u):
                    sg.done(f"L{lv}_{u}", eng.tensor_tensor(lm_w[:, u, lv % 2], ab_w[:, u, 2], lvl[:, u // 2, lv], ALU.mult))

                for lv in range(2):
                    for u in range(4):
                        if lv == 0:
                            eng.wait_ge(chunk_dve, dve + DVE_N[f"AB{u}"])
                        level(lv, u)
                for u in range(4):
                    eng.wait_ge(chunk_pool, own + POOL_N[f"L0_{u}"])
                    sg.done(f"TT{u}", eng.tensor_tensor(t_w[:, u, 1], lm_w[:, u, 0], ident, ALU.add))
                for lv in range(2, LEVELS):
                    for u in range(4):
                        eng.wait_ge(chunk_pe, pe + PE_N[f"X{lv - 2}_{u}"])
                        if lv == 2:
                            eng.wait_ge(chunk_pool, own + POOL_N[f"TT{u}"])
                        level(lv, u)

    @block.scalar
    def _(eng):
        eng.wait_ge(pre_free, 1)
        eng.activation(z[:, T_W], z[:, T_W], ACT.Tanh).then_inc(lora_act, 1)
        eng.activation(z[:, T_G], z[:, T_G], ACT.Sigmoid).then_inc(lora_act, 1)
        with eng.Fori(0, CT) as t:
            sg = Signals(pre_act, PRE_ACT)
            pp = t * len(PRE_PE)
            vc = t * V_ALL
            eng.wait_ge(chain_v, vc + 1)
            for n, (name, out, bias) in enumerate((("w0", l_ex[:, 0], "w0f"), ("w1", l_ex[:, 1], "w0b"),
                                                   ("a0", nb[:, 0], "a0f"), ("a1", nb[:, 1], "a0b"))):
                eng.wait_ge(pre_pe, pp + PRE_PE[name])
                for c in range(3):
                    ins = eng.activation(pieces(out)[c], three(3 * (n % 2))[c], ACT.Sigmoid, bias=hp[:, HP[bias]:HP[bias] + 1])
                sg.done(name, ins)
            eng.wait_ge(chain_v, vc + 2)
            sg.done("ksq", eng.activation(kd[:, 0], kk[:], ACT.Square))
            eng.wait_ge(pre_pe, pp + PRE_PE["kk"])
            for c in range(3):
                ins = eng.activation(pieces(kd[:, 0])[c], three(0)[c], ACT.Sqrt)
            sg.done("kroot", ins)
            eng.wait_ge(chain_v, vc + V_CEN)
            sg.done("e_cen", eng.activation(e_cen[:], cen[:], ACT.Exp))
            with eng.Fori(0, NCH) as i:
                it = t * NCH + i
                pe = it * len(PE_N)
                cols = ds(i * CH, CH)
                sg = Signals(chunk_act, ACT_N)
                for d in range(2):
                    for n, (src, scale, bias) in enumerate(((l_in, 1.0, ncen), (l_in, -1.0, cen), (l_ex, 1.0, ncen))):
                        ins = eng.activation(ex_w[:, n, d], src[:, d, cols], ACT.Exp, bias=bias[:, d, ds(i, 1)], scale=scale)
                sg.done("EX", ins)
                sg.done("V", eng.activation(v_w[:], z[:, ds(T_V + t, 1), cols].rearrange("p a c -> p (a c)"), ACT.Copy))
                for d in range(2):
                    eng.wait_ge(chunk_pe, pe + PE_N[f"TOK{d}"])
                    tok = TOK_BANK[d]
                    own = tok[:, 0:384].rearrange("p (h c) -> p h c", c=192)[:, :, 0:HS]
                    eng.activation(kd_w[:, 2 * d:2 * d + 2, 0], own, ACT.Copy)
                    eng.activation(kt_w[:, d], tok[:, 256:384], ACT.Copy)
                    ins = eng.activation(np_w[:, 2 * d:2 * d + 2, 0:HS], tok[:, 384:512].rearrange("p (h c) -> p h c", h=2), ACT.Copy)
                    if d == 0:
                        ins = eng.activation(tokv_w[:], V_BANK[:, 0:CH], ACT.Copy)
                    sg.done(f"TOK{d}", ins)
                for u in range(4):
                    eng.wait_ge(chunk_pe, pe + PE_N[f"D{u}"])
                    h = u % 2
                    sg.done(f"D{u}", eng.activation(kd_w[:, u, 1], X_BANK[u][:, h * HS:(h + 1) * HS], ACT.Copy))
                for lv in range(1, LEVELS):
                    for u in range(4):
                        eng.wait_ge(chunk_pe, pe + PE_N[f"X{lv}_{u}"])
                        sg.done(f"X{lv}_{u}", eng.activation(x_w[:, u], X_BANK[u][:, 0:CH], ACT.Copy))
                for u in range(4):
                    eng.wait_ge(chunk_pe, pe + PE_N[f"WU{u}"])
                    sg.done(f"WU{u}", eng.activation(wu_w[:, u].rearrange("p k c -> p (k c)"), T_BANK[u][:, 0:2 * HS], ACT.Copy))
                for d in range(2):
                    eng.wait_ge(fin_sum, 2 * it + d + 1)
                    scale = e_cen[:, d, ds(i, 1)]
                    eng.activation(m_all[:, d, ds(i * HS, HS)], mr_w[:, d, 0:HS], ACT.Copy, scale=scale)
                    sg.done(f"FIN{d}", eng.activation(r_all[:, d, cols], mr_w[:, d, HS:HS + CH], ACT.Copy, scale=scale))
                eng.wait_ge(chunk_pe, pe + PE_N["Y0"])
                sg.done("Y0", eng.activation(y[:, cols], Y_BANK[:, 0:CH], ACT.Copy))
            gs = Signals(gn_act, GN_ACT)
            eng.wait_ge(mean_off, 3 * t + 3)
            gs.done("sq", eng.activation(m_all[:, 0], y[:], ACT.Square))
            eng.wait_ge(gn_pe, t * len(GN_PE) + GN_PE["var"])
            for c in range(3):
                ins = eng.activation(pieces(m_all[:, 0])[c], three(3)[c], ACT.Sqrt, bias=eps[:, 0:1], scale=1.0 / HS)
            gs.done("root", ins)
            eng.wait_ge(gn_pe, t * len(GN_PE) + GN_PE["gate"])
            for c in range(3):
                ins = eng.activation(pieces(m_all[:, 1])[c], three(3)[c], ACT.Copy)
            gs.done("gate", ins)

    @block.vector
    def _(eng):
        eng.wait_ge(scan_in, 32)
        eng.wait_ge(kr_zero, 1)
        eng.sem_inc(chunk_dve, DV0)
        with eng.Fori(0, CT) as t:
            pa = t * len(PRE_ACT)
            ch = Chain(eng, chain_v, t * V_ALL)
            ktile = z[:, ds(T_K + t, 1)].rearrange("p a c -> p (a c)")
            rtile = z[:, ds(t, 1)].rearrange("p a c -> p (a c)")
            vtile = z[:, ds(T_V + t, 1)].rearrange("p a c -> p (a c)")
            ch(eng.tensor_copy(hp[:], par[:, ds(PCOLS["head"][0] + t * 10, 10)]))
            col = lambda n: hp[:, HP[n]:HP[n] + 1]
            ch(eng.tensor_scalar(kk[:], ktile, col("k_k"), None, ALU.mult))
            eng.wait_ge(pre_act, pa + PRE_ACT["w1"])
            ch(eng.tensor_scalar(l_ex[:], l_ex[:], -DECAY_C, None, ALU.mult))
            eng.tensor_tensor_scan(l_in[:, 0], reset[:], l_ex[:, 0], 0.0, ALU.mult, ALU.add)
            ch(eng.tensor_tensor_scan(l_in[:, 1], reset[:], l_ex[:, 1], 0.0, ALU.mult, ALU.add))
            sums = l_in[:].rearrange("p d (n c) -> p d n c", c=CH)
            eng.tensor_scalar(ncen[:], sums[:, :, :, CH - 1], -0.5, None, ALU.mult)
            ch(eng.tensor_scalar(cen[:], sums[:, :, :, CH - 1], 0.5, None, ALU.mult))
            ch(eng.scalar_tensor_tensor(m_all[:, 1].rearrange("p (n c) -> p n c", c=CH),
                                        cen[:, 1].unsqueeze(2).to_broadcast([P, NCH, CH]), 2.0, sums[:, 1],
                                        ALU.mult, ALU.subtract))
            ch(eng.tensor_tensor(l_in[:, 1], m_all[:, 1], l_ex[:, 1], ALU.add))
            eng.tensor_copy(l_ex[:, 1], m_all[:, 1])
            ch(eng.tensor_tensor(l_ex[:, 0], l_in[:, 0], l_ex[:, 0], ALU.subtract))
            assert ch.n == V_CEN
            eng.wait_ge(pre_act, pa + PRE_ACT["kroot"])
            ch(eng.tensor_scalar(kd[:, 0], kd[:, 0], 1e-12, None, ALU.max))
            ch(eng.reciprocal(kd[:, 1], kd[:, 0]))
            ch(eng.tensor_tensor(kk[:], kk[:], kd[:, 1], ALU.mult))
            assert ch.n == V_PRE
            eng.wait_ge(pre_act, pa + PRE_ACT["a1"])
            eng.tensor_scalar(ka1[:], col("k_a"), -1.0, 1.0, ALU.mult, ALU.add).then_inc(kd_ready, 1)
            eng.wait_ge(kd_ready, 4 * t + 1)
            eng.tensor_scalar(kd[:], nb[:], col("k_a"), ka1[:, 0:1], ALU.mult, ALU.add).then_inc(kd_ready, 1)
            eng.wait_ge(kd_ready, 4 * t + 2)
            eng.tensor_tensor(kd[:], kd[:], ktile.unsqueeze(1).to_broadcast([P, 2, NTOK]), ALU.mult).then_inc(kd_ready, 1)
            eng.scalar_tensor_tensor(nb[:], nb[:], -1.0, kk[:].unsqueeze(1).to_broadcast([P, 2, NTOK]),
                                     ALU.mult, ALU.mult).then_inc(kd_ready, 1)
            with eng.Fori(0, NCH) as i:
                it = t * NCH + i
                pe, act = it * len(PE_N), it * len(ACT_N)
                sg = Signals(chunk_dve, DVE_N)
                cols = ds(i * CH, CH)
                eng.wait_ge(pre_act, pa + PRE_ACT["e_cen"])
                eng.wait_ge(kd_ready, 4 * t + 4)
                eng.wait_ge(chunk_dve, DV0 + it * len(DVE_N))
                eng.wait_ge(chunk_act, act + ACT_N["EX"])
                for h in range(2):
                    eng.tensor_tensor(kr_w[H[h], :, h, 0], ex_w[H[h], 2], kk[H[h], cols].unsqueeze(1).to_broadcast([HS, 2, CH]), ALU.mult)
                    ins = eng.tensor_tensor(kr_w[H[h], :, h, 1], ex_w[H[h], 0], z[H[h], ds(t, 1), cols].to_broadcast([HS, 2, CH]), ALU.mult)
                sg.done("kr", ins)
                sg.done("kh", eng.tensor_tensor(kh_w[:], kd[:, :, cols], ex_w[:, 1], ALU.mult))
                sg.done("nb", eng.tensor_tensor(nb_w[:], nb[:, :, cols], ex_w[:, 1], ALU.mult))
                for u in range(4):
                    eng.wait_ge(chunk_pe, pe + PE_N[f"AB{u}"])
                    eng.tensor_tensor(ab_w[:, u].rearrange("p k c -> p (k c)"), T_BANK[u][:, 0:384],
                                      mask[:, u // 2].rearrange("p k c -> p (k c)"), ALU.mult)
                    sg.done(f"AB{u}", eng.tensor_tensor(np_w[:, u, HS:HS + CH], T_BANK[u][:, 384:512], mask[:, u // 2, 1], ALU.mult))
                for u in range(4):
                    eng.wait_ge(chunk_pe, pe + PE_N[f"X0_{u}"])
                    sg.done(f"X0_{u}", eng.tensor_tensor(t_w[:, u, 0], X_BANK[u][:, 0:CH], ident, ALU.add))
                for lv in range(1, LEVELS):
                    for u in range(4):
                        eng.wait_ge(chunk_pe, pe + PE_N[f"T{lv}_{u}"])
                        if lv < LEVELS - 1:
                            tt = t_w[:, u].rearrange("p k c -> p (k c)")
                            sg.done(f"T{lv}_{u}", eng.tensor_tensor(tt, T_BANK[u][:, 0:2 * CH], tt, ALU.add))
                        else:
                            sg.done(f"T{lv}_{u}", eng.tensor_tensor(t_w[:, u, 1], T_BANK[u][:, CH:2 * CH], t_w[:, u, 1], ALU.add))
                for d in range(2):
                    eng.wait_ge(chunk_pe, pe + PE_N[f"FIN{d}"])
                    fin = FIN_BANK[d]
                    eng.tensor_tensor(mr_w[:, d, 0:HS], fin[:, 0:HS], eye, ALU.add)
                    for h in range(2):
                        ins = eng.tensor_tensor(mr_w[H[h], d, HS:HS + CH], fin[H[h], HS:HS + CH], kr_w[H[h], d, h, 1], ALU.add)
                    ins.then_inc(fin_sum, 1)
                    sg.done(f"FIN{d}", eng.tensor_scalar(n_all[:, d, ds(i * HS, HS)], fin[:, HS + CH:2 * HS + CH],
                                                         e_cen[:, d, ds(i, 1)], None, ALU.mult))
            eng.wait_ge(chunk_act, (t + 1) * NCH * len(ACT_N))
            eng.wait_ge(chunk_dve, DV0 + (t + 1) * NCH * len(DVE_N))
            for d in range(2):
                eng.memset(zst[:, d, 0], 0.0).then_inc(state_dve, 1)
            for s in range(NCH):
                for d, order in enumerate((FWD, BWD)):
                    c = order[s]
                    eng.wait_ge(state_pe, t * 2 * NCH + 2 * s + d + 1)
                    eng.scalar_tensor_tensor(zst[:, d, (s + 1) % 2], banks[4 + d][:, 0:HS], e_cen[:, d, c:c + 1],
                                             n_all[:, d, c * HS:(c + 1) * HS], ALU.mult, ALU.add).then_inc(state_dve, 1)
                if s == 0:
                    eng.wait_ge(state_out, 32 * t + 32)
                    for d in range(2):
                        eng.tensor_copy(zst[:, d, 1], z0s[:, d, ds(t, 1)].rearrange("p a v -> p (a v)")).then_inc(state_dve, 1)
                for k, (lo, num) in enumerate(SPANS):
                    for d, order in enumerate((FWD, BWD)):
                        if s == max(order.index(c) for c in range(lo, lo + num)):
                            ch(eng.tensor_tensor(y[:, lo * CH:(lo + num) * CH], y[:, lo * CH:(lo + num) * CH],
                                                 banks[2 * d + k % 2][:, 0:num * CH], ALU.add))
            gp = t * len(GN_PE)
            ga = t * len(GN_ACT)
            eng.wait_ge(gn_pe, gp + GN_PE["mean"])
            for c in range(3):
                eng.scalar_tensor_tensor(pieces(y[:])[c], three(4)[c], -1.0 / HS, pieces(y[:])[c], ALU.mult, ALU.add).then_inc(mean_off, 1)
            ch(eng.tensor_tensor(r_all[:, 0], kd[:, 0], kd[:, 1], ALU.add))
            ch(eng.tensor_tensor(r_all[:, 0], r_all[:, 0], rtile, ALU.mult))
            ch(eng.tensor_scalar(r_all[:, 1], r_all[:, 0], col("r_k"), None, ALU.mult))
            eng.wait_ge(gn_act, ga + GN_ACT["root"])
            ch(eng.reciprocal(n_all[:, 0], m_all[:, 0]))
            ch(eng.tensor_tensor(y[:], y[:], n_all[:, 0], ALU.mult))
            ch(eng.tensor_scalar(y[:], y[:], col("ln_w"), col("ln_b"), ALU.mult, ALU.add))
            eng.wait_ge(gn_pe, gp + GN_PE["bonus"])
            for c in range(3):
                eng.tensor_tensor(pieces(n_all[:, 1])[c], three(0)[c], pieces(vtile)[c], ALU.mult).then_inc(bonus_v, 1)
            eng.wait_ge(bonus_v, 3 * t + 3)
            ch(eng.tensor_tensor(y[:], y[:], n_all[:, 1], ALU.add))
            eng.wait_ge(gn_act, ga + GN_ACT["gate"])
            ch(eng.tensor_tensor(rtile, y[:], m_all[:, 1], ALU.mult))
            assert ch.n == V_ALL, ch.n
            eng.sem_inc(pre_free, 1)

    @block.tensor
    def _(eng):
        eng.wait_ge(lora_act, 2)

        def mm(out, a, b, start=True, stop=True):
            return eng.matmul(out, a, b, start=start, stop=stop, skip_group_check=True)

        with eng.Fori(0, CT) as t:
            sg = Signals(pre_pe, PRE_PE)
            pa = t * len(PRE_ACT)
            vc = t * V_ALL
            eng.wait_ge(up_in, 48 * t + 48)
            for n, (name, w, src, d) in enumerate((("w0", up_w, T_W, 0), ("w1", up_w, T_W, 1),
                                                   ("a0", up_a, T_A, 0), ("a1", up_a, T_A, 1))):
                if n >= 2:
                    eng.wait_ge(pre_act, pa + PRE_ACT[("w0", "w1")[n - 2]])
                for c in range(3):
                    ins = eng.matmul(three(3 * (n % 2))[c], w[H[d]], pieces(z[H[d], src])[c], start=True, stop=True)
                sg.done(name, ins)
            eng.wait_ge(pre_act, pa + PRE_ACT["ksq"])
            for c in range(3):
                ins = eng.matmul(three(0)[c], blk, pieces(kd[:, 0])[c], start=True, stop=True)
            sg.done("kk", ins)

            with eng.Fori(0, NCH) as i:
                it = t * NCH + i
                dv, ac, po = DV0 + it * len(DVE_N), it * len(ACT_N), it * len(POOL_N)
                sg = Signals(chunk_pe, PE_N)
                eng.wait_ge(pre_act, pa + PRE_ACT["kroot"])
                eng.wait_ge(chunk_dve, dv + DVE_N["nb"])
                for u in range(4):
                    rhs = kr_w[:, u // 2, u % 2].rearrange("p k c -> p (k c)")
                    mm(T_BANK[u][:, 0:256], kh_w[:, u // 2], rhs)
                    ins = mm(T_BANK[u][:, 256:512], nb_w[:, u // 2], rhs)
                    sg.done(f"AB{u}", ins)
                eng.wait_ge(chunk_act, ac + ACT_N["V"])
                for d in range(2):
                    for n, src in enumerate((kr_w[:, d, 0, 0], kr_w[:, d, 1, 0], kh_w[:, d], nb_w[:, d])):
                        ins = eng.transpose(TOK_BANK[d][:, n * P:(n + 1) * P], src, ident)
                    if d == 0:
                        ins = eng.transpose(V_BANK[:, 0:CH], v_w[:], ident)
                    sg.done(f"TOK{d}", ins)
                for u in range(4):
                    eng.wait_ge(chunk_dve, dv + DVE_N[f"AB{u}"])
                    eng.wait_ge(chunk_act, ac + ACT_N["TOK1" if u > 1 else "TOK0"])
                    sg.done(f"D{u}", mm(X_BANK[u][:, 0:CH], ab_w[:, u, 0], tokv_w[:]))
                for u in range(4):
                    eng.wait_ge(chunk_pool, po + POOL_N[f"L0_{u}"])
                    eng.wait_ge(chunk_act, ac + ACT_N[f"D{u}"])
                    sg.done(f"X0_{u}", mm(X_BANK[u][:, 0:CH], lm_w[:, u, 0], ident))
                for lv in range(1, LEVELS):
                    for u in range(4):
                        eng.wait_ge(chunk_pool, po + POOL_N[f"L{lv}_{u}" if lv > 1 else f"TT{u}"])
                        eng.wait_ge(chunk_dve, dv + DVE_N[f"T{lv - 1}_{u}" if lv > 1 else f"X0_{u}"])
                        sg.done(f"X{lv}_{u}", mm(X_BANK[u][:, 0:CH], lm_w[:, u, lv % 2], t_w[:, u, 0]))
                    for u in range(4):
                        eng.wait_ge(chunk_act, ac + ACT_N[f"X{lv}_{u}"])
                        if lv < LEVELS - 1:
                            mm(T_BANK[u][:, 0:CH], t_w[:, u, 1], x_w[:, u])
                        sg.done(f"T{lv}_{u}", mm(T_BANK[u][:, CH:2 * CH], x_w[:, u], t_w[:, u, 1]))
                for u in range(4):
                    eng.wait_ge(chunk_dve, dv + DVE_N[f"T{LEVELS - 1}_{u}"])
                    sg.done(f"WU{u}", mm(T_BANK[u][:, 0:2 * HS], t_w[:, u, 1], kd_w[:, u].rearrange("p k c -> p (k c)")))
                for d in range(2):
                    for h in range(2):
                        u = 2 * d + h
                        hc = slice(h * HS, (h + 1) * HS)
                        eng.wait_ge(chunk_act, ac + ACT_N[f"WU{u}"])
                        mm(FIN_BANK[d][H[h], 0:HS + CH], wu_w[:, u, 0], np_w[:, u])
                        out = FIN_BANK[d][H[h], HS + CH:2 * HS + CH]
                        mm(out, kt_w[:, d, hc], tokv_w[:, hc], stop=False)
                        ins = mm(out, np_w[:, u, 0:HS], wu_w[:, u, 1], start=False)
                    sg.done(f"FIN{d}", ins)
                for h in range(2):
                    for d in range(2):
                        u = 2 * d + h
                        mm(Y_BANK[H[h], 0:CH], tokv_w[:, h * HS:(h + 1) * HS], ab_w[:, u, 1], start=d == 0, stop=False)
                        ins = mm(Y_BANK[H[h], 0:CH], wu_w[:, u, 1], np_w[:, u, HS:HS + CH], start=False, stop=d == 1)
                sg.done("Y0", ins)
            eng.wait_ge(chunk_dve, DV0 + (t + 1) * NCH * len(DVE_N))
            eng.wait_ge(chunk_act, (t + 1) * NCH * len(ACT_N))

            def carried():
                eng.sem_inc(pe_began, 1)

            s0 = t * S_ALL
            for s in range(NCH):
                for d, order in enumerate((FWD, BWD)):
                    c = order[s]
                    eng.wait_ge(state_dve, s0 + (1 + d if s == 0 else 2 * s + 3 + d))
                    carried()
                    k = [k for k, (lo, num) in enumerate(SPANS) if lo <= c < lo + num][0]
                    lo = SPANS[k][0]
                    if s == 1 and d == 0:
                        eng.wait_ge(chain_v, vc + V_PRE + 2)
                        carried()
                    for h in H:
                        mm(banks[2 * d + k % 2][h, (c - lo) * CH:(c - lo + 1) * CH], zst[h, d, s % 2], r_all[h, d, c * CH:(c + 1) * CH])
                    for h in H:
                        ins = mm(banks[4 + d][h, 0:HS], m_all[h, d, c * HS:(c + 1) * HS], zst[h, d, s % 2])
                    ins.then_inc(state_pe, 1)
            gs = Signals(gn_pe, GN_PE)
            eng.wait_ge(chain_v, vc + V_PRE + NSPAN)
            eng.wait_ge(state_dve, s0 + S_ALL)
            for c in range(3):
                ins = eng.matmul(three(4)[c], blk, pieces(y[:])[c], start=True, stop=True)
            gs.done("mean", ins)
            eng.wait_ge(gn_act, t * len(GN_ACT) + GN_ACT["sq"])
            for c in range(3):
                ins = eng.matmul(three(3)[c], blk, pieces(m_all[:, 0])[c], start=True, stop=True)
            gs.done("var", ins)
            eng.wait_ge(chain_v, vc + V_PRE + NSPAN + 3)
            for c in range(3):
                ins = eng.matmul(three(0)[c], blk, pieces(r_all[:, 1])[c], start=True, stop=True)
            gs.done("bonus", ins)
            eng.wait_ge(gn_act, t * len(GN_ACT) + GN_ACT["root"])
            for c in range(3):
                ins = eng.matmul(three(3)[c], up_g[:], pieces(z[:, T_G])[c], start=True, stop=True)
            gs.done("gate", ins)


def output_phase(nc, st, io, keep):
    sb = lambda n, s, dt=F32: st.enter_context(nc.sbuf_tensor(n, s, dt))
    ps = lambda n, s: st.enter_context(nc.psum_tensor(n, s, F32))
    sem = lambda n: st.enter_context(nc.semaphore(n))
    cst, z, probs = (keep[n] for n in ("cst", "z", "probs"))
    x1 = sb("x1_sb", [P, NT, D])
    ident = cst[:, 0:P]
    wo = sb("wo", [P, KT, D])
    wr = sb("wr", [P, KT, NE])
    gt1 = sb("gt1", [P, 2, D])
    gn2 = sb("gn2", [P, 2, D])
    sh2 = sb("sh2", [P, 2, D])
    nrm2 = sb("nrm2", [P, D])
    yT = sb("yT", [P, KT, P])
    tmp = sb("tmp", [P, D])
    h2 = sb("h2_sb", [P, D])
    h2T = sb("h2T", [P, KT, P])
    st8 = sb("st8", [P, 8])
    ex = sb("ex", [P, NE])
    prT = sb("prT", [NE + 1, NTOK])
    zero = sb("zero", [P, D])
    sm = sb("sm", [P, 8])

    ps_m = ps("ps_m", [P, 2, 512])
    ps_h = ps("ps_h", [P, 2, 512])
    ps_r = ps("ps_r", [P, 512])
    ps_pt = ps("ps_pt", [P, 512])

    out_in = sem("out_in")
    y_static = sem("y_static")
    m_done = sem("m_done")
    out_chain = sem("out_chain")
    x1_sq = sem("x1_sq")
    h2_out = sem("h2_out")
    h2_turned = sem("h2_turned")
    h2T_done = sem("h2T_done")
    logits = sem("logits")
    exps = sem("exps")
    pr_turned = sem("pr_turned")
    prT_done = sem("prT_done")
    zero_set = sem("zero_set")
    acc_zero = sem("acc_zero")
    prT_out = sem("prT_out")
    x1_out = sem("x1_out")
    row_chain = sem("row_chain")

    pr_kept = sem("pr_kept")
    V_X1, V_MS, V_H2, V_MAX, V_ALL = 2, 3, 6, 7, 9
    block = st.enter_context(nc.Block())

    def tiles(eng, body):
        body(0, 0)
        with eng.Fori(1, NT) as t:
            body(t, 1)

    @block.sync
    def _(eng):
        rows = io["modrow"].rearrange("(e s) c -> s e c", s=2)

        def bcast(dst, section):
            for s in range(2):
                src = rows[s, section * KT:(section + 1) * KT].unsqueeze(0).to_broadcast([P, KT, P])
                eng.dma_start(dst[:, s].rearrange("p (e c) -> p e c", c=P), src).then_inc(out_in, 16)

        eng.dma_start(wo[:], io["w_out"].rearrange("(k p) n -> p k n", p=P)).then_inc(out_in, 16)
        eng.dma_start(z[:, CT:KT], io["ypool"]).then_inc(out_in, 16)
        eng.dma_start(x1[:], io["x_all"].rearrange("(t p) d -> p t d", p=P)).then_inc(out_in, 16)
        bcast(gt1, 2)
        bcast(sh2, 3)
        bcast(gn2, 4)
        eng.dma_start(nrm2[:], io["norm2"].unsqueeze(0).to_broadcast([P, D])).then_inc(out_in, 16)
        eng.dma_start(wr[:], io["w_router"].rearrange("(k p) n -> p k n", p=P)).then_inc(out_in, 16)
        eng.wait_ge(zero_set, 1)
        for t in range(NT):
            eng.dma_start(io["acc"][t * P:(t + 1) * P], zero[:]).then_inc(acc_zero, 16)

        def body(t, s):
            eng.wait_ge(out_chain, t * V_ALL + V_H2)
            dst = io["h2"][t * P:(t + 1) * P] if isinstance(t, int) else io["h2"][ds(t * P, P)]
            eng.dma_start(dst, h2[:]).then_inc(h2_out, 16)

        tiles(eng, body)
        eng.wait_ge(prT_done, NT + 1)
        eng.dma_start(io["probsT"], prT[:]).then_inc(prT_out, 16)
        eng.wait_ge(prT_out, 16)
        eng.wait_ge(out_chain, (NT - 1) * V_ALL + V_X1)
        eng.dma_start(io["x1"], x1[:]).then_inc(x1_out, 16)
        eng.wait_ge(x1_out, 16)
        eng.wait_ge(acc_zero, 16 * NT)
        eng.wait_ge(h2_out, 16 * NT)

    @block.gpsimd
    def _(eng):
        eng.memset(zero[:], 0.0).then_inc(zero_set, 1)
        eng.memset(prT[:], 0.0).then_inc(prT_done, 1)

    @block.tensor
    def _(eng):
        eng.wait_ge(out_in, 16 * 11)

        def body(t, s):
            eng.wait_ge(y_static, t + 1)
            for n in range(2):
                for k in range(KT):
                    ins = eng.matmul(ps_m[:, n], yT[:, k], wo[:, k, n * 512:(n + 1) * 512], start=(k == 0), stop=(k == KT - 1))
            ins.then_inc(m_done, 1)
            eng.wait_ge(out_chain, t * V_ALL + V_H2)
            for k in range(KT):
                ins = eng.transpose(ps_h[:, k // 4, (k % 4) * P:(k % 4 + 1) * P], h2[:, k * P:(k + 1) * P], ident)
            ins.then_inc(h2_turned, 1)
            eng.wait_ge(h2T_done, t + 1)
            for k in range(KT):
                ins = eng.matmul(ps_r[:, 0:NE], h2T[:, k], wr[:, k], start=(k == 0), stop=(k == KT - 1))
            ins.then_inc(logits, 1)
            eng.wait_ge(out_chain, t * V_ALL + V_ALL)
            eng.transpose(ps_pt[0:NE, 0:P], ex[:], ident).then_inc(pr_turned, 1)

        tiles(eng, body)

    @block.scalar
    def _(eng):
        eng.wait_ge(out_in, 16 * 11)
        eng.wait_ge(prT_done, 1)

        def body(t, s):
            cols = slice(t * P, (t + 1) * P) if isinstance(t, int) else ds(t * P, P)
            if s:
                eng.wait_ge(m_done, t)
            eng.activation(yT[:], z[:, 0:KT, cols], ACT.Copy).then_inc(y_static, 1)
            eng.wait_ge(out_chain, t * V_ALL + V_X1)
            xt = x1[:, t] if isinstance(t, int) else x1[:, ds(t, 1)].rearrange("p a d -> p (a d)")
            eng.activation(tmp[:], xt, ACT.Square, accum_out=st8[:, 0:1]).then_inc(x1_sq, 1)
            eng.wait_ge(out_chain, t * V_ALL + V_MS)
            eng.activation(st8[:, 2:3], st8[:, 1:2], ACT.Sqrt).then_inc(x1_sq, 1)
            eng.wait_ge(h2_turned, t + 1)
            eng.activation(h2T[:].rearrange("p (a k) c -> p a (k c)", a=2), ps_h[:], ACT.Copy).then_inc(h2T_done, 1)
            eng.wait_ge(out_chain, t * V_ALL + V_MAX)
            eng.activation(ex[:], ps_r[:, 0:NE], ACT.Exp, bias=sm[:, 0:1], accum_out=sm[:, 1:2]).then_inc(exps, 1)
            eng.wait_ge(pr_turned, t + 1)
            eng.activation(prT[0:NE, cols], ps_pt[0:NE, 0:P], ACT.Copy).then_inc(prT_done, 1)

        tiles(eng, body)

    @block.vector
    def _(eng):
        eng.wait_ge(out_in, 16 * 11)
        rc = Chain(eng, row_chain)
        eng.memset(probs[:], 0.0)
        for s in range(2):
            rc(eng.scalar_tensor_tensor(gn2[:, s], gn2[:, s], 1.0, nrm2[:], ALU.add, ALU.mult))

        def body(t, s):
            ch = Chain(eng, out_chain, t * V_ALL)
            xt = x1[:, t] if isinstance(t, int) else x1[:, ds(t, 1)].rearrange("p a d -> p (a d)")
            eng.wait_ge(m_done, t + 1)
            ch(eng.tensor_tensor(tmp[:], ps_m[:].rearrange("p a c -> p (a c)"), gt1[:, s], ALU.mult))
            ch(eng.tensor_tensor(xt, xt, tmp[:], ALU.add))
            eng.wait_ge(x1_sq, 2 * t + 1)
            ch(eng.tensor_scalar(st8[:, 1:2], st8[:, 0:1], 1.0 / D, RMS_EPS, ALU.mult, ALU.add))
            eng.wait_ge(x1_sq, 2 * t + 2)
            ch(eng.reciprocal(st8[:, 3:4], st8[:, 2:3]))
            if s:
                eng.wait_ge(h2_out, 16 * t)
            ch(eng.scalar_tensor_tensor(h2[:], xt, st8[:, 3:4], gn2[:, s], ALU.mult, ALU.mult))
            ch(eng.tensor_tensor(h2[:], h2[:], sh2[:, s], ALU.add))
            eng.wait_ge(logits, t + 1)
            ch(eng.tensor_reduce(sm[:, 0:1], ps_r[:, 0:NE], AXX, ALU.max, negate=True))
            eng.wait_ge(exps, t + 1)
            ch(eng.reciprocal(sm[:, 2:3], sm[:, 1:2]))
            pt = probs[:, t, 0:NE] if isinstance(t, int) else probs[:, ds(t, 1), 0:NE].rearrange("p a e -> p (a e)")
            eng.tensor_scalar(pt, ex[:], sm[:, 2:3], None, ALU.mult).then_inc(pr_kept, 1)
            eng.wait_ge(pr_kept, t + 1)
            ch(eng.tensor_scalar(ex[:], ex[:], sm[:, 2:3], None, ALU.mult))

        tiles(eng, body)


NCHUNK = 4
FC = DE // NCHUNK
FT = FC // P


def expert_phase(nc, st, io, keep):
    sb = lambda n, s, dt=F32: st.enter_context(nc.sbuf_tensor(n, s, dt))
    ps = lambda n, s: st.enter_context(nc.psum_tensor(n, s, F32))
    sem = lambda n: st.enter_context(nc.semaphore(n))
    cst, probs = keep["cst"], keep["probs"]
    ident = cst[:, 0:P]
    tie, slot, tokid = (cst[:, CCOLS[n][0]:CCOLS[n][1]] for n in ("tie", "slot", "tokid"))

    w1c = sb("w1c", [P, 2, KT, FC])
    w3c = sb("w3c", [P, 2, KT, FC])
    w2c = sb("w2c", [P, 2, FT, D])
    prow = sb("prow", [P, NTOK])
    pcol = sb("pcol", [P, NT])
    cnts = sb("cnts", [P, NT, 3])
    rank = sb("rank", [P, NT])
    before = sb("before", [P, DEC - P])
    after = sb("after", [P, DEC])
    same = sb("same", [P, P])
    hot = sb("hot", [P, NT, P])
    pick = sb("pick", [P, NT, 2])
    gate_s = sb("gate_s", [P, 2, 1])
    gate_p = sb("gate_p", [CAP_P, 2, 1])
    idx_s = sb("idx_s", [P, 2, 1], U32)
    idx_p = sb("idx_p", [CAP_P, 2, 1], U32)
    xs = sb("xs", [P, D])
    xp = sb("xp", [CAP_P, D])
    xT = sb("xT", [P, KT, SLOTS])
    sig = sb("sig", [P, 2, SLOTS])
    u = sb("u", [P, 2, SLOTS])
    he = sb("he", [P, 2, FT, SLOTS])
    yT = sb("yeT", [P, KT, SLOTS])
    ys = sb("ys", [P, D])
    yp = sb("ye_p", [CAP_P, D])

    ps_y = ps("ps_ye", [P, 3, 512])
    ps_h = [ps(f"ps_h{i}", [P, 512]) for i in range(2)]
    ps_t = ps("ps_te", [P, 2, 512])
    ps_i = ps("ps_i", [P, 512])

    w13_in = [sem(f"w13_in{b}") for b in range(2)]
    w2_in = [sem(f"w2_in{b}") for b in range(2)]
    down_done = sem("down_done")
    prow_in = sem("prow_in")
    route_v = sem("route_v")
    route_pe = sem("route_pe")
    ids_done = sem("ids_done")
    gathered = sem("gathered")
    x_turned = sem("x_turned_e")
    xT_done = sem("xT_done")
    up_ps = sem("up_ps")
    sig_done = sem("sig_done")
    u_done = sem("u_done")
    he_done = sem("he_done")
    yT_done = sem("yT_done")
    y_turned = sem("y_turned")
    y_scaled = sem("y_scaled")
    scattered = sem("scattered")

    kept = sem("kept")
    acc_free = sem("acc_free")
    rank_done = sem("rank_done")
    pool_began = sem("pool_began")
    V_RANK = 3
    w1v = io["w1"].rearrange("e (k p) f -> e p k f", p=P)
    w3v = io["w3"].rearrange("e (k p) f -> e p k f", p=P)
    w2v = io["w2"].rearrange("e (t p) d -> e p t d", p=P)
    yps = lambda k: ps_y[:, k // 3, (k % 3) * SLOTS:(k % 3 + 1) * SLOTS]

    block = st.enter_context(nc.Block())

    @block.sync
    def _(eng):
        def load(e, c, first):
            b = c % 2
            sl = lambda v: v[ds(e, 1)].rearrange("o p k f -> (o p) k f")
            if not first:
                eng.wait_ge(up_ps, (e * NCHUNK + c - 1) * FT)
            eng.dma_start(w1c[:, b], sl(w1v)[:, :, c * FC:(c + 1) * FC]).then_inc(w13_in[b], 16)
            eng.dma_start(w3c[:, b], sl(w3v)[:, :, c * FC:(c + 1) * FC]).then_inc(w13_in[b], 16)
            if not first:
                eng.wait_ge(down_done, e * NCHUNK + c - 1)
            eng.dma_start(w2c[:, b], sl(w2v)[:, c * FT:(c + 1) * FT]).then_inc(w2_in[b], 16)

        for c in range(NCHUNK):
            load(0, c, c < 2)
        with eng.Fori(1, NE) as e:
            for c in range(NCHUNK):
                load(e, c, False)

    @block.scalar
    def _(eng):
        def row(e):
            src = io["probsT"][e:e + 1] if isinstance(e, int) else io["probsT"][ds(e, 1)]
            eng.dma_start(prow[:], src.to_broadcast([P, NTOK])).then_inc(prow_in, 16)

        row(0)
        with eng.Fori(0, NE) as e:
            eng.wait_ge(rank_done, e * NT + NT)
            row(e + 1)
            eng.wait_ge(x_turned, e + 1)
            eng.activation(xT[:, :, 0:CAP_S].rearrange("p (a k) c -> p a k c", a=2),
                           ps_t[:].rearrange("p a (k c) -> p a k c", c=P), ACT.Copy)
            eng.activation(xT[:, :, CAP_S:SLOTS], ps_i[:, 0:KT * CAP_P].rearrange("p (k c) -> p k c", c=CAP_P),
                           ACT.Copy).then_inc(xT_done, 1)
            for f in range(NCHUNK * FT):
                n = e * (NCHUNK * FT) + f + 1
                eng.wait_ge(up_ps, n)
                eng.activation(sig[:, f % 2], ps_h[f % 2][:, 0:SLOTS], ACT.Sigmoid).then_inc(sig_done, 1)
            eng.wait_ge(down_done, (e + 1) * NCHUNK)
            for j in range(3):
                k0, k1 = 3 * j, min(3 * j + 3, KT)
                ins = eng.activation(yT[:, k0:k1], ps_y[:, j, 0:(k1 - k0) * SLOTS].rearrange("p (k c) -> p k c", c=SLOTS), ACT.Copy)
            ins.then_inc(yT_done, 1)
            for part, (dst, g, n) in enumerate(((ys, gate_s, P), (yp, gate_p, CAP_P))):
                eng.wait_ge(y_turned, 2 * e + part + 1)
                if part == 0:
                    eng.wait_ge(kept, e + 1)
                eng.activation(dst[:].rearrange("p (a c) -> p a c", a=2), ps_t[0:n], ACT.Copy,
                               scale=g[:, 0]).then_inc(y_scaled, 1)

    @block.gpsimd
    def _(eng):
        eng.sem_inc(acc_free, 1)

        def gather(e):
            eng.wait_ge(ids_done, e + 1)
            if not isinstance(e, int):
                eng.wait_ge(x_turned, e)
                eng.sem_inc(pool_began, 1)
            eng.indirect_dma_start(xs[:], None, io["h2"], bass.IndirectOffsetOnAxis(ap=idx_s[:, 0], axis=0)).then_inc(gathered, 16)
            eng.indirect_dma_start(xp[:], None, io["h2"], bass.IndirectOffsetOnAxis(ap=idx_p[:, 0], axis=0)).then_inc(gathered, 16)

        gather(0)
        with eng.Fori(0, NE) as e:
            gather(e + 1)
            eng.wait_ge(y_scaled, 2 * e + 2)
            eng.sem_inc(pool_began, 1)
            eng.indirect_dma_start(io["acc"], bass.IndirectOffsetOnAxis(ap=idx_s[:, 1], axis=0), ys[:], None,
                                   compute_op=ALU.add).then_inc(scattered, 16)
            eng.indirect_dma_start(io["acc"], bass.IndirectOffsetOnAxis(ap=idx_p[:, 1], axis=0), yp[:], None,
                                   compute_op=ALU.add).then_inc(scattered, 16)
            eng.wait_ge(scattered, 32 * e + 32)
            eng.sem_inc(acc_free, 1)
        eng.wait_ge(gathered, 32 * NE + 32)

    @block.vector
    def _(eng):
        def route_begin(e):
            eng.wait_ge(prow_in, 16 * e + 16)
            column = probs[:, :, e] if isinstance(e, int) else probs[:, :, ds(e, 1)].rearrange("p t o -> p (t o)")
            eng.tensor_copy(pcol[:], column)
            eng.tensor_copy(pick[:, :, 1], column)
            eng.memset(cnts[:], 0.0).then_inc(route_v, 1)
            eng.wait_ge(route_v, e * V_RANK + 1)

        def route_rank(e, t):
            if isinstance(e, int) and t == 0:
                pass
            else:
                eng.wait_ge(rank_done, e * NT + t)
            lo, hi = (0, SEQ) if t == 0 else (SEQ, NTOK)
            me = t * P
            p = pcol[:, t:t + 1]
            if me > lo:
                eng.tensor_scalar(before[:, 0:me - lo], prow[:, lo:me], p, None, ALU.is_ge, ALU.add, accum_out=cnts[:, t, 0:1])
            eng.tensor_scalar(after[:, 0:hi - me], prow[:, me:hi], p, None, ALU.is_gt, ALU.add, accum_out=cnts[:, t, 1:2])
            ins = eng.scalar_tensor_tensor(same[:], prow[:, me:me + P], p, tie, ALU.is_equal, ALU.mult,
                                           accum_out=cnts[:, t, 2:3])
            ins.then_inc(rank_done, 1)

        def route_end(e):
            eng.wait_ge(rank_done, e * NT + NT)
            eng.tensor_reduce(rank[:], cnts[:], AXX, ALU.add).then_inc(route_v, 1)
            eng.wait_ge(route_v, e * V_RANK + 2)
            for t in range(NT):
                ins = eng.tensor_scalar(hot[:, t], slot, rank[:, t:t + 1], None, ALU.is_equal)
            ins.then_inc(route_v, 1)

        def ids(e):
            eng.wait_ge(route_pe, e + 1)
            eng.tensor_copy(gate_s[:, 1], ps_i[:, 257:258])
            eng.tensor_copy(gate_p[:, 1], ps_i[0:CAP_P, 259:260])
            eng.tensor_copy(idx_s[:, 0], ps_i[:, 256:257])
            eng.tensor_copy(idx_p[:, 0], ps_i[0:CAP_P, 258:259]).then_inc(ids_done, 1)

        eng.tensor_copy(pick[:, :, 0], tokid)
        eng.sem_inc(he_done, 2)
        route_begin(0)
        for t in range(NT):
            route_rank(0, t)
        route_end(0)
        ids(0)
        with eng.Fori(0, NE) as e:
            for f in range(NCHUNK * FT):
                if f == 0:
                    route_begin(e + 1)
                n = e * (NCHUNK * FT) + f + 1
                b = (f // FT) % 2
                eng.wait_ge(sig_done, n)
                eng.tensor_tensor(u[:, f % 2], ps_h[f % 2][:, 0:SLOTS], sig[:, f % 2], ALU.mult).then_inc(u_done, 1)
                eng.wait_ge(u_done, n)
                eng.tensor_tensor(he[:, b, f % FT], ps_h[f % 2][:, SLOTS:2 * SLOTS], u[:, f % 2], ALU.mult).then_inc(he_done, 1)
                if f < NT:
                    route_rank(e + 1, f)
                if f == NT:
                    route_end(e + 1)
            eng.wait_ge(acc_free, e + 1)
            eng.wait_ge(gathered, 32 * e + 32)
            eng.tensor_copy(gate_s[:, 0], gate_s[:, 1])
            eng.tensor_copy(gate_p[:, 0], gate_p[:, 1])
            eng.tensor_copy(idx_s[:, 1], idx_s[:, 0])
            eng.tensor_copy(idx_p[:, 1], idx_p[:, 0]).then_inc(kept, 1)
            eng.wait_ge(kept, e + 1)
            ids(e + 1)

    @block.tensor
    def _(eng):
        def pick_ids(e):
            eng.wait_ge(route_v, e * V_RANK + V_RANK)
            for t in range(1, NT):
                eng.matmul(ps_i[:, 256:258], hot[:, t], pick[:, t], start=(t == 1), stop=(t == NT - 1))
            eng.matmul(ps_i[0:CAP_P, 258:260], hot[:, 0, 0:CAP_P], pick[:, 0], start=True, stop=True).then_inc(route_pe, 1)

        pick_ids(0)
        with eng.Fori(0, NE) as e:
            eng.wait_ge(gathered, 32 * e + 32)
            eng.wait_ge(ids_done, e + 1)
            for k in range(KT):
                eng.transpose(ps_t[:, k // 4, (k % 4) * P:(k % 4 + 1) * P], xs[:, k * P:(k + 1) * P], ident)
            for k in range(KT):
                ins = eng.transpose(ps_i[:, k * CAP_P:(k + 1) * CAP_P], xp[:, k * P:(k + 1) * P], ident[0:CAP_P, 0:CAP_P])
            ins.then_inc(x_turned, 1)
            eng.wait_ge(xT_done, e + 1)

            def up(c):
                b = c % 2
                eng.wait_ge(w13_in[b], 64 * e + 32 * (c // 2) + 32)
                for f in range(FT):
                    g = c * FT + f
                    eng.wait_ge(he_done, e * (NCHUNK * FT) + g + 1)
                    for w, off in ((w1c, 0), (w3c, SLOTS)):
                        for k in range(KT):
                            ins = eng.matmul(ps_h[g % 2][:, off:off + SLOTS], w[:, b, k, f * P:(f + 1) * P], xT[:, k],
                                             start=(k == 0), stop=(k == KT - 1))
                    ins.then_inc(up_ps, 1)

            def down(c):
                b = c % 2
                eng.wait_ge(w2_in[b], 32 * e + 16 * (c // 2) + 16)
                eng.wait_ge(he_done, 2 + e * (NCHUNK * FT) + (c + 1) * FT)
                for f in range(FT):
                    for k in range(KT):
                        ins = eng.matmul(yps(k), w2c[:, b, f, k * P:(k + 1) * P], he[:, b, f],
                                         start=(c == 0 and f == 0 and k % 3 == 0), stop=(c == NCHUNK - 1 and f == FT - 1),
                                         skip_group_check=True)
                ins.then_inc(down_done, 1)

            up(0)
            for c in range(1, NCHUNK):
                up(c)
                if c == NCHUNK - 1:
                    pick_ids(e + 1)
                down(c - 1)
            down(NCHUNK - 1)
            eng.wait_ge(yT_done, e + 1)
            for k in range(KT):
                ins = eng.transpose(ps_t[:, k // 4, (k % 4) * P:(k % 4 + 1) * P], yT[:, k, 0:CAP_S], ident)
            ins.then_inc(y_turned, 1)
            eng.wait_ge(y_scaled, 2 * e + 1)
            for k in range(KT):
                ins = eng.transpose(ps_t[0:CAP_P, k // 4, (k % 4) * P:(k % 4 + 1) * P], yT[:, k, CAP_S:SLOTS], ident)
            ins.then_inc(y_turned, 1)
            eng.wait_ge(y_scaled, 2 * e + 2)


def final_phase(nc, st, io, keep):
    sb = lambda n, s, dt=F32: st.enter_context(nc.sbuf_tensor(n, s, dt))
    sem = lambda n: st.enter_context(nc.semaphore(n))
    x1 = sb("x1_again", [P, NT, D])
    gt2 = sb("gt2", [P, 2, D])
    nf = sb("nf", [P, D])
    acc = sb("acc_sb", [P, NT, D])
    tmp = sb("ftmp", [P, D])
    out = sb("fout", [P, 2, D])
    s4 = sb("fs4", [P, 4])
    fin_in = sem("fin_in")
    fin_chain = sem("fin_chain")
    fin_act = sem("fin_act")
    stored = [sem(f"stored{b}") for b in range(2)]
    V_ALL = 5
    block = st.enter_context(nc.Block())

    @block.sync
    def _(eng):
        rows = io["modrow"].rearrange("(e s) c -> s e c", s=2)
        for s in range(2):
            eng.dma_start(gt2[:, s].rearrange("p (e c) -> p e c", c=P),
                          rows[s, 5 * KT:6 * KT].unsqueeze(0).to_broadcast([P, KT, P])).then_inc(fin_in, 16)
        eng.dma_start(nf[:], io["norm_f"].unsqueeze(0).to_broadcast([P, D])).then_inc(fin_in, 16)
        eng.dma_start(acc[:], io["acc"].rearrange("(t p) d -> p t d", p=P)).then_inc(fin_in, 16)
        eng.dma_start(x1[:], io["x1"]).then_inc(fin_in, 16)
        for t in range(NT):
            eng.wait_ge(fin_chain, t * V_ALL + V_ALL)
            eng.dma_start(io["y_out"][t * P:(t + 1) * P], out[:, t % 2]).then_inc(stored[t % 2], 16)
        for b in range(2):
            eng.wait_ge(stored[b], 16 * ((NT + 1 - b) // 2))

    @block.vector
    def _(eng):
        eng.wait_ge(fin_in, 80)
        ch = Chain(eng, fin_chain)
        for t in range(NT):
            ch(eng.tensor_tensor(acc[:, t], acc[:, t], gt2[:, min(t, 1)], ALU.mult))
            ch(eng.tensor_tensor(acc[:, t], acc[:, t], x1[:, t], ALU.add))
            eng.wait_ge(fin_act, 2 * t + 1)
            ch(eng.tensor_scalar(s4[:, 1:2], s4[:, 0:1], 1.0 / D, RMS_EPS, ALU.mult, ALU.add))
            eng.wait_ge(fin_act, 2 * t + 2)
            ch(eng.reciprocal(s4[:, 3:4], s4[:, 2:3]))
            if t >= 2:
                eng.wait_ge(stored[t % 2], 16 * (t // 2))
            ch(eng.scalar_tensor_tensor(out[:, t % 2], acc[:, t], s4[:, 3:4], nf[:], ALU.mult, ALU.mult))

    @block.scalar
    def _(eng):
        for t in range(NT):
            eng.wait_ge(fin_chain, t * V_ALL + 2)
            eng.activation(tmp[:], acc[:, t], ACT.Square, accum_out=s4[:, 0:1]).then_inc(fin_act, 1)
            eng.wait_ge(fin_chain, t * V_ALL + 3)
            eng.activation(s4[:, 2:3], s4[:, 1:2], ACT.Sqrt).then_inc(fin_act, 1)


PHASES = 5


def build(nc, io):
    dram = lambda n, s: nc.dram_tensor(n, s, F32).ap()
    io["modrow"] = dram("modrow", [96, P])
    io["ypool"] = dram("ypool", [P, len(WINDOWS), NTOK])
    io["h2"] = dram("h2", [NTOK, D])
    io["probsT"] = dram("probsT", [NE + 1, NTOK])
    io["x1"] = dram("x1_dram", [P, NT, D])
    io["acc"] = dram("acc", [NTOK, D])
    with ExitStack() as st:
        sb = lambda s, n, shape: s.enter_context(nc.sbuf_tensor(n, shape, F32))
        keep = {"cst": sb(st, "cst", [P, NCONST]), "probs": sb(st, "probs", [P, NT, NE + 1])}
        with ExitStack() as front:
            keep["par"] = sb(front, "par", [P, NPARAM])
            keep["mod"] = sb(front, "mod", [P, 48, 2])
            keep["z"] = sb(front, "z", [P, NZ, NTOK])
            with ExitStack() as early:
                keep["zpool"] = sb(early, "zpool", [P, 4, NTOK])
                with ExitStack() as s:
                    project_phase(nc, s, io, keep)
                if PHASES > 1:
                    with ExitStack() as s:
                        pool_phase(nc, s, io, keep)
            if PHASES > 1:
                with ExitStack() as s:
                    scan_phase(nc, s, io, keep)
            if PHASES > 2:
                with ExitStack() as s:
                    output_phase(nc, s, io, keep)
        if PHASES > 3:
            with ExitStack() as s:
                expert_phase(nc, s, io, keep)
            with ExitStack() as s:
                final_phase(nc, s, io, keep)


def constants():
    c = np.zeros((P, NCONST), np.float32)

    def put(name, a):
        c[:, CCOLS[name][0]:CCOLS[name][1]] = a.reshape(P, -1)

    i = np.arange(P)
    put("ident", np.eye(P, dtype=np.float32))
    put("blk", (i[:, None] // HS == i[None] // HS).astype(np.float32))
    j = i[:, None]
    t = i[None]
    put("eye", (j % HS == t[:, :HS]).astype(np.float32))
    lvl = np.zeros((P, 2, LEVELS, CH), np.float32)
    mask = np.zeros((P, 2, 3, CH), np.float32)
    for d, (strict, incl) in enumerate(((j < t, j <= t), (j > t, j >= t))):
        for lv in range(LEVELS):
            s = 1 << lv
            lvl[:, d, lv] = strict & (j // (2 * s) == t // (2 * s)) & (j // s != t // s)
        for k in range(3):
            mask[:, d, k] = incl if k % 2 else strict
    put("lvl", lvl)
    put("mask", mask)
    put("tie", (i[None] < i[:, None]).astype(np.float32))
    put("slot", np.broadcast_to(i[None].astype(np.float32), (P, P)))
    put("tokid", (i[:, None] + P * np.arange(NT)[None]).astype(np.float32))
    reset = (np.arange(NTOK) % CH != 0).astype(np.float32)
    inv = np.zeros((len(WINDOWS), NTOK), np.float32)

    def count(n, win):
        pos = np.arange(n)
        return (np.clip(pos + win - win // 2, 0, n) - np.clip(pos - win // 2, 0, n)).astype(np.float64)

    for g, win in enumerate(WINDOWS):
        inv[g, :SEQ] = 1.0 / count(SEQ, win)
        inv[g, SEQ:] = (1.0 / (count(ROWS, win)[:, None] * count(GRID_W, win)[None])).reshape(-1)
    return c, reset, inv


def kernel(**inputs):
    import concourse.bacc as bacc
    from concourse.bass_utils import run_bass_kernel_spmd

    a = {n: np.asarray(v) for n, v in inputs.items()}
    cols = lambda v: np.ascontiguousarray(v.reshape(-1, P).T)
    par = np.zeros((P, NPARAM), np.float32)
    par[:, 0:16:2] = cols(a["c_ctx"])
    par[:, 1:16:2] = cols(a["c"][0])
    for name, v in (("norm1", a["norm1"][0]), ("ada_b", a["ada_b"][0]), ("mu", a["mu_shift"][0]), ("pool_scale", a["pool_scale"][0])):
        par[:, PCOLS[name][0]:PCOLS[name][1]] = cols(v)
    for name, v in (("w0f", a["w0"][0, 0]), ("w0b", a["w0"][0, 1]), ("a0f", a["a0"][0, 0]), ("a0b", a["a0"][0, 1]),
                    ("k_k", a["k_k"][0]), ("k_a", a["k_a"][0]), ("r_k", a["r_k"][0]), ("ln_w", a["ln_x_w"][0]), ("ln_b", a["ln_x_b"][0])):
        lo = PCOLS["head"][0] + HP[name]
        par[:, lo:lo + 40:10] = cols(v)
    consts, reset, inv = constants()
    state0 = np.ascontiguousarray(a["state_rwkv"][0, 0].transpose(0, 1, 3, 2)).reshape(2, CT, P, HS)
    arrays = {
        "consts": consts, "params": par, "reset": reset, "inv_cnt": inv, "state0": state0,
        "x_all": np.concatenate([a["x_prompt"][0], a["x_sample"][0]]),
        "ada_w": a["ada_w"][0], "w_in": a["w_in"][0], "pool_w": a["pool_w"][0],
        "w_up": a["w_up"][0].reshape(P, DR), "a_up": a["a_up"][0].reshape(P, DR), "g_up": a["g_up"][0],
        "w_out": a["w_out"][0], "norm2": a["norm2"][0], "norm_f": a["norm_f"], "w_router": a["w_router"][0],
        "w1": a["w1"][0], "w3": a["w3"][0], "w2": a["w2"][0],
    }
    arrays = {n: np.ascontiguousarray(v) for n, v in arrays.items()}
    nc = bacc.Bacc("TRN2", target_bir_lowering=False, num_devices=1)
    io = {n: nc.dram_tensor(f"in_{n}", v.shape, F32, kind="ExternalInput").ap() for n, v in arrays.items()}
    io["y_out"] = nc.dram_tensor("out_y", [NTOK, D], F32, kind="ExternalOutput").ap()
    io["state_out"] = nc.dram_tensor("out_state", [2, CT, P, HS], F32, kind="ExternalOutput").ap()
    build(nc, io)
    r = run_bass_kernel_spmd(nc, [{f"in_{n}": v for n, v in arrays.items()}], core_ids=[0]).results[0]
    y = r["out_y"]
    state = r["out_state"].reshape(2, 2 * CT, HS, HS).transpose(0, 1, 3, 2)
    return y[None, :SEQ], y[None, SEQ:], np.ascontiguousarray(state)[None, None]
```

```python
from contextlib import ExitStack

import numpy as np

import concourse.bass as bass
from concourse import mybir

ALU = mybir.AluOpType
ACT = mybir.ActivationFunctionType
AXX = mybir.AxisListType.X
F32 = mybir.dt.float32
U32 = mybir.dt.uint32
ds = bass.ds

P = 128
D = 1024
KT = D // P
SEQ, DEC = 128, 1024
NTOK = SEQ + DEC
NT = NTOK // P
GRID_W = 64
ROWS = DEC // GRID_W
DR = 512
HS = 64
CT = DR // P
NPROJ = 19
NZ = 15
T_R, T_K, T_V, T_G, T_W, T_A, T_POOL = 0, 4, 8, 12, 13, 14, 15
CH = 128
NCH = NTOK // CH
LEVELS = 7
WINDOWS = (2, 4, 8, 16)
NE = 16
DE = 2 * D
CAP_S = 2 * DEC // NE
CAP_P = 2 * SEQ // NE
SLOTS = CAP_S + CAP_P
RMS_EPS = 1e-6
GN_EPS = 64e-5
DECAY_C = float(np.exp(-0.5))
PIECE = NTOK // 3

PCOLS = {}
_n = 0
for _name, _k in (("c", 16), ("norm1", 8), ("ada_b", 48), ("mu", NZ), ("pool_scale", 4), ("head", 4 * 10)):
    PCOLS[_name] = (_n, _n + _k)
    _n += _k
NPARAM = _n
HP = {n: i for i, n in enumerate(("w0f", "w0b", "a0f", "a0b", "k_k", "k_a", "r_k", "ln_w", "ln_b", "zero"))}

CCOLS = {}
_n = 0
for _name, _k in (("ident", P), ("blk", P), ("eye", HS), ("lvl", 2 * LEVELS * CH), ("mask", 2 * 3 * CH),
                  ("tie", P), ("slot", P), ("tokid", NT)):
    CCOLS[_name] = (_n, _n + _k)
    _n += _k
NCONST = _n


class Steps:

    def __init__(self, names):
        self.names = names
        self.n = {x: i + 1 for i, x in enumerate(names)}
        assert len(self.n) == len(names)

    def __len__(self):
        return len(self.names)

    def __getitem__(self, name):
        return self.n[name]


class Signals:

    def __init__(self, sem, steps):
        self.sem, self.steps, self.at = sem, steps, 0

    def done(self, name, ins):
        assert self.steps.names[self.at] == name, (self.steps.names[self.at], name)
        self.at += 1
        ins.then_inc(self.sem, 1)


class Chain:

    def __init__(self, eng, sem, base=0):
        self.eng, self.sem, self.base, self.n = eng, sem, base, 0

    def __call__(self, ins):
        ins.then_inc(self.sem, 1)
        self.n += 1
        self.eng.wait_ge(self.sem, self.base + self.n)


def project_phase(nc, st, io, keep):
    sb = lambda n, s, dt=F32: st.enter_context(nc.sbuf_tensor(n, s, dt))
    ps = lambda n, s: st.enter_context(nc.psum_tensor(n, s, F32))
    sem = lambda n: st.enter_context(nc.semaphore(n))
    cst, par, z, zpool, mod = (keep[n] for n in ("cst", "par", "z", "zpool", "mod"))

    hT = keep["wide"][:].rearrange("p (k c) -> p k c", k=KT)
    ada = sb("ada", [P, 2, KT, 256])
    xt = sb("xt", [P, 2, D])
    win = sb("win", [P, 2, KT, P])
    pad = sb("pad", [P, 2, NTOK + 3])
    nsum = sb("nsum", [P, NTOK + 1])
    silu_c = sb("silu_c", [P, KT, 2])
    sig_c = sb("sig_c", [P, 16])
    sq = sb("sq", [P, D])
    ss = sb("ss", [P, 8])
    g1 = sb("g1", [P, KT, 2])
    mus = sb("mus", [P, 2, NZ])
    modT = sb("modT", [96, P])

    ps_mod = ps("ps_mod", [P, 512])
    ps_t = ps("ps_t", [P, 2, 512])
    ps_p = ps("ps_p", [P, 3, 512])

    const_in = sem("const_in")
    silu_done = sem("silu_done")
    ada_in = [sem(f"ada_in{b}") for b in range(2)]
    ada_used = sem("ada_used")
    mod_done = sem("mod_done")
    modT_out = sem("modT_out")
    mod_sb = sem("mod_sb")
    x_in = [sem(f"x_in{b}") for b in range(2)]
    x_scaled = sem("x_scaled")
    x_turned = sem("x_turned")
    x_stored = sem("x_stored")
    sq_done = sem("sq_done")
    rms_v = sem("rms_v")
    rms_s = sem("rms_s")
    h_done = sem("h_done")
    win_in = [sem(f"win_in{b}") for b in range(2)]
    win_used = sem("win_used")
    p_copied = sem("p_copied")
    pad_used = sem("pad_used")
    pad_zero = sem("pad_zero")
    modrow_out = sem("modrow_out")
    pool_copied = sem("pool_copied")
    pre_chain = sem("pre_chain")
    shift_chain = sem("shift_chain")

    NADA = 6 * D // 256
    NROUND = NADA // 2
    ada_v = io["ada_w"].rearrange("(k p) e -> p k e", p=P)
    win_v = io["w_in"].rearrange("(k p) e -> p k e", p=P)
    x_v = io["x_all"].rearrange("(t p) d -> t p d", p=P)

    block = st.enter_context(nc.Block())

    @block.sync
    def _(eng):
        eng.dma_start(cst[:], io["consts"]).then_inc(const_in, 16)
        eng.dma_start(par[:], io["params"]).then_inc(const_in, 16)
        for b in range(2):
            eng.dma_start(xt[:, b], x_v[b]).then_inc(x_in[b], 16)
        for b in range(2):
            eng.dma_start(win[:, b], win_v[:, :, b * P:(b + 1) * P]).then_inc(win_in[b], 16)
            eng.dma_start(ada[:, b], ada_v[:, :, b * 256:(b + 1) * 256]).then_inc(ada_in[b], 16)
        for t in range(2, NT):
            eng.wait_ge(x_turned, t - 1)
            eng.dma_start(xt[:, t % 2], x_v[t]).then_inc(x_in[t % 2], 16)
        with eng.Fori(1, NROUND) as i:
            for b in range(2):
                eng.wait_ge(ada_used, 2 * i - 1 + b)
                eng.dma_start(ada[:, b], ada_v[:, :, ds(i * 512 + b * 256, 256)]).then_inc(ada_in[b], 16)
        with eng.Fori(1, NPROJ // 2) as i:
            for b in range(2):
                eng.wait_ge(win_used, 2 * i - 1 + b)
                eng.dma_start(win[:, b], win_v[:, :, ds(i * 256 + b * P, P)]).then_inc(win_in[b], 16)
        eng.wait_ge(win_used, NPROJ - 2)
        eng.dma_start(win[:, 0], win_v[:, :, (NPROJ - 1) * P:NPROJ * P]).then_inc(win_in[0], 16)
        eng.wait_ge(modT_out, 1)
        eng.dma_start(io["modrow"], modT[:, :]).then_inc(modrow_out, 16)
        eng.wait_ge(modrow_out, 16)

    @block.gpsimd
    def _(eng):
        eng.memset(pad[:], 0.0).then_inc(pad_zero, 1)

    @block.scalar
    def _(eng):
        eng.wait_ge(const_in, 32)
        eng.activation(sig_c[:], par[:, 0:16], ACT.Sigmoid).then_inc(silu_done, 1)
        for t in range(NT):
            b = t % 2
            eng.wait_ge(x_in[b], 16 * (t // 2 + 1))
            if t >= 1:
                eng.wait_ge(rms_v, 3 * t)
            eng.activation(sq[:], xt[:, b], ACT.Square, accum_out=ss[:, 0:1]).then_inc(sq_done, 1)
            eng.wait_ge(rms_v, 3 * t + 1)
            eng.activation(ss[:, 2:3], ss[:, 1:2], ACT.Sqrt).then_inc(rms_s, 1)
            eng.wait_ge(x_turned, t + 1)
            eng.activation(hT[:, :, t * P:(t + 1) * P], ps_t[:].rearrange("p a (k c) -> p (a k) c", c=P),
                           ACT.Copy).then_inc(x_stored, 1)

        def project(m, b, first):
            eng.wait_ge(win_used, m + 1)
            if not first:
                eng.wait_ge(pad_used, m - 1)
            eng.activation(pad[:, b, 1:1 + SEQ], ps_p[:, 0, 0:SEQ], ACT.Copy).then_inc(p_copied, 1)
            eng.activation(pad[:, b, 2 + SEQ:2 + PIECE], ps_p[:, 0, SEQ:PIECE], ACT.Copy).then_inc(p_copied, 1)
            eng.activation(pad[:, b, 2 + PIECE:2 + NTOK].rearrange("p (a c) -> p a c", a=2),
                           ps_p[:, 1:3, 0:PIECE], ACT.Copy).then_inc(p_copied, 1)

        eng.wait_ge(pad_zero, 1)
        project(0, 0, True)
        project(1, 1, True)
        with eng.Fori(1, NPROJ // 2) as i:
            for b in range(2):
                project(2 * i + b, b, False)
        project(NPROJ - 1, 0, False)

    @block.vector
    def _(eng):
        ch = Chain(eng, pre_chain)
        eng.wait_ge(silu_done, 1)
        ch(eng.tensor_tensor(silu_c[:].rearrange("p k s -> p (k s)"), sig_c[:], par[:, 0:16], ALU.mult))
        m0, m1 = PCOLS["mu"]
        ch(eng.tensor_scalar(mus[:, 0], par[:, m0:m1], -1.0, 1.0, ALU.mult, ALU.add))
        ch(eng.tensor_scalar(mus[:, 1], par[:, m0:m1], 0.5, None, ALU.mult))
        for t in range(NT):
            b = t % 2
            eng.wait_ge(sq_done, t + 1)
            eng.tensor_scalar(ss[:, 1:2], ss[:, 0:1], 1.0 / D, RMS_EPS, ALU.mult, ALU.add).then_inc(rms_v, 1)
            eng.wait_ge(rms_s, t + 1)
            eng.reciprocal(ss[:, 3:4], ss[:, 2:3]).then_inc(rms_v, 1)
            eng.wait_ge(rms_v, 3 * t + 2)
            eng.tensor_scalar(xt[:, b], xt[:, b], ss[:, 3:4], None, ALU.mult).then_inc(rms_v, 1)
        eng.wait_ge(mod_done, 1)
        a0, a1 = PCOLS["ada_b"]
        ch(eng.tensor_tensor(mod[:], ps_mod[:, 0:96].rearrange("p (e s) -> p e s", s=2),
                             par[:, a0:a1].unsqueeze(2).to_broadcast([P, 48, 2]), ALU.add))
        n0, n1 = PCOLS["norm1"]
        ch(eng.tensor_scalar(g1[:], mod[:, KT:2 * KT], 1.0, None, ALU.add))
        ch(eng.tensor_tensor(g1[:], g1[:], par[:, n0:n1].unsqueeze(2).to_broadcast([P, KT, 2]), ALU.mult))
        eng.sem_inc(mod_sb, 1)
        eng.wait_ge(x_stored, NT)
        for k in range(KT):
            for s, (lo, hi) in enumerate(((0, SEQ), (SEQ, NTOK))):
                eng.tensor_scalar(hT[:, k, lo:hi], hT[:, k, lo:hi], g1[:, k, s:s + 1], mod[:, k, s:s + 1],
                                  ALU.mult, ALU.add).then_inc(h_done, 1)
        eng.wait_ge(mod_done, 2)
        eng.tensor_copy(modT[:, :], ps_mod[0:96, 128:256]).then_inc(modT_out, 1)

        def shift(m, b, sh):
            eng.wait_ge(p_copied, 3 * m + 3)
            sh(eng.tensor_tensor(nsum[:], pad[:, b, 0:NTOK + 1], pad[:, b, 2:NTOK + 3], ALU.add))
            for lo, hi, g in ((0, SEQ, 0), (SEQ, NTOK, 1)):
                eng.tensor_scalar(z[:, m, lo:hi] if isinstance(m, int) else z[:, ds(m, 1), lo:hi],
                                  pad[:, b, 1 + lo + g:1 + hi + g] if isinstance(m, int) else pad[:, b:b + 1, 1 + lo + g:1 + hi + g],
                                  mus[:, 0, m:m + 1] if isinstance(m, int) else mus[:, 0, ds(m, 1)],
                                  None, ALU.mult).then_inc(shift_chain, 1)
            sh.n += 2
            eng.wait_ge(shift_chain, sh.base + sh.n)
            eng.tensor_scalar(nsum[:], nsum[:], mus[:, 1, m:m + 1] if isinstance(m, int) else mus[:, 1, ds(m, 1)],
                              None, ALU.mult).then_inc(shift_chain, 1)
            sh.n += 1
            eng.wait_ge(shift_chain, sh.base + sh.n)
            for lo, hi, g in ((0, SEQ, 0), (SEQ, NTOK, 1)):
                zz = z[:, m, lo:hi] if isinstance(m, int) else z[:, ds(m, 1), lo:hi].rearrange("p a c -> p (a c)")
                eng.tensor_tensor(zz, zz, nsum[:, lo + g:hi + g], ALU.add).then_inc(shift_chain, 1)
            sh.n += 2
            eng.wait_ge(shift_chain, sh.base + sh.n)
            eng.sem_inc(pad_used, 1)

        PER = 6
        sh = Chain(eng, shift_chain)
        with eng.Fori(0, NZ // 2) as i:
            for b in range(2):
                sh = Chain(eng, shift_chain, (2 * i + b) * PER)
                shift(2 * i + b, b, sh)
        shift(NZ - 1, 0, Chain(eng, shift_chain, (NZ - 1) * PER))
        for m in range(NZ, NPROJ):
            eng.wait_ge(p_copied, 3 * m + 3)
            eng.tensor_copy(zpool[:, m - NZ, 0:SEQ], pad[:, m % 2, 1:1 + SEQ]).then_inc(pool_copied, 1)
            eng.tensor_copy(zpool[:, m - NZ, SEQ:NTOK], pad[:, m % 2, 2 + SEQ:2 + NTOK]).then_inc(pad_used, 1)

    @block.tensor
    def _(eng):
        ident = cst[:, 0:P]
        eng.wait_ge(const_in, 32)
        for t in range(NT):
            eng.wait_ge(rms_v, 3 * t + 3)
            if t >= 1:
                eng.wait_ge(x_stored, t)
            for k in range(KT):
                ins = eng.transpose(ps_t[:, k // 4, (k % 4) * P:(k % 4 + 1) * P], xt[:, t % 2, k * P:(k + 1) * P], ident)
            ins.then_inc(x_turned, 1)
        eng.wait_ge(pre_chain, 1)
        with eng.Fori(0, NROUND) as i:
            for b in range(2):
                eng.wait_ge(ada_in[b], 16 * i + 16)
                for e in range(2):
                    for k in range(KT):
                        ins = eng.matmul(ps_mod[:, ds(i * 8 + b * 4 + e * 2, 2)], ada[:, b, k, e * P:(e + 1) * P],
                                         silu_c[:, k], start=(k == 0), stop=(k == KT - 1))
                ins.then_inc(ada_used, 1)
        eng.wait_ge(ada_used, NADA)
        eng.sem_inc(mod_done, 1)
        eng.wait_ge(mod_sb, 1)
        eng.transpose(ps_mod[0:96, 128:256], mod[:].rearrange("p e s -> p (e s)"), ident).then_inc(mod_done, 1)
        eng.wait_ge(h_done, 2 * KT)

        def project(m, b, first):
            eng.wait_ge(win_in[b], 16 * (m // 2 + 1) if isinstance(m, int) else m * 8 - 8 * b + 16)
            if not first:
                eng.wait_ge(p_copied, 3 * m)
            for c in range(3):
                for k in range(KT):
                    ins = eng.matmul(ps_p[:, c, 0:PIECE], win[:, b, k], hT[:, k, c * PIECE:(c + 1) * PIECE],
                                     start=(k == 0), stop=(k == KT - 1))
            ins.then_inc(win_used, 1)

        project(0, 0, True)
        project(1, 1, False)
        with eng.Fori(1, NPROJ // 2) as i:
            for b in range(2):
                project(2 * i + b, b, False)
        project(NPROJ - 1, 0, False)


def pool_phase(nc, st, io, keep):
    sb = lambda n, s, dt=F32: st.enter_context(nc.sbuf_tensor(n, s, dt))
    sem = lambda n: st.enter_context(nc.semaphore(n))
    zpool, par = keep["zpool"], keep["par"]
    NG = len(WINDOWS)
    cnt, diff = (keep["wide"][:, j * NG * NTOK:(j + 1) * NG * NTOK].rearrange("p (g c) -> p g c", g=NG) for j in range(2))
    seq = sb("seq", [P, 2, SEQ + 16])
    col = sb("col", [P, 2, ROWS, GRID_W + 16])
    row = sb("row", [P, 2, ROWS + 16, GRID_W])
    pw = sb("pw", [P, NG, P])
    yp = sb("yp", [P, NG, NTOK])
    ps_y = st.enter_context(nc.psum_tensor("ps_y", [P, 2, 3, 512], F32))
    pool_in = sem("pool_in")
    pool_chain = sem("pool_chain")
    diff_done = sem("diff_done")
    y_ready = sem("y_ready")
    y_copied = sem("y_copied")
    y_out = sem("y_out")
    zero = sb("zero", [P, D])
    zero_set = sem("zero_set")
    acc_zero = sem("acc_zero")
    block = st.enter_context(nc.Block())

    @block.gpsimd
    def _(eng):
        eng.memset(zero[:], 0.0).then_inc(zero_set, 1)

    @block.sync
    def _(eng):
        eng.dma_start(pw[:], io["pool_w"].rearrange("g c d -> c g d")).then_inc(pool_in, 16)
        eng.dma_start(cnt[:], io["inv_cnt"].unsqueeze(0).to_broadcast([P, NG, NTOK])).then_inc(pool_in, 16)
        eng.wait_ge(zero_set, 1)
        for t in range(NT):
            eng.dma_start(io["acc"][t * P:(t + 1) * P], zero[:]).then_inc(acc_zero, 16)
        eng.wait_ge(y_copied, NG)
        eng.dma_start(io["ypool"], yp[:]).then_inc(y_out, 16)
        eng.wait_ge(y_out, 16)
        eng.wait_ge(acc_zero, 16 * NT)

    @block.vector
    def _(eng):
        ch = Chain(eng, pool_chain)
        eng.wait_ge(pool_in, 32)
        for g, win in enumerate(WINDOWS):
            hi = win - 1 - win // 2
            zg = zpool[:, g]
            for t in (seq, col, row):
                ch(eng.memset(t[:], 0.0))
            ch(eng.tensor_copy(seq[:, 0, 0:SEQ], zg[:, 0:SEQ]))
            ch(eng.tensor_copy(col[:, 0, :, 0:GRID_W], zg[:, SEQ:NTOK].rearrange("p (r c) -> p r c", c=GRID_W)))

            def doubled(buf):
                step, cur = 1, 0
                while step < win:
                    ch(eng.tensor_tensor(buf(1 - cur, step, None), buf(cur, step, None), buf(cur, 0, -step), ALU.add))
                    ch(eng.tensor_copy(buf(1 - cur, 0, step), buf(cur, 0, step)))
                    step, cur = 2 * step, 1 - cur
                return cur

            n = doubled(lambda i, a, b: seq[:, i, a:b])
            ch(eng.tensor_tensor(diff[:, g, 0:SEQ], seq[:, n, hi:hi + SEQ], cnt[:, g, 0:SEQ], ALU.mult))
            n = doubled(lambda i, a, b: col[:, i, :, a:b])
            ch(eng.tensor_copy(row[:, 0, 0:ROWS], col[:, n, :, hi:hi + GRID_W]))
            n = doubled(lambda i, a, b: row[:, i, a:b])
            ch(eng.tensor_tensor(diff[:, g, SEQ:NTOK], row[:, n, hi:hi + ROWS].rearrange("p r c -> p (r c)"),
                                 cnt[:, g, SEQ:NTOK], ALU.mult))
            eng.tensor_tensor(diff[:, g], diff[:, g], zg, ALU.subtract).then_inc(diff_done, 1)

    @block.tensor
    def _(eng):
        for g in range(NG):
            eng.wait_ge(diff_done, g + 1)
            if g >= 2:
                eng.wait_ge(y_copied, g - 1)
            for c in range(3):
                ins = eng.matmul(ps_y[:, g % 2, c, 0:PIECE], pw[:, g], diff[:, g, c * PIECE:(c + 1) * PIECE],
                                 start=True, stop=True)
            ins.then_inc(y_ready, 1)

    @block.scalar
    def _(eng):
        s0 = PCOLS["pool_scale"][0]
        for g in range(NG):
            eng.wait_ge(y_ready, g + 1)
            eng.activation(yp[:, g].rearrange("p (a c) -> p a c", a=3), ps_y[:, g % 2, :, 0:PIECE], ACT.Copy,
                           scale=par[:, s0 + g:s0 + g + 1]).then_inc(y_copied, 1)


CHUNK_PE = ([f"AB{u}" for u in range(4)] + ["TOK0", "TOK1"] + [f"D{u}" for u in range(4)] + [f"X0_{u}" for u in range(4)]
            + [f"{k}{lv}_{u}" for lv in range(1, LEVELS) for k in "XT" for u in range(4)]
            + [f"WU{u}" for u in range(4)] + ["FIN0", "FIN1", "Y0"])
CHUNK_DVE = ([f"AB{u}" for u in range(4)] + [f"X0_{u}" for u in range(4)]
             + [f"T{lv}_{u}" for lv in range(1, LEVELS) for u in range(4)] + ["FIN0", "FIN1"])
CHUNK_ACT = (["V", "RH", "TOK0", "TOK1"] + [f"D{u}" for u in range(4)]
             + [f"X{lv}_{u}" for lv in range(1, LEVELS) for u in range(4)]
             + [f"WU{u}" for u in range(4)] + ["FIN0", "FIN1", "Y0"])
CHUNK_POOL = [f"L{lv}_{u}" for lv in range(2) for u in range(4)] + [f"TT{u}" for u in range(4)]
CHUNK_POOL += [f"L{lv}_{u}" for lv in range(2, LEVELS) for u in range(4)]
SPANS = ((0, 1), (1, 4), (5, 4))


def scan_phase(nc, st, io, keep):
    sb = lambda n, s, dt=F32: st.enter_context(nc.sbuf_tensor(n, s, dt))
    sem = lambda n: st.enter_context(nc.semaphore(n))
    cst, par, z = keep["cst"], keep["par"], keep["z"]

    def const(name):
        return cst[:, CCOLS[name][0]:CCOLS[name][1]]

    ident, blk, eye = const("ident"), const("blk"), const("eye")
    lvl = const("lvl").rearrange("p (d l c) -> p d l c", d=2, l=LEVELS)
    mask = const("mask").rearrange("p (d k c) -> p d k c", d=2, k=3)

    reset = sb("reset", [P, NTOK])
    hp = sb("hp", [P, 10])
    ka1 = sb("ka1", [P, 1])
    up_w = sb("up_w", [P, P])
    up_a = sb("up_a", [P, P])
    up_g = sb("up_g", [P, P])
    l_in, l_ex, kd, nb = (keep["wide"][:, j * 2 * NTOK:(j + 1) * 2 * NTOK].rearrange("p (d c) -> p d c", d=2) for j in range(4))
    cen = sb("cen", [P, 2, NCH])
    ncen = sb("ncen", [P, 2, NCH])
    e_cen = sb("e_cen", [P, 2, NCH])
    kk = sb("kk", [P, NTOK])
    y = sb("y", [P, NTOK])
    m_all = sb("m_all", [P, 2, NTOK])
    r_all = sb("r_all", [P, 2, NTOK])
    n_all = sb("n_all", [P, 2, NTOK])
    eps = sb("eps", [P, 1])
    ex_w = sb("ex_w", [P, 3, 2, CH])
    kr_w = sb("kr_w", [P, 2, 2, 2, CH])
    kh_w = sb("kh_w", [P, 2, CH])
    nb_w = sb("nb_w", [P, 2, CH])
    v_w = sb("v_w", [P, CH])
    ab_w = sb("ab_w", [P, 4, 3, CH])
    np_w = sb("np_w", [P, 4, HS + CH])
    lm_w = sb("lm_w", [P, 4, 2, CH])
    kt_w = sb("kt_w", [P, 2, CH])
    tokv_w = sb("tokv_w", [P, CH])
    kd_w = sb("kd_w", [P, 4, 2, HS])
    x_w = sb("x_w", [P, 4, CH])
    t_w = sb("t_w", [P, 4, 2, CH])
    wu_w = sb("wu_w", [P, 4, 2, HS])
    rh_w = sb("rh_w", [P, 2, CH])
    mr_w = sb("mr_w", [P, 2, HS + CH])
    zst = sb("zst", [P, 2, 2, HS])
    z0s = sb("z0s", [P, 2, CT, HS])

    banks = [st.enter_context(nc.psum_tensor(f"bank{i}", [P, 512], F32)) for i in range(8)]
    T_BANK = [banks[i] for i in (4, 5, 0, 1)]
    X_BANK = [banks[i] for i in (2, 3, 6, 7)]
    TOK_BANK = banks[6:8]
    FIN_BANK = banks[2:4]
    V_BANK, Y_BANK = banks[2], banks[6]

    scan_in = sem("scan_in")
    up_in = sem("up_in")
    lora_act = sem("lora_act")
    pre_pe = sem("pre_pe")
    pre_act = sem("pre_act")
    chain_v = sem("chain_v")
    chunk_pe = sem("chunk_pe")
    chunk_dve = sem("chunk_dve")
    chunk_act = sem("chunk_act")
    chunk_pool = sem("chunk_pool")
    state_pe = sem("state_pe")
    state_dve = sem("state_dve")
    gn_pe = sem("gn_pe")
    gn_act = sem("gn_act")
    state_out = sem("state_out")
    pre_free = sem("pre_free")
    pe_began = sem("pe_began")
    kd_ready = sem("kd_ready")
    mean_off = sem("mean_off")
    bonus_v = sem("bonus_v")
    kr_zero = sem("kr_zero")
    fin_sum = sem("fin_sum")
    ex_ready = sem("ex_ready")
    prod_ready = sem("prod_ready")

    PE_N, DVE_N, ACT_N, POOL_N = (Steps(x) for x in (CHUNK_PE, CHUNK_DVE, CHUNK_ACT, CHUNK_POOL))
    PRE_PE = Steps(["w0", "w1", "a0", "a1", "kk"])
    PRE_ACT = Steps(["w0", "w1", "a0", "a1", "ksq", "kroot", "e_cen"])
    GN_PE = Steps(["mean", "var", "bonus", "gate"])
    GN_ACT = Steps(["sq", "root", "gate"])
    V_CEN = 8
    V_PRE = 11
    V_ALL = 25
    DV0 = 1
    LV_NEXT = 3
    NSPAN = 2 * len(SPANS)
    S_ALL = 2 * NCH + 4
    H = (slice(0, HS), slice(HS, P))
    FWD = list(range(NCH))
    BWD = [0] + list(range(NCH - 1, 0, -1))

    def three(bank0):
        return [banks[bank0 + i][:, 0:PIECE] for i in range(3)]

    def pieces(ap):
        return [ap[:, c * PIECE:(c + 1) * PIECE] for c in range(3)]

    def chunks(eng, body):
        with eng.Fori(0, NCH - 1) as i:
            body(i, True)
        body(NCH - 1, False)

    block = st.enter_context(nc.Block())

    @block.sync
    def _(eng):
        eng.dma_start(reset[:], io["reset"].unsqueeze(0).to_broadcast([P, NTOK])).then_inc(scan_in, 16)
        eng.dma_start(z0s[:], io["state0"].rearrange("d t p v -> p d t v")).then_inc(scan_in, 16)
        with eng.Fori(0, CT) as t:
            eng.wait_ge(pre_free, t + 1)
            eng.dma_start(up_w[:], io["w_up"][:, ds(t * P, P)]).then_inc(up_in, 16)
            eng.dma_start(up_a[:], io["a_up"][:, ds(t * P, P)]).then_inc(up_in, 16)
            eng.dma_start(up_g[:], io["g_up"][:, ds(t * P, P)]).then_inc(up_in, 16)
            for d in range(2):
                eng.wait_ge(state_dve, t * S_ALL + 3 + d)
                eng.dma_start(io["state_out"][d, ds(t, 1)].rearrange("o p v -> (o p) v"), zst[:, d, 1]).then_inc(state_out, 16)
        eng.wait_ge(state_out, 32 * CT)

    @block.gpsimd
    def _(eng):
        eng.memset(eps[:], GN_EPS).then_inc(pre_free, 1)
        eng.memset(kr_w[:], 0.0).then_inc(kr_zero, 1)
        with eng.Fori(0, CT) as t:
            with eng.Fori(0, NCH) as i:
                it = t * NCH + i
                dve, pe, own = DV0 + it * len(DVE_N), it * len(PE_N), it * len(POOL_N)
                sg = Signals(chunk_pool, POOL_N)

                def level(lv, u):
                    sg.done(f"L{lv}_{u}", eng.tensor_tensor(lm_w[:, u, lv % 2], ab_w[:, u, 2], lvl[:, u // 2, lv], ALU.mult))

                for lv in range(2):
                    for u in range(4):
                        if lv == 0:
                            eng.wait_ge(chunk_dve, dve + DVE_N[f"AB{u}"])
                        level(lv, u)
                for u in range(4):
                    eng.wait_ge(chunk_pool, own + POOL_N[f"L0_{u}"])
                    sg.done(f"TT{u}", eng.tensor_tensor(t_w[:, u, 1], lm_w[:, u, 0], ident, ALU.add))
                for lv in range(2, LEVELS):
                    for u in range(4):
                        eng.wait_ge(chunk_pe, pe + PE_N[f"X{lv - 2}_{u}"])
                        if lv == 2:
                            eng.wait_ge(chunk_pool, own + POOL_N[f"TT{u}"])
                        level(lv, u)

    @block.scalar
    def _(eng):
        eng.wait_ge(pre_free, 1)
        eng.activation(z[:, T_W], z[:, T_W], ACT.Tanh).then_inc(lora_act, 1)
        eng.activation(z[:, T_G], z[:, T_G], ACT.Sigmoid).then_inc(lora_act, 1)
        with eng.Fori(0, CT) as t:
            sg = Signals(pre_act, PRE_ACT)
            pp = t * len(PRE_PE)
            vc = t * V_ALL
            eng.wait_ge(chain_v, vc + 1)
            for n, (name, out, bias) in enumerate((("w0", l_ex[:, 0], "w0f"), ("w1", l_ex[:, 1], "w0b"),
                                                   ("a0", nb[:, 0], "a0f"), ("a1", nb[:, 1], "a0b"))):
                eng.wait_ge(pre_pe, pp + PRE_PE[name])
                for c in range(3):
                    ins = eng.activation(pieces(out)[c], three(3 * (n % 2))[c], ACT.Sigmoid, bias=hp[:, HP[bias]:HP[bias] + 1])
                sg.done(name, ins)
            eng.wait_ge(chain_v, vc + 2)
            sg.done("ksq", eng.activation(kd[:, 0], kk[:], ACT.Square))
            eng.wait_ge(pre_pe, pp + PRE_PE["kk"])
            for c in range(3):
                ins = eng.activation(pieces(kd[:, 0])[c], three(0)[c], ACT.Sqrt)
            sg.done("kroot", ins)
            eng.wait_ge(chain_v, vc + V_CEN)
            sg.done("e_cen", eng.activation(e_cen[:], cen[:], ACT.Exp))

            def exps(i):
                cols = ds(i * CH, CH)
                for d in range(2):
                    for n, (src, scale, bias) in enumerate(((l_in, 1.0, ncen), (l_in, -1.0, cen), (l_ex, 1.0, ncen))):
                        ins = eng.activation(ex_w[:, n, d], src[:, d, cols], ACT.Exp, bias=bias[:, d, ds(i, 1)], scale=scale)
                ins.then_inc(ex_ready, 1)

            exps(0)

            def chunk(i, more):
                it = t * NCH + i
                pe = it * len(PE_N)
                cols = ds(i * CH, CH)
                sg = Signals(chunk_act, ACT_N)
                sg.done("V", eng.activation(v_w[:], z[:, ds(T_V + t, 1), cols].rearrange("p a c -> p (a c)"), ACT.Copy))
                eng.wait_ge(prod_ready, it + 1)
                for h in range(2):
                    ins = eng.activation(rh_w[H[h]], kr_w[H[h], :, h, 1], ACT.Copy)
                sg.done("RH", ins)
                for d in range(2):
                    eng.wait_ge(chunk_pe, pe + PE_N[f"TOK{d}"])
                    tok = TOK_BANK[d]
                    own = tok[:, 0:384].rearrange("p (h c) -> p h c", c=192)[:, :, 0:HS]
                    eng.activation(kd_w[:, 2 * d:2 * d + 2, 0], own, ACT.Copy)
                    eng.activation(kt_w[:, d], tok[:, 256:384], ACT.Copy)
                    ins = eng.activation(np_w[:, 2 * d:2 * d + 2, 0:HS], tok[:, 384:512].rearrange("p (h c) -> p h c", h=2), ACT.Copy)
                    if d == 0:
                        ins = eng.activation(tokv_w[:], V_BANK[:, 0:CH], ACT.Copy)
                    sg.done(f"TOK{d}", ins)
                for u in range(4):
                    eng.wait_ge(chunk_pe, pe + PE_N[f"D{u}"])
                    h = u % 2
                    sg.done(f"D{u}", eng.activation(kd_w[:, u, 1], X_BANK[u][:, h * HS:(h + 1) * HS], ACT.Copy))
                for lv in range(1, LEVELS):
                    for u in range(4):
                        eng.wait_ge(chunk_pe, pe + PE_N[f"X{lv}_{u}"])
                        sg.done(f"X{lv}_{u}", eng.activation(x_w[:, u], X_BANK[u][:, 0:CH], ACT.Copy))
                    if more and lv == LV_NEXT - 1:
                        exps(i + 1)
                for u in range(4):
                    eng.wait_ge(chunk_pe, pe + PE_N[f"WU{u}"])
                    sg.done(f"WU{u}", eng.activation(wu_w[:, u].rearrange("p k c -> p (k c)"), T_BANK[u][:, 0:2 * HS], ACT.Copy))
                for d in range(2):
                    eng.wait_ge(fin_sum, 2 * it + d + 1)
                    scale = e_cen[:, d, ds(i, 1)]
                    eng.activation(m_all[:, d, ds(i * HS, HS)], mr_w[:, d, 0:HS], ACT.Copy, scale=scale)
                    sg.done(f"FIN{d}", eng.activation(r_all[:, d, cols], mr_w[:, d, HS:HS + CH], ACT.Copy, scale=scale))
                eng.wait_ge(chunk_pe, pe + PE_N["Y0"])
                sg.done("Y0", eng.activation(y[:, cols], Y_BANK[:, 0:CH], ACT.Copy))

            chunks(eng, chunk)
            gs = Signals(gn_act, GN_ACT)
            eng.wait_ge(mean_off, 3 * t + 3)
            gs.done("sq", eng.activation(m_all[:, 0], y[:], ACT.Square))
            eng.wait_ge(gn_pe, t * len(GN_PE) + GN_PE["var"])
            for c in range(3):
                ins = eng.activation(pieces(m_all[:, 0])[c], three(3)[c], ACT.Sqrt, bias=eps[:, 0:1], scale=1.0 / HS)
            gs.done("root", ins)
            eng.wait_ge(gn_pe, t * len(GN_PE) + GN_PE["gate"])
            for c in range(3):
                ins = eng.activation(pieces(m_all[:, 1])[c], three(3)[c], ACT.Copy)
            gs.done("gate", ins)

    @block.vector
    def _(eng):
        eng.wait_ge(scan_in, 32)
        eng.wait_ge(kr_zero, 1)
        eng.sem_inc(chunk_dve, DV0)
        with eng.Fori(0, CT) as t:
            pa = t * len(PRE_ACT)
            ch = Chain(eng, chain_v, t * V_ALL)
            ktile = z[:, ds(T_K + t, 1)].rearrange("p a c -> p (a c)")
            rtile = z[:, ds(t, 1)].rearrange("p a c -> p (a c)")
            vtile = z[:, ds(T_V + t, 1)].rearrange("p a c -> p (a c)")
            ch(eng.tensor_copy(hp[:], par[:, ds(PCOLS["head"][0] + t * 10, 10)]))
            col = lambda n: hp[:, HP[n]:HP[n] + 1]
            ch(eng.tensor_scalar(kk[:], ktile, col("k_k"), None, ALU.mult))
            eng.wait_ge(pre_act, pa + PRE_ACT["w1"])
            ch(eng.tensor_scalar(l_ex[:], l_ex[:], -DECAY_C, None, ALU.mult))
            eng.tensor_tensor_scan(l_in[:, 0], reset[:], l_ex[:, 0], 0.0, ALU.mult, ALU.add)
            ch(eng.tensor_tensor_scan(l_in[:, 1], reset[:], l_ex[:, 1], 0.0, ALU.mult, ALU.add))
            sums = l_in[:].rearrange("p d (n c) -> p d n c", c=CH)
            eng.tensor_scalar(ncen[:], sums[:, :, :, CH - 1], -0.5, None, ALU.mult)
            ch(eng.tensor_scalar(cen[:], sums[:, :, :, CH - 1], 0.5, None, ALU.mult))
            ch(eng.scalar_tensor_tensor(m_all[:, 1].rearrange("p (n c) -> p n c", c=CH),
                                        cen[:, 1].unsqueeze(2).to_broadcast([P, NCH, CH]), 2.0, sums[:, 1],
                                        ALU.mult, ALU.subtract))
            ch(eng.tensor_tensor(l_in[:, 1], m_all[:, 1], l_ex[:, 1], ALU.add))
            eng.tensor_copy(l_ex[:, 1], m_all[:, 1])
            ch(eng.tensor_tensor(l_ex[:, 0], l_in[:, 0], l_ex[:, 0], ALU.subtract))
            assert ch.n == V_CEN
            eng.wait_ge(pre_act, pa + PRE_ACT["kroot"])
            ch(eng.tensor_scalar(kd[:, 0], kd[:, 0], 1e-12, None, ALU.max))
            ch(eng.reciprocal(kd[:, 1], kd[:, 0]))
            ch(eng.tensor_tensor(kk[:], kk[:], kd[:, 1], ALU.mult))
            assert ch.n == V_PRE
            eng.wait_ge(pre_act, pa + PRE_ACT["a1"])
            eng.tensor_scalar(ka1[:], col("k_a"), -1.0, 1.0, ALU.mult, ALU.add).then_inc(kd_ready, 1)
            eng.wait_ge(kd_ready, 4 * t + 1)
            eng.tensor_scalar(kd[:], nb[:], col("k_a"), ka1[:, 0:1], ALU.mult, ALU.add).then_inc(kd_ready, 1)
            eng.wait_ge(kd_ready, 4 * t + 2)
            eng.tensor_tensor(kd[:], kd[:], ktile.unsqueeze(1).to_broadcast([P, 2, NTOK]), ALU.mult).then_inc(kd_ready, 1)
            eng.scalar_tensor_tensor(nb[:], nb[:], -1.0, kk[:].unsqueeze(1).to_broadcast([P, 2, NTOK]),
                                     ALU.mult, ALU.mult).then_inc(kd_ready, 1)

            def products(i, part):
                it = t * NCH + i
                cols = ds(i * CH, CH)
                if part == 0:
                    eng.wait_ge(ex_ready, it + 1)
                for h in range(2) if part == 0 else ():
                    eng.tensor_tensor(kr_w[H[h], :, h, 0], ex_w[H[h], 2], kk[H[h], cols].unsqueeze(1).to_broadcast([HS, 2, CH]), ALU.mult)
                    eng.tensor_tensor(kr_w[H[h], :, h, 1], ex_w[H[h], 0], z[H[h], ds(t, 1), cols].to_broadcast([HS, 2, CH]), ALU.mult)
                if part == 1:
                    eng.tensor_tensor(kh_w[:], kd[:, :, cols], ex_w[:, 1], ALU.mult)
                    eng.tensor_tensor(nb_w[:], nb[:, :, cols], ex_w[:, 1], ALU.mult).then_inc(prod_ready, 1)

            eng.wait_ge(pre_act, pa + PRE_ACT["e_cen"])
            eng.wait_ge(kd_ready, 4 * t + 4)
            products(0, 0)
            products(0, 1)

            def chunk(i, more):
                it = t * NCH + i
                pe, act = it * len(PE_N), it * len(ACT_N)
                sg = Signals(chunk_dve, DVE_N)
                cols = ds(i * CH, CH)
                for u in range(4):
                    eng.wait_ge(chunk_pe, pe + PE_N[f"AB{u}"])
                    eng.tensor_tensor(ab_w[:, u].rearrange("p k c -> p (k c)"), T_BANK[u][:, 0:384],
                                      mask[:, u // 2].rearrange("p k c -> p (k c)"), ALU.mult)
                    sg.done(f"AB{u}", eng.tensor_tensor(np_w[:, u, HS:HS + CH], T_BANK[u][:, 384:512], mask[:, u // 2, 1], ALU.mult))
                for u in range(4):
                    eng.wait_ge(chunk_pe, pe + PE_N[f"X0_{u}"])
                    sg.done(f"X0_{u}", eng.tensor_tensor(t_w[:, u, 0], X_BANK[u][:, 0:CH], ident, ALU.add))
                for lv in range(1, LEVELS):
                    for u in range(4):
                        eng.wait_ge(chunk_pe, pe + PE_N[f"T{lv}_{u}"])
                        if lv < LEVELS - 1:
                            tt = t_w[:, u].rearrange("p k c -> p (k c)")
                            sg.done(f"T{lv}_{u}", eng.tensor_tensor(tt, T_BANK[u][:, 0:2 * CH], tt, ALU.add))
                        else:
                            sg.done(f"T{lv}_{u}", eng.tensor_tensor(t_w[:, u, 1], T_BANK[u][:, CH:2 * CH], t_w[:, u, 1], ALU.add))
                    if more and lv == LV_NEXT:
                        eng.wait_ge(chunk_act, act + ACT_N["RH"])
                        products(i + 1, 0)
                    if more and lv == LV_NEXT + 1:
                        products(i + 1, 1)
                for d in range(2):
                    eng.wait_ge(chunk_pe, pe + PE_N[f"FIN{d}"])
                    fin = FIN_BANK[d]
                    eng.tensor_tensor(mr_w[:, d, 0:HS], fin[:, 0:HS], eye, ALU.add)
                    eng.tensor_tensor(mr_w[:, d, HS:HS + CH], fin[:, HS:HS + CH], rh_w[:, d], ALU.add).then_inc(fin_sum, 1)
                    sg.done(f"FIN{d}", eng.tensor_scalar(n_all[:, d, ds(i * HS, HS)], fin[:, HS + CH:2 * HS + CH],
                                                         e_cen[:, d, ds(i, 1)], None, ALU.mult))

            chunks(eng, chunk)
            eng.wait_ge(chunk_act, (t + 1) * NCH * len(ACT_N))
            eng.wait_ge(chunk_dve, DV0 + (t + 1) * NCH * len(DVE_N))
            for d in range(2):
                eng.memset(zst[:, d, 0], 0.0).then_inc(state_dve, 1)
            for s in range(NCH):
                for d, order in enumerate((FWD, BWD)):
                    c = order[s]
                    eng.wait_ge(state_pe, t * 2 * NCH + 2 * s + d + 1)
                    eng.scalar_tensor_tensor(zst[:, d, (s + 1) % 2], banks[4 + d][:, 0:HS], e_cen[:, d, c:c + 1],
                                             n_all[:, d, c * HS:(c + 1) * HS], ALU.mult, ALU.add).then_inc(state_dve, 1)
                if s == 0:
                    eng.wait_ge(state_out, 32 * t + 32)
                    for d in range(2):
                        eng.tensor_copy(zst[:, d, 1], z0s[:, d, ds(t, 1)].rearrange("p a v -> p (a v)")).then_inc(state_dve, 1)
                for k, (lo, num) in enumerate(SPANS):
                    for d, order in enumerate((FWD, BWD)):
                        if s == max(order.index(c) for c in range(lo, lo + num)):
                            ch(eng.tensor_tensor(y[:, lo * CH:(lo + num) * CH], y[:, lo * CH:(lo + num) * CH],
                                                 banks[2 * d + k % 2][:, 0:num * CH], ALU.add))
            gp = t * len(GN_PE)
            ga = t * len(GN_ACT)
            eng.wait_ge(gn_pe, gp + GN_PE["mean"])
            for c in range(3):
                eng.scalar_tensor_tensor(pieces(y[:])[c], three(4)[c], -1.0 / HS, pieces(y[:])[c], ALU.mult, ALU.add).then_inc(mean_off, 1)
            ch(eng.tensor_tensor(r_all[:, 0], kd[:, 0], kd[:, 1], ALU.add))
            ch(eng.tensor_tensor(r_all[:, 0], r_all[:, 0], rtile, ALU.mult))
            ch(eng.tensor_scalar(r_all[:, 1], r_all[:, 0], col("r_k"), None, ALU.mult))
            eng.wait_ge(gn_act, ga + GN_ACT["root"])
            ch(eng.reciprocal(n_all[:, 0], m_all[:, 0]))
            ch(eng.tensor_tensor(y[:], y[:], n_all[:, 0], ALU.mult))
            ch(eng.tensor_scalar(y[:], y[:], col("ln_w"), col("ln_b"), ALU.mult, ALU.add))
            eng.wait_ge(gn_pe, gp + GN_PE["bonus"])
            for c in range(3):
                eng.tensor_tensor(pieces(n_all[:, 1])[c], three(0)[c], pieces(vtile)[c], ALU.mult).then_inc(bonus_v, 1)
            eng.wait_ge(bonus_v, 3 * t + 3)
            ch(eng.tensor_tensor(y[:], y[:], n_all[:, 1], ALU.add))
            eng.wait_ge(gn_act, ga + GN_ACT["gate"])
            ch(eng.tensor_tensor(rtile, y[:], m_all[:, 1], ALU.mult))
            assert ch.n == V_ALL, ch.n
            eng.sem_inc(pre_free, 1)

    @block.tensor
    def _(eng):
        eng.wait_ge(lora_act, 2)

        def mm(out, a, b, start=True, stop=True):
            return eng.matmul(out, a, b, start=start, stop=stop, skip_group_check=True)

        with eng.Fori(0, CT) as t:
            sg = Signals(pre_pe, PRE_PE)
            pa = t * len(PRE_ACT)
            vc = t * V_ALL
            eng.wait_ge(up_in, 48 * t + 48)
            for n, (name, w, src, d) in enumerate((("w0", up_w, T_W, 0), ("w1", up_w, T_W, 1),
                                                   ("a0", up_a, T_A, 0), ("a1", up_a, T_A, 1))):
                if n >= 2:
                    eng.wait_ge(pre_act, pa + PRE_ACT[("w0", "w1")[n - 2]])
                for c in range(3):
                    ins = eng.matmul(three(3 * (n % 2))[c], w[H[d]], pieces(z[H[d], src])[c], start=True, stop=True)
                sg.done(name, ins)
            eng.wait_ge(pre_act, pa + PRE_ACT["ksq"])
            for c in range(3):
                ins = eng.matmul(three(0)[c], blk, pieces(kd[:, 0])[c], start=True, stop=True)
            sg.done("kk", ins)

            def chunk(i, more):
                it = t * NCH + i
                dv, ac, po = DV0 + it * len(DVE_N), it * len(ACT_N), it * len(POOL_N)
                sg = Signals(chunk_pe, PE_N)
                eng.wait_ge(pre_act, pa + PRE_ACT["kroot"])
                eng.wait_ge(prod_ready, it + 1)
                for u in range(4):
                    rhs = kr_w[:, u // 2, u % 2].rearrange("p k c -> p (k c)")
                    mm(T_BANK[u][:, 0:256], kh_w[:, u // 2], rhs)
                    ins = mm(T_BANK[u][:, 256:512], nb_w[:, u // 2], rhs)
                    sg.done(f"AB{u}", ins)
                eng.wait_ge(chunk_dve, dv)
                eng.wait_ge(chunk_act, ac + ACT_N["V"])
                for d in range(2):
                    for n, src in enumerate((kr_w[:, d, 0, 0], kr_w[:, d, 1, 0], kh_w[:, d], nb_w[:, d])):
                        ins = eng.transpose(TOK_BANK[d][:, n * P:(n + 1) * P], src, ident)
                    if d == 0:
                        ins = eng.transpose(V_BANK[:, 0:CH], v_w[:], ident)
                    sg.done(f"TOK{d}", ins)
                for u in range(4):
                    eng.wait_ge(chunk_dve, dv + DVE_N[f"AB{u}"])
                    eng.wait_ge(chunk_act, ac + ACT_N["TOK1" if u > 1 else "TOK0"])
                    sg.done(f"D{u}", mm(X_BANK[u][:, 0:CH], ab_w[:, u, 0], tokv_w[:]))
                for u in range(4):
                    eng.wait_ge(chunk_pool, po + POOL_N[f"L0_{u}"])
                    eng.wait_ge(chunk_act, ac + ACT_N[f"D{u}"])
                    sg.done(f"X0_{u}", mm(X_BANK[u][:, 0:CH], lm_w[:, u, 0], ident))
                for lv in range(1, LEVELS):
                    for u in range(4):
                        eng.wait_ge(chunk_pool, po + POOL_N[f"L{lv}_{u}" if lv > 1 else f"TT{u}"])
                        eng.wait_ge(chunk_dve, dv + DVE_N[f"T{lv - 1}_{u}" if lv > 1 else f"X0_{u}"])
                        sg.done(f"X{lv}_{u}", mm(X_BANK[u][:, 0:CH], lm_w[:, u, lv % 2], t_w[:, u, 0]))
                    for u in range(4):
                        eng.wait_ge(chunk_act, ac + ACT_N[f"X{lv}_{u}"])
                        if lv < LEVELS - 1:
                            mm(T_BANK[u][:, 0:CH], t_w[:, u, 1], x_w[:, u])
                        sg.done(f"T{lv}_{u}", mm(T_BANK[u][:, CH:2 * CH], x_w[:, u], t_w[:, u, 1]))
                for u in range(4):
                    eng.wait_ge(chunk_dve, dv + DVE_N[f"T{LEVELS - 1}_{u}"])
                    sg.done(f"WU{u}", mm(T_BANK[u][:, 0:2 * HS], t_w[:, u, 1], kd_w[:, u].rearrange("p k c -> p (k c)")))
                for d in range(2):
                    for h in range(2):
                        u = 2 * d + h
                        hc = slice(h * HS, (h + 1) * HS)
                        eng.wait_ge(chunk_act, ac + ACT_N[f"WU{u}"])
                        mm(FIN_BANK[d][H[h], 0:HS + CH], wu_w[:, u, 0], np_w[:, u])
                        out = FIN_BANK[d][H[h], HS + CH:2 * HS + CH]
                        mm(out, kt_w[:, d, hc], tokv_w[:, hc], stop=False)
                        ins = mm(out, np_w[:, u, 0:HS], wu_w[:, u, 1], start=False)
                    sg.done(f"FIN{d}", ins)
                for h in range(2):
                    for d in range(2):
                        u = 2 * d + h
                        mm(Y_BANK[H[h], 0:CH], tokv_w[:, h * HS:(h + 1) * HS], ab_w[:, u, 1], start=d == 0, stop=False)
                        ins = mm(Y_BANK[H[h], 0:CH], wu_w[:, u, 1], np_w[:, u, HS:HS + CH], start=False, stop=d == 1)
                sg.done("Y0", ins)

            chunks(eng, chunk)
            eng.wait_ge(chunk_dve, DV0 + (t + 1) * NCH * len(DVE_N))
            eng.wait_ge(chunk_act, (t + 1) * NCH * len(ACT_N))

            def carried():
                eng.sem_inc(pe_began, 1)

            s0 = t * S_ALL
            for s in range(NCH):
                for d, order in enumerate((FWD, BWD)):
                    c = order[s]
                    eng.wait_ge(state_dve, s0 + (1 + d if s == 0 else 2 * s + 3 + d))
                    carried()
                    k = [k for k, (lo, num) in enumerate(SPANS) if lo <= c < lo + num][0]
                    lo = SPANS[k][0]
                    if s == 1 and d == 0:
                        eng.wait_ge(chain_v, vc + V_PRE + 2)
                        carried()
                    for h in H:
                        mm(banks[2 * d + k % 2][h, (c - lo) * CH:(c - lo + 1) * CH], zst[h, d, s % 2], r_all[h, d, c * CH:(c + 1) * CH])
                    for h in H:
                        ins = mm(banks[4 + d][h, 0:HS], m_all[h, d, c * HS:(c + 1) * HS], zst[h, d, s % 2])
                    ins.then_inc(state_pe, 1)
            gs = Signals(gn_pe, GN_PE)
            eng.wait_ge(chain_v, vc + V_PRE + NSPAN)
            eng.wait_ge(state_dve, s0 + S_ALL)
            for c in range(3):
                ins = eng.matmul(three(4)[c], blk, pieces(y[:])[c], start=True, stop=True)
            gs.done("mean", ins)
            eng.wait_ge(gn_act, t * len(GN_ACT) + GN_ACT["sq"])
            for c in range(3):
                ins = eng.matmul(three(3)[c], blk, pieces(m_all[:, 0])[c], start=True, stop=True)
            gs.done("var", ins)
            eng.wait_ge(chain_v, vc + V_PRE + NSPAN + 3)
            for c in range(3):
                ins = eng.matmul(three(0)[c], blk, pieces(r_all[:, 1])[c], start=True, stop=True)
            gs.done("bonus", ins)
            eng.wait_ge(gn_act, t * len(GN_ACT) + GN_ACT["root"])
            for c in range(3):
                ins = eng.matmul(three(3)[c], up_g[:], pieces(z[:, T_G])[c], start=True, stop=True)
            gs.done("gate", ins)


def output_phase(nc, st, io, keep):
    sb = lambda n, s, dt=F32: st.enter_context(nc.sbuf_tensor(n, s, dt))
    ps = lambda n, s: st.enter_context(nc.psum_tensor(n, s, F32))
    sem = lambda n: st.enter_context(nc.semaphore(n))
    cst, z, probs = (keep[n] for n in ("cst", "z", "probs"))
    x1 = keep["wide"][:].rearrange("p (t c) -> p t c", t=NT)
    ident = cst[:, 0:P]
    wo = sb("wo", [P, KT, D])
    wr = sb("wr", [P, KT, NE])
    gt1 = sb("gt1", [P, 2, D])
    gn2 = sb("gn2", [P, 2, D])
    sh2 = sb("sh2", [P, 2, D])
    nrm2 = sb("nrm2", [P, D])
    yT = sb("yT", [P, KT, P])
    tmp = sb("tmp", [P, D])
    h2 = sb("h2_sb", [P, D])
    h2T = sb("h2T", [P, KT, P])
    st8 = sb("st8", [P, 8])
    ex = sb("ex", [P, NE])
    prT = sb("prT", [NE + 1, NTOK])
    sm = sb("sm", [P, 8])

    ps_m = ps("ps_m", [P, 2, 512])
    ps_h = ps("ps_h", [P, 2, 512])
    ps_r = ps("ps_r", [P, 512])
    ps_pt = ps("ps_pt", [P, 512])

    y_in = sem("y_in")
    wo_in = sem("wo_in")
    res_in = sem("res_in")
    norm_in = sem("norm_in")
    y_static = sem("y_static")
    m_half = sem("m_half")
    m_done = sem("m_done")
    norm_chain = sem("norm_chain")
    soft_chain = sem("soft_chain")
    x1_sq = sem("x1_sq")
    h2_out = sem("h2_out")
    h2_turned = sem("h2_turned")
    h2T_done = sem("h2T_done")
    logits = sem("logits")
    exps = sem("exps")
    pr_turned = sem("pr_turned")
    prT_done = sem("prT_done")
    prT_out = sem("prT_out")
    row_chain = sem("row_chain")
    pr_kept = sem("pr_kept")
    V_TAKEN, V_X1, V_MS, V_H2, V_NORM = 1, 2, 3, 6, 6
    V_MAX, V_SOFT = 1, 3
    HK = KT // 2
    block = st.enter_context(nc.Block())

    def tile_of(buf, t):
        return buf[:, t] if isinstance(t, int) else buf[:, ds(t, 1)].rearrange("p a d -> p (a d)")

    def columns(t):
        return slice(t * P, (t + 1) * P) if isinstance(t, int) else ds(t * P, P)

    @block.sync
    def _(eng):
        rows = io["modrow"].rearrange("(e s) c -> s e c", s=2)

        def bcast(dst, section, got):
            for s in range(2):
                src = rows[s, section * KT:(section + 1) * KT].unsqueeze(0).to_broadcast([P, KT, P])
                eng.dma_start(dst[:, s].rearrange("p (e c) -> p e c", c=P), src).then_inc(got, 16)

        eng.dma_start(z[:, CT:KT], io["ypool"]).then_inc(y_in, 16)
        w_out = io["w_out"].rearrange("(k p) n -> p k n", p=P)
        for half in range(2):
            eng.dma_start(wo[:, half * HK:(half + 1) * HK], w_out[:, half * HK:(half + 1) * HK]).then_inc(wo_in, 16)
        bcast(gt1, 2, res_in)
        eng.dma_start(x1[:], io["x_all"].rearrange("(t p) d -> p t d", p=P)).then_inc(res_in, 16)
        bcast(gn2, 4, norm_in)
        eng.dma_start(nrm2[:], io["norm2"].unsqueeze(0).to_broadcast([P, D])).then_inc(norm_in, 16)
        bcast(sh2, 3, norm_in)
        eng.dma_start(wr[:], io["w_router"].rearrange("(k p) n -> p k n", p=P)).then_inc(norm_in, 16)

        def store(t):
            eng.wait_ge(norm_chain, t * V_NORM + V_H2)
            dst = io["h2"][t * P:(t + 1) * P] if isinstance(t, int) else io["h2"][ds(t * P, P)]
            eng.dma_start(dst, h2[:]).then_inc(h2_out, 16)

        store(0)
        with eng.Fori(1, NT) as t:
            store(t)
        eng.wait_ge(prT_done, NT + 1)
        eng.dma_start(io["probsT"], prT[:]).then_inc(prT_out, 16)
        eng.wait_ge(prT_out, 16)
        eng.wait_ge(h2_out, 16 * NT)

    @block.gpsimd
    def _(eng):
        eng.memset(prT[:], 0.0).then_inc(prT_done, 1)

    @block.tensor
    def _(eng):
        def main(t):
            if not isinstance(t, int) or t > 0:
                eng.wait_ge(norm_chain, (t - 1) * V_NORM + V_TAKEN)
            for half in range(2):
                eng.wait_ge(y_static, 2 * t + half + 1)
                for k in range(half * HK, (half + 1) * HK):
                    for n in range(2):
                        ins = eng.matmul(ps_m[:, n], yT[:, k], wo[:, k, n * 512:(n + 1) * 512], start=(k == 0), stop=(k == KT - 1))
                ins.then_inc(m_half if half == 0 else m_done, 1)

        def turn(t):
            eng.wait_ge(norm_chain, t * V_NORM + V_H2)
            for k in range(KT):
                ins = eng.transpose(ps_h[:, k // 4, (k % 4) * P:(k % 4 + 1) * P], h2[:, k * P:(k + 1) * P], ident)
            ins.then_inc(h2_turned, 1)

        def route(t):
            eng.wait_ge(h2T_done, t + 1)
            for k in range(KT):
                ins = eng.matmul(ps_r[:, 0:NE], h2T[:, k], wr[:, k], start=(k == 0), stop=(k == KT - 1))
            ins.then_inc(logits, 1)

        def turn_probs(t):
            eng.wait_ge(soft_chain, t * V_SOFT + V_SOFT)
            eng.transpose(ps_pt[0:NE, 0:P], ex[:], ident).then_inc(pr_turned, 1)

        eng.wait_ge(wo_in, 32)
        main(0)
        main(1)
        turn(0)
        eng.wait_ge(norm_in, 96)
        route(0)
        with eng.Fori(2, NT) as t:
            main(t)
            turn(t - 1)
            turn_probs(t - 2)
            route(t - 1)
        turn(NT - 1)
        turn_probs(NT - 2)
        route(NT - 1)
        turn_probs(NT - 1)

    @block.scalar
    def _(eng):
        def take_y(t, half):
            if not isinstance(t, int) or t > 0:
                eng.wait_ge(m_half if half == 0 else m_done, t)
            eng.activation(yT[:, half * HK:(half + 1) * HK], z[:, half * HK:(half + 1) * HK, columns(t)],
                           ACT.Copy).then_inc(y_static, 1)

        def squares(t):
            eng.wait_ge(norm_chain, t * V_NORM + V_X1)
            eng.activation(tmp[:], tile_of(x1, t), ACT.Square, accum_out=st8[:, 0:1]).then_inc(x1_sq, 1)

        def root(t):
            eng.wait_ge(norm_chain, t * V_NORM + V_MS)
            eng.activation(st8[:, 2:3], st8[:, 1:2], ACT.Sqrt).then_inc(x1_sq, 1)

        def take_h2T(t):
            eng.wait_ge(h2_turned, t + 1)
            eng.activation(h2T[:].rearrange("p (a k) c -> p a (k c)", a=2), ps_h[:], ACT.Copy).then_inc(h2T_done, 1)

        def exp(t):
            eng.wait_ge(soft_chain, t * V_SOFT + V_MAX)
            eng.activation(ex[:], ps_r[:, 0:NE], ACT.Exp, bias=sm[:, 0:1], accum_out=sm[:, 1:2]).then_inc(exps, 1)

        def take_probs(t):
            eng.wait_ge(pr_turned, t + 1)
            eng.activation(prT[0:NE, columns(t)], ps_pt[0:NE, 0:P], ACT.Copy).then_inc(prT_done, 1)

        take_y(0, 0)
        eng.wait_ge(y_in, 16)
        take_y(0, 1)
        eng.wait_ge(prT_done, 1)
        for half in range(2):
            take_y(1, half)
        squares(0)
        root(0)
        for half in range(2):
            take_y(2, half)
        take_h2T(0)
        squares(1)
        exp(0)
        root(1)
        with eng.Fori(2, NT - 1) as t:
            for half in range(2):
                take_y(t + 1, half)
            take_h2T(t - 1)
            take_probs(t - 2)
            squares(t)
            exp(t - 1)
            root(t)
        take_h2T(NT - 2)
        take_probs(NT - 3)
        squares(NT - 1)
        exp(NT - 2)
        root(NT - 1)
        take_h2T(NT - 1)
        take_probs(NT - 2)
        exp(NT - 1)
        take_probs(NT - 1)

    @block.vector
    def _(eng):
        def residual(t, s, ch):
            eng.wait_ge(m_done, t + 1)
            ch(eng.tensor_tensor(tmp[:], ps_m[:].rearrange("p a c -> p (a c)"), gt1[:, s], ALU.mult))
            ch(eng.tensor_tensor(tile_of(x1, t), tile_of(x1, t), tmp[:], ALU.add))

        def mean_square(t, ch):
            eng.wait_ge(x1_sq, 2 * t + 1)
            ch(eng.tensor_scalar(st8[:, 1:2], st8[:, 0:1], 1.0 / D, RMS_EPS, ALU.mult, ALU.add))

        def norm(t, s, ch):
            eng.wait_ge(x1_sq, 2 * t + 2)
            ch(eng.reciprocal(st8[:, 3:4], st8[:, 2:3]))
            if not isinstance(t, int) or t > 0:
                eng.wait_ge(h2_out, 16 * t)
                eng.wait_ge(h2_turned, t)
            ch(eng.scalar_tensor_tensor(h2[:], tile_of(x1, t), st8[:, 3:4], gn2[:, s], ALU.mult, ALU.mult))
            ch(eng.tensor_tensor(h2[:], h2[:], sh2[:, s], ALU.add))

        def highest(t, so):
            eng.wait_ge(logits, t + 1)
            so(eng.tensor_reduce(sm[:, 0:1], ps_r[:, 0:NE], AXX, ALU.max, negate=True))

        def softmax(t, so):
            eng.wait_ge(exps, t + 1)
            so(eng.reciprocal(sm[:, 2:3], sm[:, 1:2]))
            pt = probs[:, t, 0:NE] if isinstance(t, int) else probs[:, ds(t, 1), 0:NE].rearrange("p a e -> p (a e)")
            eng.tensor_scalar(pt, ex[:], sm[:, 2:3], None, ALU.mult).then_inc(pr_kept, 1)
            eng.wait_ge(pr_kept, t + 1)
            so(eng.tensor_scalar(ex[:], ex[:], sm[:, 2:3], None, ALU.mult))

        def step(t, s):
            ch = Chain(eng, norm_chain, t * V_NORM)
            so = Chain(eng, soft_chain, (t - 1) * V_SOFT)
            residual(t, s, ch)
            highest(t - 1, so)
            mean_square(t, ch)
            softmax(t - 1, so)
            norm(t, s, ch)

        eng.memset(probs[:], 0.0)
        eng.wait_ge(res_in, 48)
        ch = Chain(eng, norm_chain)
        residual(0, 0, ch)
        mean_square(0, ch)
        eng.wait_ge(norm_in, 96)
        rc = Chain(eng, row_chain)
        for s in range(2):
            rc(eng.scalar_tensor_tensor(gn2[:, s], gn2[:, s], 1.0, nrm2[:], ALU.add, ALU.mult))
        norm(0, 0, ch)
        step(1, 1)
        with eng.Fori(2, NT) as t:
            step(t, 1)
        so = Chain(eng, soft_chain, (NT - 1) * V_SOFT)
        highest(NT - 1, so)
        softmax(NT - 1, so)


NCHUNK = 4
FC = DE // NCHUNK
FT = FC // P


def expert_phase(nc, st, io, keep):
    sb = lambda n, s, dt=F32: st.enter_context(nc.sbuf_tensor(n, s, dt))
    ps = lambda n, s: st.enter_context(nc.psum_tensor(n, s, F32))
    sem = lambda n: st.enter_context(nc.semaphore(n))
    cst, probs = keep["cst"], keep["probs"]
    ident = cst[:, 0:P]
    tie, slot, tokid = (cst[:, CCOLS[n][0]:CCOLS[n][1]] for n in ("tie", "slot", "tokid"))

    w1c = sb("w1c", [P, 2, KT, FC])
    w3c = sb("w3c", [P, 2, KT, FC])
    w2c = sb("w2c", [P, 2, FT, D])
    prow = sb("prow", [P, NTOK])
    pcol = sb("pcol", [P, NT])
    cnts = sb("cnts", [P, NT, 3])
    rank = sb("rank", [P, NT])
    before = sb("before", [P, DEC - P])
    after = sb("after", [P, DEC])
    same = sb("same", [P, P])
    hot = sb("hot", [P, NT, P])
    pick = sb("pick", [P, NT, 2])
    gate_s = sb("gate_s", [P, 2, 1])
    gate_p = sb("gate_p", [CAP_P, 2, 1])
    idx_s = sb("idx_s", [P, 2, 1], U32)
    idx_p = sb("idx_p", [CAP_P, 2, 1], U32)
    xs = sb("xs", [P, D])
    xp = sb("xp", [CAP_P, D])
    xT = sb("xT", [P, KT, SLOTS])
    sig = sb("sig", [P, 2, SLOTS])
    u = sb("u", [P, 2, SLOTS])
    he = sb("he", [P, 2, FT, SLOTS])
    yT = sb("yeT", [P, KT, SLOTS])
    ys = sb("ys", [P, D])
    yp = sb("ye_p", [CAP_P, D])

    ps_y = ps("ps_ye", [P, 3, 512])
    ps_h = [ps(f"ps_h{i}", [P, 512]) for i in range(2)]
    ps_t = ps("ps_te", [P, 2, 512])
    ps_i = ps("ps_i", [P, 512])

    w13_in = [sem(f"w13_in{b}") for b in range(2)]
    w2_in = [sem(f"w2_in{b}") for b in range(2)]
    down_done = sem("down_done")
    prow_in = sem("prow_in")
    route_v = sem("route_v")
    route_pe = sem("route_pe")
    ids_done = sem("ids_done")
    gathered = sem("gathered")
    x_turned = sem("x_turned_e")
    xT_done = sem("xT_done")
    up_ps = sem("up_ps")
    sig_done = sem("sig_done")
    u_done = sem("u_done")
    he_done = sem("he_done")
    yT_done = sem("yT_done")
    y_turned = sem("y_turned")
    y_scaled = sem("y_scaled")
    scattered = sem("scattered")

    kept = sem("kept")
    acc_free = sem("acc_free")
    last_in = sem("last_in")
    rank_done = sem("rank_done")
    pool_began = sem("pool_began")
    V_RANK = 3
    w1v = io["w1"].rearrange("e (k p) f -> e p k f", p=P)
    w3v = io["w3"].rearrange("e (k p) f -> e p k f", p=P)
    w2v = io["w2"].rearrange("e (t p) d -> e p t d", p=P)
    yps = lambda k: ps_y[:, k // 3, (k % 3) * SLOTS:(k % 3 + 1) * SLOTS]

    block = st.enter_context(nc.Block())

    @block.sync
    def _(eng):
        def load(e, c, first):
            b = c % 2
            sl = lambda v: v[ds(e, 1)].rearrange("o p k f -> (o p) k f")
            if not first:
                eng.wait_ge(up_ps, (e * NCHUNK + c - 1) * FT)
            eng.dma_start(w1c[:, b], sl(w1v)[:, :, c * FC:(c + 1) * FC]).then_inc(w13_in[b], 16)
            eng.dma_start(w3c[:, b], sl(w3v)[:, :, c * FC:(c + 1) * FC]).then_inc(w13_in[b], 16)
            if not first:
                eng.wait_ge(down_done, e * NCHUNK + c - 1)
            eng.dma_start(w2c[:, b], sl(w2v)[:, c * FT:(c + 1) * FT]).then_inc(w2_in[b], 16)

        for c in range(NCHUNK):
            load(0, c, c < 2)
        rows = io["modrow"].rearrange("(e s) c -> s e c", s=2)
        for s in range(2):
            eng.dma_start(keep["gt2"][:, s].rearrange("p (e c) -> p e c", c=P),
                          rows[s, 5 * KT:6 * KT].unsqueeze(0).to_broadcast([P, KT, P])).then_inc(last_in, 16)
        eng.dma_start(keep["nf"][:], io["norm_f"].unsqueeze(0).to_broadcast([P, D])).then_inc(last_in, 16)
        with eng.Fori(1, NE) as e:
            for c in range(NCHUNK):
                load(e, c, False)
        eng.wait_ge(last_in, 48)

    @block.scalar
    def _(eng):
        def row(e):
            src = io["probsT"][e:e + 1] if isinstance(e, int) else io["probsT"][ds(e, 1)]
            eng.dma_start(prow[:], src.to_broadcast([P, NTOK])).then_inc(prow_in, 16)

        row(0)
        with eng.Fori(0, NE) as e:
            eng.wait_ge(rank_done, e * NT + NT)
            row(e + 1)
            eng.wait_ge(x_turned, e + 1)
            eng.activation(xT[:, :, 0:CAP_S].rearrange("p (a k) c -> p a k c", a=2),
                           ps_t[:].rearrange("p a (k c) -> p a k c", c=P), ACT.Copy)
            eng.activation(xT[:, :, CAP_S:SLOTS], ps_i[:, 0:KT * CAP_P].rearrange("p (k c) -> p k c", c=CAP_P),
                           ACT.Copy).then_inc(xT_done, 1)
            for f in range(NCHUNK * FT):
                n = e * (NCHUNK * FT) + f + 1
                eng.wait_ge(up_ps, n)
                eng.activation(sig[:, f % 2], ps_h[f % 2][:, 0:SLOTS], ACT.Sigmoid).then_inc(sig_done, 1)
            eng.wait_ge(down_done, (e + 1) * NCHUNK)
            for j in range(3):
                k0, k1 = 3 * j, min(3 * j + 3, KT)
                ins = eng.activation(yT[:, k0:k1], ps_y[:, j, 0:(k1 - k0) * SLOTS].rearrange("p (k c) -> p k c", c=SLOTS), ACT.Copy)
            ins.then_inc(yT_done, 1)
            for part, (dst, g, n) in enumerate(((ys, gate_s, P), (yp, gate_p, CAP_P))):
                eng.wait_ge(y_turned, 2 * e + part + 1)
                if part == 0:
                    eng.wait_ge(kept, e + 1)
                eng.activation(dst[:].rearrange("p (a c) -> p a c", a=2), ps_t[0:n], ACT.Copy,
                               scale=g[:, 0]).then_inc(y_scaled, 1)

    @block.gpsimd
    def _(eng):
        eng.sem_inc(acc_free, 1)

        def gather(e):
            eng.wait_ge(ids_done, e + 1)
            if not isinstance(e, int):
                eng.wait_ge(x_turned, e)
                eng.sem_inc(pool_began, 1)
            eng.indirect_dma_start(xs[:], None, io["h2"], bass.IndirectOffsetOnAxis(ap=idx_s[:, 0], axis=0)).then_inc(gathered, 16)
            eng.indirect_dma_start(xp[:], None, io["h2"], bass.IndirectOffsetOnAxis(ap=idx_p[:, 0], axis=0)).then_inc(gathered, 16)

        gather(0)
        with eng.Fori(0, NE) as e:
            gather(e + 1)
            eng.wait_ge(y_scaled, 2 * e + 2)
            eng.sem_inc(pool_began, 1)
            eng.indirect_dma_start(io["acc"], bass.IndirectOffsetOnAxis(ap=idx_s[:, 1], axis=0), ys[:], None,
                                   compute_op=ALU.add).then_inc(scattered, 16)
            eng.indirect_dma_start(io["acc"], bass.IndirectOffsetOnAxis(ap=idx_p[:, 1], axis=0), yp[:], None,
                                   compute_op=ALU.add).then_inc(scattered, 16)
            eng.wait_ge(scattered, 32 * e + 32)
            eng.sem_inc(acc_free, 1)
        eng.wait_ge(gathered, 32 * NE + 32)

    @block.vector
    def _(eng):
        def route_begin(e):
            eng.wait_ge(prow_in, 16 * e + 16)
            column = probs[:, :, e] if isinstance(e, int) else probs[:, :, ds(e, 1)].rearrange("p t o -> p (t o)")
            eng.tensor_copy(pcol[:], column)
            eng.tensor_copy(pick[:, :, 1], column)
            eng.memset(cnts[:], 0.0).then_inc(route_v, 1)
            eng.wait_ge(route_v, e * V_RANK + 1)

        def route_rank(e, t):
            if isinstance(e, int) and t == 0:
                pass
            else:
                eng.wait_ge(rank_done, e * NT + t)
            lo, hi = (0, SEQ) if t == 0 else (SEQ, NTOK)
            me = t * P
            p = pcol[:, t:t + 1]
            if me > lo:
                eng.tensor_scalar(before[:, 0:me - lo], prow[:, lo:me], p, None, ALU.is_ge, ALU.add, accum_out=cnts[:, t, 0:1])
            eng.tensor_scalar(after[:, 0:hi - me], prow[:, me:hi], p, None, ALU.is_gt, ALU.add, accum_out=cnts[:, t, 1:2])
            ins = eng.scalar_tensor_tensor(same[:], prow[:, me:me + P], p, tie, ALU.is_equal, ALU.mult,
                                           accum_out=cnts[:, t, 2:3])
            ins.then_inc(rank_done, 1)

        def route_end(e):
            eng.wait_ge(rank_done, e * NT + NT)
            eng.tensor_reduce(rank[:], cnts[:], AXX, ALU.add).then_inc(route_v, 1)
            eng.wait_ge(route_v, e * V_RANK + 2)
            for t in range(NT):
                ins = eng.tensor_scalar(hot[:, t], slot, rank[:, t:t + 1], None, ALU.is_equal)
            ins.then_inc(route_v, 1)

        def ids(e):
            eng.wait_ge(route_pe, e + 1)
            eng.tensor_copy(gate_s[:, 1], ps_i[:, 257:258])
            eng.tensor_copy(gate_p[:, 1], ps_i[0:CAP_P, 259:260])
            eng.tensor_copy(idx_s[:, 0], ps_i[:, 256:257])
            eng.tensor_copy(idx_p[:, 0], ps_i[0:CAP_P, 258:259]).then_inc(ids_done, 1)

        eng.tensor_copy(pick[:, :, 0], tokid)
        eng.sem_inc(he_done, 2)
        route_begin(0)
        for t in range(NT):
            route_rank(0, t)
        route_end(0)
        ids(0)
        with eng.Fori(0, NE) as e:
            for f in range(NCHUNK * FT):
                if f == 0:
                    route_begin(e + 1)
                n = e * (NCHUNK * FT) + f + 1
                b = (f // FT) % 2
                eng.wait_ge(sig_done, n)
                eng.tensor_tensor(u[:, f % 2], ps_h[f % 2][:, 0:SLOTS], sig[:, f % 2], ALU.mult).then_inc(u_done, 1)
                eng.wait_ge(u_done, n)
                eng.tensor_tensor(he[:, b, f % FT], ps_h[f % 2][:, SLOTS:2 * SLOTS], u[:, f % 2], ALU.mult).then_inc(he_done, 1)
                if f < NT:
                    route_rank(e + 1, f)
                if f == NT:
                    route_end(e + 1)
            eng.wait_ge(acc_free, e + 1)
            eng.wait_ge(gathered, 32 * e + 32)
            eng.tensor_copy(gate_s[:, 0], gate_s[:, 1])
            eng.tensor_copy(gate_p[:, 0], gate_p[:, 1])
            eng.tensor_copy(idx_s[:, 1], idx_s[:, 0])
            eng.tensor_copy(idx_p[:, 1], idx_p[:, 0]).then_inc(kept, 1)
            eng.wait_ge(kept, e + 1)
            ids(e + 1)

    @block.tensor
    def _(eng):
        def pick_ids(e):
            eng.wait_ge(route_v, e * V_RANK + V_RANK)
            for t in range(1, NT):
                eng.matmul(ps_i[:, 256:258], hot[:, t], pick[:, t], start=(t == 1), stop=(t == NT - 1))
            eng.matmul(ps_i[0:CAP_P, 258:260], hot[:, 0, 0:CAP_P], pick[:, 0], start=True, stop=True).then_inc(route_pe, 1)

        pick_ids(0)
        with eng.Fori(0, NE) as e:
            eng.wait_ge(gathered, 32 * e + 32)
            eng.wait_ge(ids_done, e + 1)
            for k in range(KT):
                eng.transpose(ps_t[:, k // 4, (k % 4) * P:(k % 4 + 1) * P], xs[:, k * P:(k + 1) * P], ident)
            for k in range(KT):
                ins = eng.transpose(ps_i[:, k * CAP_P:(k + 1) * CAP_P], xp[:, k * P:(k + 1) * P], ident[0:CAP_P, 0:CAP_P])
            ins.then_inc(x_turned, 1)
            eng.wait_ge(xT_done, e + 1)

            def up(c):
                b = c % 2
                eng.wait_ge(w13_in[b], 64 * e + 32 * (c // 2) + 32)
                for f in range(FT):
                    g = c * FT + f
                    eng.wait_ge(he_done, e * (NCHUNK * FT) + g + 1)
                    for w, off in ((w1c, 0), (w3c, SLOTS)):
                        for k in range(KT):
                            ins = eng.matmul(ps_h[g % 2][:, off:off + SLOTS], w[:, b, k, f * P:(f + 1) * P], xT[:, k],
                                             start=(k == 0), stop=(k == KT - 1))
                    ins.then_inc(up_ps, 1)

            def down(c):
                b = c % 2
                eng.wait_ge(w2_in[b], 32 * e + 16 * (c // 2) + 16)
                eng.wait_ge(he_done, 2 + e * (NCHUNK * FT) + (c + 1) * FT)
                for f in range(FT):
                    for k in range(KT):
                        ins = eng.matmul(yps(k), w2c[:, b, f, k * P:(k + 1) * P], he[:, b, f],
                                         start=(c == 0 and f == 0 and k % 3 == 0), stop=(c == NCHUNK - 1 and f == FT - 1),
                                         skip_group_check=True)
                ins.then_inc(down_done, 1)

            up(0)
            for c in range(1, NCHUNK):
                up(c)
                if c == NCHUNK - 1:
                    pick_ids(e + 1)
                down(c - 1)
            down(NCHUNK - 1)
            eng.wait_ge(yT_done, e + 1)
            for k in range(KT):
                ins = eng.transpose(ps_t[:, k // 4, (k % 4) * P:(k % 4 + 1) * P], yT[:, k, 0:CAP_S], ident)
            ins.then_inc(y_turned, 1)
            eng.wait_ge(y_scaled, 2 * e + 1)
            for k in range(KT):
                ins = eng.transpose(ps_t[0:CAP_P, k // 4, (k % 4) * P:(k % 4 + 1) * P], yT[:, k, CAP_S:SLOTS], ident)
            ins.then_inc(y_turned, 1)
            eng.wait_ge(y_scaled, 2 * e + 2)


def final_phase(nc, st, io, keep):
    sb = lambda n, s, dt=F32: st.enter_context(nc.sbuf_tensor(n, s, dt))
    sem = lambda n: st.enter_context(nc.semaphore(n))
    x1 = keep["wide"][:].rearrange("p (t c) -> p t c", t=NT)
    gt2, nf = keep["gt2"], keep["nf"]
    acc = sb("acc_sb", [P, NT, D])
    tmp = sb("ftmp", [P, D])
    out = sb("fout", [P, 2, D])
    s4 = sb("fs4", [P, NT, 4])
    acc_in = [sem(f"acc_in{t}") for t in range(NT)]
    gated = sem("gated")
    summed = sem("summed")
    fin_chain = sem("fin_chain")
    fin_act = sem("fin_act")
    stored = [sem(f"stored{b}") for b in range(2)]
    V_MS, V_OUT, V_ALL = 1, 3, 3
    block = st.enter_context(nc.Block())

    @block.sync
    def _(eng):
        for t in range(NT):
            eng.dma_start(acc[:, t], io["acc"][t * P:(t + 1) * P]).then_inc(acc_in[t], 16)
        for t in range(NT):
            eng.wait_ge(fin_chain, t * V_ALL + V_OUT)
            eng.dma_start(io["y_out"][t * P:(t + 1) * P], out[:, t % 2]).then_inc(stored[t % 2], 16)
        for b in range(2):
            eng.wait_ge(stored[b], 16 * ((NT + 1 - b) // 2))

    @block.gpsimd
    def _(eng):
        for t in range(1, NT, 2):
            eng.wait_ge(acc_in[t], 16)
            eng.tensor_tensor(acc[:, t], acc[:, t], gt2[:, 1], ALU.mult).then_inc(gated, 1)

    @block.vector
    def _(eng):
        def residual(t):
            if t % 2:
                eng.wait_ge(gated, t // 2 + 1)
            else:
                eng.wait_ge(acc_in[t], 16)
                eng.tensor_tensor(acc[:, t], acc[:, t], gt2[:, min(t, 1)], ALU.mult).then_inc(summed, 1)
                eng.wait_ge(summed, t + t // 2 + 1)
            eng.tensor_tensor(acc[:, t], acc[:, t], x1[:, t], ALU.add).then_inc(summed, 1)

        def norm(t):
            ch = Chain(eng, fin_chain, t * V_ALL)
            eng.wait_ge(fin_act, 2 * t + 1)
            ch(eng.tensor_scalar(s4[:, t, 1:2], s4[:, t, 0:1], 1.0 / D, RMS_EPS, ALU.mult, ALU.add))
            eng.wait_ge(fin_act, 2 * t + 2)
            ch(eng.reciprocal(s4[:, t, 3:4], s4[:, t, 2:3]))
            if t >= 2:
                eng.wait_ge(stored[t % 2], 16 * (t // 2))
            ch(eng.scalar_tensor_tensor(out[:, t % 2], acc[:, t], s4[:, t, 3:4], nf[:], ALU.mult, ALU.mult))

        residual(0)
        for t in range(1, NT):
            residual(t)
            norm(t - 1)
        norm(NT - 1)

    @block.scalar
    def _(eng):
        for t in range(NT):
            eng.wait_ge(summed, (t + 1) + (t // 2 + 1))
            eng.activation(tmp[:], acc[:, t], ACT.Square, accum_out=s4[:, t, 0:1]).then_inc(fin_act, 1)
            eng.wait_ge(fin_chain, t * V_ALL + V_MS)
            eng.activation(s4[:, t, 2:3], s4[:, t, 1:2], ACT.Sqrt).then_inc(fin_act, 1)


PHASES = 5


def build(nc, io):
    dram = lambda n, s: nc.dram_tensor(n, s, F32).ap()
    io["modrow"] = dram("modrow", [96, P])
    io["ypool"] = dram("ypool", [P, len(WINDOWS), NTOK])
    io["h2"] = dram("h2", [NTOK, D])
    io["probsT"] = dram("probsT", [NE + 1, NTOK])
    io["acc"] = dram("acc", [NTOK, D])
    with ExitStack() as st:
        sb = lambda s, n, shape: s.enter_context(nc.sbuf_tensor(n, shape, F32))
        keep = {"cst": sb(st, "cst", [P, NCONST]), "probs": sb(st, "probs", [P, NT, NE + 1])}
        assert KT * NTOK == NT * D and 4 * 2 * NTOK == NT * D and 2 * len(WINDOWS) * NTOK == NT * D
        keep["wide"] = sb(st, "wide", [P, NT * D])
        with ExitStack() as front:
            keep["par"] = sb(front, "par", [P, NPARAM])
            keep["mod"] = sb(front, "mod", [P, 48, 2])
            keep["z"] = sb(front, "z", [P, NZ, NTOK])
            with ExitStack() as early:
                keep["zpool"] = sb(early, "zpool", [P, 4, NTOK])
                with ExitStack() as s:
                    project_phase(nc, s, io, keep)
                if PHASES > 1:
                    with ExitStack() as s:
                        pool_phase(nc, s, io, keep)
            if PHASES > 1:
                with ExitStack() as s:
                    scan_phase(nc, s, io, keep)
            if PHASES > 2:
                with ExitStack() as s:
                    output_phase(nc, s, io, keep)
        if PHASES > 3:
            keep["gt2"] = sb(st, "gt2", [P, 2, D])
            keep["nf"] = sb(st, "nf", [P, D])
            with ExitStack() as s:
                expert_phase(nc, s, io, keep)
            with ExitStack() as s:
                final_phase(nc, s, io, keep)


def constants():
    c = np.zeros((P, NCONST), np.float32)

    def put(name, a):
        c[:, CCOLS[name][0]:CCOLS[name][1]] = a.reshape(P, -1)

    i = np.arange(P)
    put("ident", np.eye(P, dtype=np.float32))
    put("blk", (i[:, None] // HS == i[None] // HS).astype(np.float32))
    j = i[:, None]
    t = i[None]
    put("eye", (j % HS == t[:, :HS]).astype(np.float32))
    lvl = np.zeros((P, 2, LEVELS, CH), np.float32)
    mask = np.zeros((P, 2, 3, CH), np.float32)
    for d, (strict, incl) in enumerate(((j < t, j <= t), (j > t, j >= t))):
        for lv in range(LEVELS):
            s = 1 << lv
            lvl[:, d, lv] = strict & (j // (2 * s) == t // (2 * s)) & (j // s != t // s)
        for k in range(3):
            mask[:, d, k] = incl if k % 2 else strict
    put("lvl", lvl)
    put("mask", mask)
    put("tie", (i[None] < i[:, None]).astype(np.float32))
    put("slot", np.broadcast_to(i[None].astype(np.float32), (P, P)))
    put("tokid", (i[:, None] + P * np.arange(NT)[None]).astype(np.float32))
    reset = (np.arange(NTOK) % CH != 0).astype(np.float32)
    inv = np.zeros((len(WINDOWS), NTOK), np.float32)

    def count(n, win):
        pos = np.arange(n)
        return (np.clip(pos + win - win // 2, 0, n) - np.clip(pos - win // 2, 0, n)).astype(np.float64)

    for g, win in enumerate(WINDOWS):
        inv[g, :SEQ] = 1.0 / count(SEQ, win)
        inv[g, SEQ:] = (1.0 / (count(ROWS, win)[:, None] * count(GRID_W, win)[None])).reshape(-1)
    return c, reset, inv


def kernel(**inputs):
    import concourse.bacc as bacc
    from concourse.bass_utils import run_bass_kernel_spmd

    a = {n: np.asarray(v) for n, v in inputs.items()}
    cols = lambda v: np.ascontiguousarray(v.reshape(-1, P).T)
    par = np.zeros((P, NPARAM), np.float32)
    par[:, 0:16:2] = cols(a["c_ctx"])
    par[:, 1:16:2] = cols(a["c"][0])
    for name, v in (("norm1", a["norm1"][0]), ("ada_b", a["ada_b"][0]), ("mu", a["mu_shift"][0]), ("pool_scale", a["pool_scale"][0])):
        par[:, PCOLS[name][0]:PCOLS[name][1]] = cols(v)
    for name, v in (("w0f", a["w0"][0, 0]), ("w0b", a["w0"][0, 1]), ("a0f", a["a0"][0, 0]), ("a0b", a["a0"][0, 1]),
                    ("k_k", a["k_k"][0]), ("k_a", a["k_a"][0]), ("r_k", a["r_k"][0]), ("ln_w", a["ln_x_w"][0]), ("ln_b", a["ln_x_b"][0])):
        lo = PCOLS["head"][0] + HP[name]
        par[:, lo:lo + 40:10] = cols(v)
    consts, reset, inv = constants()
    state0 = np.ascontiguousarray(a["state_rwkv"][0, 0].transpose(0, 1, 3, 2)).reshape(2, CT, P, HS)
    arrays = {
        "consts": consts, "params": par, "reset": reset, "inv_cnt": inv, "state0": state0,
        "x_all": np.concatenate([a["x_prompt"][0], a["x_sample"][0]]),
        "ada_w": a["ada_w"][0], "w_in": a["w_in"][0], "pool_w": a["pool_w"][0],
        "w_up": a["w_up"][0].reshape(P, DR), "a_up": a["a_up"][0].reshape(P, DR), "g_up": a["g_up"][0],
        "w_out": a["w_out"][0], "norm2": a["norm2"][0], "norm_f": a["norm_f"], "w_router": a["w_router"][0],
        "w1": a["w1"][0], "w3": a["w3"][0], "w2": a["w2"][0],
    }
    arrays = {n: np.ascontiguousarray(v) for n, v in arrays.items()}
    nc = bacc.Bacc("TRN2", target_bir_lowering=False, num_devices=1)
    io = {n: nc.dram_tensor(f"in_{n}", v.shape, F32, kind="ExternalInput").ap() for n, v in arrays.items()}
    io["y_out"] = nc.dram_tensor("out_y", [NTOK, D], F32, kind="ExternalOutput").ap()
    io["state_out"] = nc.dram_tensor("out_state", [2, CT, P, HS], F32, kind="ExternalOutput").ap()
    build(nc, io)
    r = run_bass_kernel_spmd(nc, [{f"in_{n}": v for n, v in arrays.items()}], core_ids=[0]).results[0]
    y = r["out_y"]
    state = r["out_state"].reshape(2, 2 * CT, HS, HS).transpose(0, 1, 3, 2)
    return y[None, :SEQ], y[None, SEQ:], np.ascontiguousarray(state)[None, None]
```

```python
from contextlib import ExitStack

import numpy as np

import concourse.bass as bass
from concourse import mybir

ALU = mybir.AluOpType
ACT = mybir.ActivationFunctionType
AXX = mybir.AxisListType.X
F32 = mybir.dt.float32
U32 = mybir.dt.uint32
ds = bass.ds

P = 128
D = 1024
KT = D // P
SEQ, DEC = 128, 1024
NTOK = SEQ + DEC
NT = NTOK // P
GRID_W = 64
ROWS = DEC // GRID_W
DR = 512
HS = 64
CT = DR // P
NPROJ = 19
NZ = 15
T_R, T_K, T_V, T_G, T_W, T_A, T_POOL = 0, 4, 8, 12, 13, 14, 15
CH = 128
NCH = NTOK // CH
LEVELS = 7
WINDOWS = (2, 4, 8, 16)
NE = 16
DE = 2 * D
CAP_S = 2 * DEC // NE
CAP_P = 2 * SEQ // NE
SLOTS = CAP_S + CAP_P
RMS_EPS = 1e-6
GN_EPS = 64e-5
DECAY_C = float(np.exp(-0.5))
PIECE = NTOK // 3

PCOLS = {}
_n = 0
for _name, _k in (("c", 16), ("norm1", 8), ("mu", NZ), ("pool_scale", 4), ("head", 4 * 10)):
    PCOLS[_name] = (_n, _n + _k)
    _n += _k
NPARAM = _n
HP = {n: i for i, n in enumerate(("w0f", "w0b", "a0f", "a0b", "k_k", "k_a", "r_k", "ln_w", "ln_b", "zero"))}

CCOLS = {}
_n = 0
for _name, _k in (("ident", P), ("blk", P), ("eye", HS), ("lvl", 2 * LEVELS * CH), ("mask", 2 * 3 * CH),
                  ("tie", P), ("slot", P), ("tokid", NT)):
    CCOLS[_name] = (_n, _n + _k)
    _n += _k
NCONST = _n


class Steps:

    def __init__(self, names):
        self.names = names
        self.n = {x: i + 1 for i, x in enumerate(names)}
        assert len(self.n) == len(names)

    def __len__(self):
        return len(self.names)

    def __getitem__(self, name):
        return self.n[name]


class Signals:

    def __init__(self, sem, steps):
        self.sem, self.steps, self.at = sem, steps, 0

    def done(self, name, ins):
        assert self.steps.names[self.at] == name, (self.steps.names[self.at], name)
        self.at += 1
        ins.then_inc(self.sem, 1)


class Chain:

    def __init__(self, eng, sem, base=0):
        self.eng, self.sem, self.base, self.n = eng, sem, base, 0

    def __call__(self, ins):
        ins.then_inc(self.sem, 1)
        self.n += 1
        self.eng.wait_ge(self.sem, self.base + self.n)


def project_phase(nc, st, io, keep):
    sb = lambda n, s, dt=F32: st.enter_context(nc.sbuf_tensor(n, s, dt))
    sem = lambda n: st.enter_context(nc.semaphore(n))
    cst, par, z, zpool = (keep[n] for n in ("cst", "par", "z", "zpool"))
    ident = cst[:, 0:P]
    ones = cst[0:1, CCOLS["blk"][0]:CCOLS["blk"][0] + 2]

    hT = keep["wide"][:].rearrange("p (k c) -> p k c", k=KT)
    HK = KT // 2
    ada = sb("ada", [P, 2, HK, 512])
    ada_b = sb("ada_bias", [1, 512])
    mod_row = sb("mod_row", [2, 512])
    mod_sum = sb("mod_sum", [P, 2, 512])
    pick_row = sb("pick_row", [P, 2, 2])
    mod = sb("mod", [P, 2 * KT, 2])
    xt = z[:].rearrange("p m c -> p (m c)")[:, 0:NT * D].rearrange("p (t c) -> p t c", t=NT)
    XG = NT // 3
    sq = keep["wide"][:].rearrange("p (t c) -> p t c", t=NT)
    win = sb("win", [P, 2, KT, P])
    pad = sb("pad", [P, 2, NTOK + 3])
    nsum = sb("nsum", [P, NTOK + 1])
    silu_c = sb("silu_c", [P, KT, 2])
    sig_c = sb("sig_c", [P, 16])
    ss = sb("ss", [P, 4, NT])
    g1 = sb("g1", [P, KT, 2])
    mus = sb("mus", [P, 2, NZ])
    NG, HW, MAXW = len(WINDOWS), GRID_W // 2, max(WINDOWS)
    pw = sb("pw", [P, NG, P])
    cnt = sb("cnt", [P, NTOK])
    seq = sb("seq", [P, 2, SEQ + MAXW])
    col = sb("col", [P, 2, ROWS, GRID_W + MAXW])
    row = sb("row", [P, 2, ROWS + MAXW, HW])
    zero = sb("zero", [P, D // 4])

    banks = [st.enter_context(nc.psum_tensor(f"front_bank{i}", [P, 512], F32)) for i in range(8)]
    ps_p = (banks[0:3], banks[3:6])
    ps_t = (banks[0:2], banks[2:4], banks[4:6])
    ps_row, ps_mod = banks[6], banks[7]

    const_in = sem("const_in")
    par_in = sem("par_in")
    silu_done = sem("silu_done")
    ada_in = [sem(f"ada_in{b}") for b in range(2)]
    ada_used = sem("ada_used")
    row_sb = sem("row_sb")
    pick_set = sem("pick_set")
    mod_chain = sem("mod_chain")
    row_ps = sem("row_ps")
    row_out = sem("row_out")
    mod_turned = sem("mod_turned")
    x_in = [sem(f"x_in{g}") for g in range(3)]
    x_scaled = sem("x_scaled")
    x_turned = sem("x_turned")
    x_stored = sem("x_stored")
    sq_done = sem("sq_done")
    rms_v = sem("rms_v")
    rms_s = sem("rms_s")
    h_done_v = sem("h_done_v")
    h_done_s = sem("h_done_s")
    g1_done = sem("g1_done")
    win_in = [sem(f"win_in{b}") for b in range(2)]
    win_used = sem("win_used")
    p_copied = sem("p_copied")
    pad_used = sem("pad_used")
    pad_zero = sem("pad_zero")
    pool_copied = sem("pool_copied")
    pre_chain = sem("pre_chain")
    shift_chain = sem("shift_chain")
    pw_in = sem("pw_in")
    cnt_in = sem("cnt_in")
    pool_chain = sem("pool_chain")
    diff_done = sem("diff_done")
    y_ready = sem("y_ready")
    y_copied = sem("y_copied")
    y_out = sem("y_out")
    zero_set = sem("zero_set")
    acc_zero = sem("acc_zero")

    NADA = 6 * D // 512
    NEARLY = 2 * D // 512
    NPAIR = NPROJ // 2
    assert NADA - NEARLY == NPAIR - 1 and NG == 4
    ada_v = io["ada_w"].rearrange("(h k p) e -> h p k e", p=P, h=2)
    win_v = io["w_in"].rearrange("(k p) e -> p k e", p=P)
    x_v = io["x_all"].rearrange("(t p) d -> p t d", p=P)

    def source(n):
        return NZ + n if isinstance(n, int) and n < NG else n - NG

    block = st.enter_context(nc.Block())

    @block.sync
    def _(eng):
        def load_ada(j):
            for h in range(2):
                if not isinstance(j, int) or j > 0:
                    eng.wait_ge(ada_used, 2 * j - 1 + h)
                eng.dma_start(ada[:, h], ada_v[h, :, :, ds(j * 512, 512)]).then_inc(ada_in[h], 16)
            if not isinstance(j, int) or j > NEARLY:
                eng.wait_ge(row_ps, j - NEARLY)
            eng.dma_start(ada_b[:], io["ada_b"][ds(j * 512, 512)].unsqueeze(0)).then_inc(ada_in[1], 16)

        def load_win(n):
            b = n % 2
            eng.dma_start(win[:, b], win_v[:, :, source(n) * P:(source(n) + 1) * P]).then_inc(win_in[b], 16)

        def load_x(g):
            eng.dma_start(xt[:, g * XG:(g + 1) * XG], x_v[:, g * XG:(g + 1) * XG]).then_inc(x_in[g], 16)

        eng.dma_start(par[:], io["params"]).then_inc(par_in, 16)
        load_x(0)
        eng.dma_start(cst[:], io["consts"]).then_inc(const_in, 16)
        load_ada(0)
        load_x(1)
        load_x(2)
        for j in range(1, NEARLY):
            load_ada(j)
            if j == 2:
                for n in range(2):
                    load_win(n)
        for n in range(2, 4):
            eng.wait_ge(win_used, n - 1)
            load_win(n)
        load_ada(NEARLY)
        eng.dma_start(pw[:], io["pool_w"].rearrange("g c d -> c g d")).then_inc(pw_in, 16)
        eng.wait_ge(zero_set, 1)
        for t in range(NT):
            eng.dma_start(io["acc"][t * P:(t + 1) * P].rearrange("p (a c) -> p a c", a=4),
                          zero[:].unsqueeze(1).to_broadcast([P, 4, D // 4])).then_inc(acc_zero, 16)
        with eng.Fori(2, NPAIR) as i:
            for b in range(2):
                eng.wait_ge(win_used, 2 * i - 1 + b)
                eng.dma_start(win[:, b], win_v[:, :, ds(i * 256 + (b - NG) * P, P)]).then_inc(win_in[b], 16)
            load_ada(i + NEARLY - 1)
        eng.wait_ge(win_used, NPROJ - 2)
        load_win(NPROJ - 1)
        for g in range(NG):
            eng.wait_ge(y_copied, g + 1)
            eng.dma_start(io["ypool"][:, g], zpool[:, g]).then_inc(y_out, 16)
        eng.wait_ge(y_out, 16 * NG)
        eng.wait_ge(acc_zero, 16 * NT)

    @block.gpsimd
    def _(eng):
        def count(g):
            eng.dma_start(cnt[:], io["inv_cnt"][g].unsqueeze(0).to_broadcast([P, NTOK])).then_inc(cnt_in, 16)

        eng.memset(zero[:], 0.0).then_inc(zero_set, 1)
        for s in range(2):
            for r in range(2):
                eng.memset(pick_row[:, s, r:r + 1], float(r == s)).then_inc(pick_set, 1)
        eng.memset(pad[:], 0.0).then_inc(pad_zero, 1)
        count(0)
        ch = Chain(eng, pool_chain)
        for g, w in enumerate(WINDOWS):
            hi = w - 1 - w // 2
            zg = zpool[:, g]

            def doubled(buf, length):
                step, cur = 1, 0
                while step < w:
                    ch(eng.tensor_tensor(buf(1 - cur, step, length), buf(cur, step, length), buf(cur, 0, length - step), ALU.add))
                    ch(eng.tensor_copy(buf(1 - cur, 0, step), buf(cur, 0, step)))
                    step, cur = 2 * step, 1 - cur
                return cur

            ch(eng.memset(seq[:, 0, SEQ:SEQ + w], 0.0))
            ch(eng.memset(col[:, 0, :, GRID_W:GRID_W + w], 0.0))
            eng.wait_ge(pool_copied, g + 1)
            eng.wait_ge(pad_used, g + 1)
            eng.wait_ge(cnt_in, 16 * (g + 1))
            ch(eng.tensor_copy(seq[:, 0, 0:SEQ], zg[:, 0:SEQ]))
            ch(eng.tensor_copy(col[:, 0, :, 0:GRID_W], zg[:, SEQ:NTOK].rearrange("p (r c) -> p r c", c=GRID_W)))
            n = doubled(lambda i, a, b: seq[:, i, a:b], SEQ + w)
            ch(eng.tensor_tensor(seq[:, n, hi:hi + SEQ], seq[:, n, hi:hi + SEQ], cnt[:, 0:SEQ], ALU.mult))
            ch(eng.tensor_tensor(zg[:, 0:SEQ], seq[:, n, hi:hi + SEQ], zg[:, 0:SEQ], ALU.subtract))
            m = doubled(lambda i, a, b: col[:, i, :, a:b], GRID_W + w)
            for half in range(2):
                c0 = half * HW
                ch(eng.memset(row[:, 0, ROWS:ROWS + w], 0.0))
                ch(eng.tensor_copy(row[:, 0, 0:ROWS], col[:, m, :, hi + c0:hi + c0 + HW]))
                n = doubled(lambda i, a, b: row[:, i, a:b], ROWS + w)
                part = lambda ap: ap[:, SEQ:NTOK].rearrange("p (r c) -> p r c", c=GRID_W)[:, :, c0:c0 + HW]
                ch(eng.tensor_tensor(row[:, n, hi:hi + ROWS], row[:, n, hi:hi + ROWS], part(cnt), ALU.mult))
                ch(eng.tensor_tensor(part(zg), row[:, n, hi:hi + ROWS], part(zg), ALU.subtract))
            eng.sem_inc(diff_done, 1)
            if g + 1 < NG:
                count(g + 1)

    @block.scalar
    def _(eng):
        def take_row(j, late=False):
            if late:
                eng.wait_ge(row_ps, j - NEARLY + 1)
            else:
                eng.wait_ge(ada_used, 2 * j + 2)
            eng.activation(mod_row[:], ps_row[0:2], ACT.Copy).then_inc(row_sb, 1)

        def squares(g):
            eng.wait_ge(x_in[g], 16)
            for t in range(g * XG, (g + 1) * XG):
                ins = eng.activation(sq[:, t], xt[:, t], ACT.Square, accum_out=ss[:, 0, t:t + 1])
            ins.then_inc(sq_done, 1)

        def root(g):
            ts = slice(g * XG, (g + 1) * XG)
            eng.wait_ge(rms_v, 3 * g + 1)
            eng.activation(ss[:, 2, ts], ss[:, 1, ts], ACT.Sqrt).then_inc(rms_s, 1)

        def take_x(g):
            for t in range(g * XG, (g + 1) * XG):
                eng.wait_ge(x_turned, t + 1)
                for a in range(2):
                    ins = eng.activation(hT[:, a * HK:(a + 1) * HK, t * P:(t + 1) * P],
                                         ps_t[t % 3][a][:].rearrange("p (k c) -> p k c", c=P), ACT.Copy)
                ins.then_inc(x_stored, 1)

        eng.wait_ge(par_in, 16)
        eng.activation(sig_c[:], par[:, 0:16], ACT.Sigmoid).then_inc(silu_done, 1)
        squares(0)
        root(0)
        squares(1)
        root(1)
        squares(2)
        root(2)
        eng.wait_ge(sq_done, 3)
        take_x(0)
        take_row(0)
        take_x(1)
        take_x(2)
        for j in range(1, NEARLY):
            eng.wait_ge(mod_turned, j)
            take_row(j)
        eng.wait_ge(g1_done, 1)
        for k in range(1, KT, 2):
            for s, (lo, hi) in enumerate(((0, SEQ), (SEQ, NTOK))):
                eng.activation(hT[:, k, lo:hi], hT[:, k, lo:hi], ACT.Identity, bias=mod[:, k, s:s + 1],
                               scale=g1[:, k, s:s + 1]).then_inc(h_done_s, 1)

        def project(n, b, first):
            eng.wait_ge(win_used, n + 1)
            if not first:
                eng.wait_ge(pad_used, n - 1)
            eng.activation(pad[:, b, 1:1 + SEQ], ps_p[b][0][:, 0:SEQ], ACT.Copy).then_inc(p_copied, 1)
            eng.activation(pad[:, b, 2 + SEQ:2 + PIECE], ps_p[b][0][:, SEQ:PIECE], ACT.Copy).then_inc(p_copied, 1)
            for c in range(1, 3):
                eng.activation(pad[:, b, 2 + c * PIECE:2 + (c + 1) * PIECE], ps_p[b][c][:, 0:PIECE], ACT.Copy).then_inc(p_copied, 1)

        def pair(i):
            for b in range(2):
                project(2 * i + b, b, False)
            if not isinstance(i, int) or i > 1:
                eng.wait_ge(row_out, 16 * i - 16)
            else:
                eng.wait_ge(mod_turned, NEARLY)
            take_row(i + NEARLY - 1, late=True)
            eng.wait_ge(row_sb, i + NEARLY)
            eng.dma_start(io["modrow"][:, ds((i - 1) * 512, 512)], mod_row[:]).then_inc(row_out, 16)

        eng.wait_ge(pad_zero, 1)
        project(0, 0, True)
        project(1, 1, True)
        pair(1)
        with eng.Fori(2, NPAIR) as i:
            pair(i)
        s0 = PCOLS["pool_scale"][0]
        for g in range(NG):
            eng.wait_ge(y_ready, g + 1)
            for c in range(3):
                ins = eng.activation(zpool[:, g, c * PIECE:(c + 1) * PIECE], ps_p[g % 2][c][:, 0:PIECE], ACT.Copy,
                                     scale=par[:, s0 + g:s0 + g + 1])
            ins.then_inc(y_copied, 1)
        eng.wait_ge(pad_used, NPROJ - 1)
        eng.activation(z[:, T_W], z[:, T_W], ACT.Tanh)
        eng.activation(z[:, T_G], z[:, T_G], ACT.Sigmoid)
        project(NPROJ - 1, 0, False)
        eng.wait_ge(row_out, 16 * (NPAIR - 1))

    @block.vector
    def _(eng):
        ch = Chain(eng, pre_chain)
        eng.wait_ge(silu_done, 1)
        ch(eng.tensor_tensor(silu_c[:].rearrange("p k s -> p (k s)"), sig_c[:], par[:, 0:16], ALU.mult))
        m0, m1 = PCOLS["mu"]
        ch(eng.tensor_scalar(mus[:, 0], par[:, m0:m1], -1.0, 1.0, ALU.mult, ALU.add))
        ch(eng.tensor_scalar(mus[:, 1], par[:, m0:m1], 0.5, None, ALU.mult))
        for g in range(3):
            ts = slice(g * XG, (g + 1) * XG)
            eng.wait_ge(sq_done, g + 1)
            eng.tensor_scalar(ss[:, 1, ts], ss[:, 0, ts], 1.0 / D, RMS_EPS, ALU.mult, ALU.add).then_inc(rms_v, 1)
            eng.wait_ge(rms_s, g + 1)
            eng.reciprocal(ss[:, 3, ts], ss[:, 2, ts]).then_inc(rms_v, 1)
            eng.wait_ge(rms_v, 3 * g + 2)
            for t in range(g * XG, (g + 1) * XG):
                ins = eng.tensor_scalar(xt[:, t], xt[:, t], ss[:, 3, t:t + 1], None, ALU.mult)
                ins.then_inc(x_scaled, 1)
            eng.sem_inc(rms_v, 1)
        eng.wait_ge(mod_turned, NEARLY)
        ch(eng.tensor_copy(mod[:], ps_mod[:, 0:4 * KT].rearrange("p (e s) -> p e s", s=2)))
        n0, n1 = PCOLS["norm1"]
        ch(eng.tensor_scalar(g1[:], mod[:, KT:2 * KT], 1.0, None, ALU.add))
        ch(eng.tensor_tensor(g1[:], g1[:], par[:, n0:n1].unsqueeze(2).to_broadcast([P, KT, 2]), ALU.mult))
        eng.sem_inc(g1_done, 1)
        eng.wait_ge(x_stored, NT)
        for k in range(0, KT, 2):
            for s, (lo, hi) in enumerate(((0, SEQ), (SEQ, NTOK))):
                eng.tensor_scalar(hT[:, k, lo:hi], hT[:, k, lo:hi], g1[:, k, s:s + 1], mod[:, k, s:s + 1],
                                  ALU.mult, ALU.add).then_inc(h_done_v, 1)

        def shift(m, b, sh):
            eng.wait_ge(p_copied, 4 * (m + NG) + 4)
            sh(eng.tensor_tensor(nsum[:], pad[:, b, 0:NTOK + 1], pad[:, b, 2:NTOK + 3], ALU.add))
            for lo, hi, g in ((0, SEQ, 0), (SEQ, NTOK, 1)):
                eng.tensor_scalar(z[:, m, lo:hi] if isinstance(m, int) else z[:, ds(m, 1), lo:hi],
                                  pad[:, b, 1 + lo + g:1 + hi + g] if isinstance(m, int) else pad[:, b:b + 1, 1 + lo + g:1 + hi + g],
                                  mus[:, 0, m:m + 1] if isinstance(m, int) else mus[:, 0, ds(m, 1)],
                                  None, ALU.mult).then_inc(shift_chain, 1)
            sh.n += 2
            eng.wait_ge(shift_chain, sh.base + sh.n)
            eng.tensor_scalar(nsum[:], nsum[:], mus[:, 1, m:m + 1] if isinstance(m, int) else mus[:, 1, ds(m, 1)],
                              None, ALU.mult).then_inc(shift_chain, 1)
            sh.n += 1
            eng.wait_ge(shift_chain, sh.base + sh.n)
            for lo, hi, g in ((0, SEQ, 0), (SEQ, NTOK, 1)):
                zz = z[:, m, lo:hi] if isinstance(m, int) else z[:, ds(m, 1), lo:hi].rearrange("p a c -> p (a c)")
                eng.tensor_tensor(zz, zz, nsum[:, lo + g:hi + g], ALU.add).then_inc(shift_chain, 1)
            sh.n += 2
            eng.wait_ge(shift_chain, sh.base + sh.n)
            eng.sem_inc(pad_used, 1)

        def modulate(i):
            mc = Chain(eng, mod_chain, i * 2 * KT)
            if not isinstance(i, int) or i > 0:
                eng.wait_ge(row_ps, i)
            for h in range(2):
                eng.wait_ge(ada_in[h], (i + NEARLY + 1) * 16 * (h + 1))
                for k in range(HK):
                    for s in range(2):
                        c = silu_c[:, h * HK + k, s:s + 1]
                        out = mod_sum[:, s]
                        if h == 0 and k == 0:
                            mc(eng.tensor_scalar(out, ada[:, h, k], c, None, ALU.mult))
                        else:
                            mc(eng.scalar_tensor_tensor(out, ada[:, h, k], c, out, ALU.mult, ALU.add))
                eng.sem_inc(ada_used, 1)

        for n in range(NG):
            if n == 2:
                modulate(0)
            eng.wait_ge(p_copied, 4 * n + 4)
            eng.tensor_copy(zpool[:, n, 0:SEQ], pad[:, n % 2, 1:1 + SEQ]).then_inc(pool_copied, 1)
            eng.tensor_copy(zpool[:, n, SEQ:NTOK], pad[:, n % 2, 2 + SEQ:2 + NTOK]).then_inc(pad_used, 1)
        PER = 6
        with eng.Fori(0, NZ // 2) as i:
            modulate(i + 1)
            for b in range(2):
                shift(2 * i + b, b, Chain(eng, shift_chain, (2 * i + b) * PER))
        shift(NZ - 1, 0, Chain(eng, shift_chain, (NZ - 1) * PER))

    @block.tensor
    def _(eng):
        def modulate(j):
            for h in range(2):
                eng.wait_ge(ada_in[h], 16 * (h + 1) * (j + 1))
                if h == 0 and j > 0:
                    eng.wait_ge(row_sb, j)
                for k in range(HK):
                    ins = eng.matmul(ps_row[0:2], silu_c[:, h * HK + k], ada[:, h, k], start=(h == 0 and k == 0), stop=False)
                if h == 1:
                    ins = eng.matmul(ps_row[0:2], ones, ada_b[:], start=False, stop=True)
                ins.then_inc(ada_used, 1)

        def add_up(i):
            if not isinstance(i, int) or i > 0:
                eng.wait_ge(row_sb, i + NEARLY)
            eng.wait_ge(mod_chain, i * 2 * KT + 2 * KT)
            for s in range(2):
                eng.matmul(ps_row[0:2], pick_row[:, s], mod_sum[:, s], start=(s == 0), stop=False)
            eng.matmul(ps_row[0:2], ones, ada_b[:], start=False, stop=True).then_inc(row_ps, 1)

        def turn_row(j):
            eng.wait_ge(row_sb, j + 1)
            for q in range(4):
                e = 4 * j + q
                ins = eng.transpose(ps_mod[:, 2 * e:2 * e + 2], mod_row[:, q * P:(q + 1) * P], ident[0:2, 0:2])
            ins.then_inc(mod_turned, 1)

        def turn_x(g):
            for t in range(g * XG, (g + 1) * XG):
                eng.wait_ge(x_scaled, t + 1)
                if t >= 3:
                    eng.wait_ge(x_stored, t - 2)
                for k in range(KT):
                    ins = eng.transpose(ps_t[t % 3][k // 4][:, (k % 4) * P:(k % 4 + 1) * P], xt[:, t, k * P:(k + 1) * P], ident)
                ins.then_inc(x_turned, 1)

        eng.wait_ge(const_in, 16)
        turn_x(0)
        eng.wait_ge(pre_chain, 1)
        modulate(0)
        turn_x(1)
        turn_x(2)
        turn_row(0)
        for j in range(1, NEARLY):
            modulate(j)
            turn_row(j)

        def project(n, b):
            eng.wait_ge(win_in[b], 16 * (n // 2 + 1) if isinstance(n, int) else n * 8 - 8 * b + 16)
            if not isinstance(n, int) or n >= 2:
                eng.wait_ge(p_copied, 4 * n - 4)
            for c in range(3):
                for k in range(KT):
                    if c == 0 and isinstance(n, int) and n == 0:
                        eng.wait_ge(h_done_s if k % 2 else h_done_v, 2 * (k // 2) + 2)
                    ins = eng.matmul(ps_p[b][c][:, 0:PIECE], win[:, b, k], hT[:, k, c * PIECE:(c + 1) * PIECE],
                                     start=(k == 0), stop=(k == KT - 1))
            ins.then_inc(win_used, 1)

        def pair(i):
            for b in range(2):
                project(2 * i + b, b)
            add_up(i - 1)

        eng.wait_ge(x_stored, NT)
        for n in range(2):
            project(n, n)
        eng.wait_ge(pick_set, 4)
        pair(1)
        with eng.Fori(2, NPAIR) as i:
            pair(i)
        eng.wait_ge(p_copied, 4 * (NPROJ - 1))
        eng.wait_ge(pw_in, 16)
        for g in range(NG):
            eng.wait_ge(diff_done, g + 1)
            if g >= 2:
                eng.wait_ge(y_copied, g - 1)
            for c in range(3):
                ins = eng.matmul(ps_p[g % 2][c][:, 0:PIECE], pw[:, g], zpool[:, g, c * PIECE:(c + 1) * PIECE],
                                 start=True, stop=True)
            ins.then_inc(y_ready, 1)
        eng.wait_ge(y_copied, NG - 1)
        project(NPROJ - 1, 0)


CHUNK_PE = ([f"AB{u}" for u in range(4)] + ["TOK0", "TOK1"] + [f"D{u}" for u in range(4)] + [f"X0_{u}" for u in range(4)]
            + [f"{k}{lv}_{u}" for lv in range(1, LEVELS) for k in "XT" for u in range(4)]
            + [f"WU{u}" for u in range(4)] + ["FIN0", "FIN1", "Y0"])
CHUNK_DVE = ([f"AB{u}" for u in range(4)] + [f"X0_{u}" for u in range(4)]
             + [f"T{lv}_{u}" for lv in range(1, LEVELS) for u in range(4)] + ["FIN0", "FIN1"])
CHUNK_ACT = (["V", "RH", "TOK0", "TOK1"] + [f"D{u}" for u in range(4)]
             + [f"X{lv}_{u}" for lv in range(1, LEVELS) for u in range(4)]
             + [f"WU{u}" for u in range(4)] + ["FIN0", "FIN1", "Y0"])
CHUNK_POOL = [f"L{lv}_{u}" for lv in range(2) for u in range(4)] + [f"TT{u}" for u in range(4)]
CHUNK_POOL += [f"L{lv}_{u}" for lv in range(2, LEVELS) for u in range(4)]
WO_TILES = (T_V, T_V + 1, T_V + 2, T_W, T_A)
SPANS = ((0, 1), (1, 4), (5, 4))


def scan_phase(nc, st, io, keep):
    sb = lambda n, s, dt=F32: st.enter_context(nc.sbuf_tensor(n, s, dt))
    sem = lambda n: st.enter_context(nc.semaphore(n))
    cst, par, z = keep["cst"], keep["par"], keep["z"]

    def const(name):
        return cst[:, CCOLS[name][0]:CCOLS[name][1]]

    ident, blk, eye = const("ident"), const("blk"), const("eye")
    lvl = const("lvl").rearrange("p (d l c) -> p d l c", d=2, l=LEVELS)
    mask = const("mask").rearrange("p (d k c) -> p d k c", d=2, k=3)

    reset = sb("reset", [P, NTOK])
    hp = sb("hp", [P, 10])
    hn = sb("hn", [P, 10])
    ka1 = sb("ka1", [P, 1])
    up_w = sb("up_w", [P, 2, P])
    up_a = sb("up_a", [P, 2, P])
    up_g = sb("up_g", [P, P])
    l_in, l_ex, kd, nb = (keep["wide"][:, j * 2 * NTOK:(j + 1) * 2 * NTOK].rearrange("p (d c) -> p d c", d=2) for j in range(4))
    cen = sb("cen", [P, 2, NCH])
    ncen = sb("ncen", [P, 2, NCH])
    e_cen = sb("e_cen", [P, 2, NCH])
    total = sb("total", [P, NCH])
    kk = sb("kk", [P, NTOK])
    y = sb("y", [P, NTOK])
    m_all = sb("m_all", [P, 2, NTOK])
    r_all = sb("r_all", [P, 2, NTOK])
    n_all = sb("n_all", [P, 2, NTOK])
    eps = sb("eps", [P, 1])
    ex_w = sb("ex_w", [P, 3, 2, CH])
    kr_w = sb("kr_w", [P, 2, 2, 2, CH])
    kh_w = sb("kh_w", [P, 2, CH])
    nb_w = sb("nb_w", [P, 2, CH])
    v_w = sb("v_w", [P, CH])
    ab_w = sb("ab_w", [P, 4, 3, CH])
    np_w = sb("np_w", [P, 4, HS + CH])
    lm_w = sb("lm_w", [P, 4, 2, CH])
    kt_w = sb("kt_w", [P, 2, CH])
    tokv_w = sb("tokv_w", [P, CH])
    kd_w = sb("kd_w", [P, 4, 2, HS])
    x_w = sb("x_w", [P, 4, CH])
    t_w = sb("t_w", [P, 4, 2, CH])
    wu_w = sb("wu_w", [P, 4, 2, HS])
    rh_w = sb("rh_w", [P, 2, CH])
    mr_w = sb("mr_w", [P, 2, HS + CH])
    key_w = sb("key_w", [P, 2, CH])
    zst = sb("zst", [P, 2, 2, P])
    z_ctx = sb("z_ctx", [P, 2, HS])
    z0s = sb("z0s", [P, 2, CT, HS])

    banks = [st.enter_context(nc.psum_tensor(f"bank{i}", [P, 512], F32)) for i in range(8)]
    T_BANK = [banks[i] for i in (4, 5, 0, 1)]
    X_BANK = [banks[i] for i in (2, 3, 6, 7)]
    TOK_BANK = banks[6:8]
    FIN_BANK = banks[2:4]
    V_BANK, Y_BANK = banks[2], banks[6]

    scan_in = sem("scan_in")
    up_in = sem("up_in")
    upg_in = sem("upg_in")
    wo_early = sem("wo_early")
    norm_par = sem("norm_par")
    norm_pool = sem("norm_pool")
    lora_pe = sem("lora_pe")
    lora_act = sem("lora_act")
    key_chain = sem("key_chain")
    bonus_pool = sem("bonus_pool")
    pre_pe = sem("pre_pe")
    pre_act = sem("pre_act")
    chain_v = sem("chain_v")
    chunk_pe = sem("chunk_pe")
    chunk_dve = sem("chunk_dve")
    chunk_act = sem("chunk_act")
    chunk_pool = sem("chunk_pool")
    state_pe = sem("state_pe")
    state_dve = sem("state_dve")
    gn_pe = sem("gn_pe")
    gn_act = sem("gn_act")
    state_out = sem("state_out")
    eps_set = sem("eps_set")
    pe_began = sem("pe_began")
    pool_began = sem("pool_began_scan")
    mean_off = sem("mean_off")
    bonus_v = sem("bonus_v")
    kr_zero = sem("kr_zero")
    fin_sum = sem("fin_sum")
    ex_ready = sem("ex_ready")
    prod_ready = sem("prod_ready")

    PE_N, DVE_N, ACT_N, POOL_N = (Steps(x) for x in (CHUNK_PE, CHUNK_DVE, CHUNK_ACT, CHUNK_POOL))
    LORA = Steps(["w0", "w1", "a0", "a1"])
    KEY = Steps(["max", "inverse", "kk", "scale", "kd", "nb"])
    PRE_PE = Steps(["kk"])
    PRE_ACT = Steps(["ksq", "kroot", "e_cen"])
    GN_PE = Steps(["mean", "bonus", "var", "gate"])
    GN_ACT = Steps(["sq", "root", "gate"])
    V_PRE = 8
    V_ALL = 15
    DV0 = 1
    LV_NEXT = 3
    NSPAN = 2 * len(SPANS)
    S_ALL = 2 * NCH + 4
    H = (slice(0, HS), slice(HS, P))
    FWD = list(range(NCH))
    BWD = [0] + list(range(NCH - 1, 0, -1))

    def three(bank0):
        return [banks[bank0 + i][:, 0:PIECE] for i in range(3)]

    SET_A, SET_B = three(0), three(3)
    LORA_SET = {"w0": SET_B, "w1": SET_B, "a0": SET_A, "a1": SET_B}

    def pairs_of_heads(eng, body):
        with eng.Fori(0, CT - 1) as t:
            body(t, True)
        body(CT - 1, False)

    def pieces(ap):
        return [ap[:, c * PIECE:(c + 1) * PIECE] for c in range(3)]

    def chunks(eng, body):
        with eng.Fori(0, NCH - 1) as i:
            body(i, True)
        body(NCH - 1, False)

    block = st.enter_context(nc.Block())

    @block.sync
    def _(eng):
        eng.dma_start(reset[:], io["reset"].unsqueeze(0).to_broadcast([P, NTOK])).then_inc(scan_in, 16)
        eng.dma_start(z0s[:], io["state0"].rearrange("d t p v -> p d t v")).then_inc(scan_in, 16)

        def load_up(t):
            for w, src in ((up_w, io["w_up"]), (up_a, io["a_up"])):
                for d in range(2):
                    eng.dma_start(w[H[d], d], src[H[d], ds(t * P, P)]).then_inc(up_in, 16)

        def load_g(t):
            eng.dma_start(up_g[:], io["g_up"][:, ds(t * P, P)]).then_inc(upg_in, 16)

        def body(t, more):
            for d in range(2):
                eng.wait_ge(state_dve, t * S_ALL + 3 + d)
                eng.dma_start(io["state_out"][d, ds(t, 1)].rearrange("o p v -> (o p) v"), z_ctx[:, d]).then_inc(state_out, 16)
            if more:
                eng.wait_ge(gn_pe, t * len(GN_PE) + GN_PE["gate"])
                load_g(t + 1)

        eng.wait_ge(kr_zero, 2)
        load_up(0)
        load_g(0)
        eng.wait_ge(lora_pe, len(LORA))
        load_up(1)

        with eng.Fori(0, CT - 2) as t:
            body(t, True)
            eng.wait_ge(lora_pe, t * len(LORA) + 2 * len(LORA))
            load_up(t + 2)
        body(CT - 2, True)
        eng.wait_ge(chain_v, (CT - 1) * V_ALL)
        eng.wait_ge(lora_act, CT * len(LORA))
        for k, m in enumerate(WO_TILES):
            eng.dma_start(z[:, m, 0:D], io["w_out"][k * P:(k + 1) * P]).then_inc(wo_early, 16)
        body(CT - 1, False)
        eng.wait_ge(wo_early, 16 * len(WO_TILES))
        eng.wait_ge(state_out, 32 * CT)

    @block.gpsimd
    def _(eng):
        def carried():
            eng.sem_inc(pool_began, 1)

        eng.memset(eps[:], GN_EPS).then_inc(eps_set, 1)
        eng.memset(kr_w[:], 0.0)
        eng.memset(zst[:], 0.0).then_inc(kr_zero, 1)
        eng.memset(up_w[:], 0.0)
        eng.memset(up_a[:], 0.0).then_inc(kr_zero, 1)
        with eng.Fori(0, CT) as t:
            with eng.Fori(0, NCH) as i:
                it = t * NCH + i
                dve, pe, own = DV0 + it * len(DVE_N), it * len(PE_N), it * len(POOL_N)
                sg = Signals(chunk_pool, POOL_N)

                def level(lv, u):
                    sg.done(f"L{lv}_{u}", eng.tensor_tensor(lm_w[:, u, lv % 2], ab_w[:, u, 2], lvl[:, u // 2, lv], ALU.mult))

                for lv in range(2):
                    for u in range(4):
                        if lv == 0:
                            eng.wait_ge(chunk_dve, dve + DVE_N[f"AB{u}"])
                        level(lv, u)
                for u in range(4):
                    eng.wait_ge(chunk_pool, own + POOL_N[f"L0_{u}"])
                    sg.done(f"TT{u}", eng.tensor_tensor(t_w[:, u, 1], lm_w[:, u, 0], ident, ALU.add))
                for lv in range(2, LEVELS):
                    for u in range(4):
                        eng.wait_ge(chunk_pe, pe + PE_N[f"X{lv - 2}_{u}"])
                        if lv == 2:
                            eng.wait_ge(chunk_pool, own + POOL_N[f"TT{u}"])
                        level(lv, u)
            ch = Chain(eng, bonus_pool, 3 * t)
            eng.wait_ge(chunk_act, t * NCH * len(ACT_N) + NCH * len(ACT_N))
            eng.wait_ge(chunk_dve, t * NCH * len(DVE_N) + DV0 + NCH * len(DVE_N))
            ch(eng.tensor_tensor(l_in[:, 0], kd[:, 0], kd[:, 1], ALU.add))
            ch(eng.tensor_tensor(l_in[:, 0], l_in[:, 0], z[:, ds(t, 1)].rearrange("p a c -> p (a c)"), ALU.mult))
            carried()
            ch(eng.tensor_scalar(l_in[:, 0], l_in[:, 0], hp[:, HP["r_k"]:HP["r_k"] + 1], None, ALU.mult))
            carried()
            eng.tensor_copy(hn[:], hp[:]).then_inc(norm_par, 1)
            eng.wait_ge(gn_act, t * len(GN_ACT) + GN_ACT["gate"])
            eng.wait_ge(chain_v, t * V_ALL + V_ALL)
            ch = Chain(eng, norm_pool, 4 * t)
            ch(eng.tensor_tensor(y[:], y[:], n_all[:, 0], ALU.mult))
            eng.wait_ge(norm_par, t + 1)
            carried()
            ch(eng.tensor_scalar(y[:], y[:], hn[:, HP["ln_w"]:HP["ln_w"] + 1], hn[:, HP["ln_b"]:HP["ln_b"] + 1], ALU.mult, ALU.add))
            ch(eng.tensor_tensor(y[:], y[:], n_all[:, 1], ALU.add))
            carried()
            ch(eng.tensor_tensor(z[:, ds(t, 1)].rearrange("p a c -> p (a c)"), y[:], m_all[:, 1], ALU.mult))

    @block.scalar
    def _(eng):
        eng.wait_ge(eps_set, 1)
        h0 = PCOLS["head"][0]

        def lora(t, name):
            out, bias = {"w0": (l_ex[:, 0], "w0f"), "w1": (l_ex[:, 1], "w0b"), "a0": (nb[:, 0], "a0f"), "a1": (nb[:, 1], "a0b")}[name]
            eng.wait_ge(lora_pe, t * len(LORA) + LORA[name])
            for c in range(3):
                ins = eng.activation(pieces(out)[c], LORA_SET[name][c], ACT.Sigmoid, bias=par[:, ds(h0 + t * 10 + HP[bias], 1)])
            ins.then_inc(lora_act, 1)

        for name in LORA.names:
            lora(0, name)

        def body(t, following):
            sg = Signals(pre_act, PRE_ACT)
            pp = t * len(PRE_PE)
            vc = t * V_ALL
            eng.wait_ge(chain_v, vc + 2)
            sg.done("ksq", eng.activation(kd[:, 0], kk[:], ACT.Square))
            eng.wait_ge(pre_pe, pp + PRE_PE["kk"])
            for c in range(3):
                ins = eng.activation(pieces(kd[:, 0])[c], three(0)[c], ACT.Sqrt)
            sg.done("kroot", ins)
            eng.wait_ge(chain_v, vc + V_PRE)
            sg.done("e_cen", eng.activation(e_cen[:], cen[:], ACT.Exp))

            def exps(i):
                cols = ds(i * CH, CH)
                for d in range(2):
                    for n, (src, scale, bias) in enumerate(((l_in, -DECAY_C, ncen), (l_in, DECAY_C, cen), (l_ex, -DECAY_C, ncen))):
                        ins = eng.activation(ex_w[:, n, d], src[:, d, cols], ACT.Exp, bias=bias[:, d, ds(i, 1)], scale=scale)
                ins.then_inc(ex_ready, 1)

            exps(0)

            def chunk(i, more):
                it = t * NCH + i
                pe = it * len(PE_N)
                cols = ds(i * CH, CH)
                sg = Signals(chunk_act, ACT_N)
                sg.done("V", eng.activation(v_w[:], z[:, ds(T_V + t, 1), cols].rearrange("p a c -> p (a c)"), ACT.Copy))
                eng.wait_ge(prod_ready, it + 1)
                for h in range(2):
                    ins = eng.activation(rh_w[H[h]], kr_w[H[h], :, h, 1], ACT.Copy)
                sg.done("RH", ins)
                for d in range(2):
                    eng.wait_ge(chunk_pe, pe + PE_N[f"TOK{d}"])
                    tok = TOK_BANK[d]
                    own = tok[:, 0:384].rearrange("p (h c) -> p h c", c=192)[:, :, 0:HS]
                    eng.activation(kd_w[:, 2 * d:2 * d + 2, 0], own, ACT.Copy)
                    eng.activation(kt_w[:, d], tok[:, 256:384], ACT.Copy)
                    ins = eng.activation(np_w[:, 2 * d:2 * d + 2, 0:HS], tok[:, 384:512].rearrange("p (h c) -> p h c", h=2), ACT.Copy)
                    if d == 0:
                        ins = eng.activation(tokv_w[:], V_BANK[:, 0:CH], ACT.Copy)
                    sg.done(f"TOK{d}", ins)
                for u in range(4):
                    eng.wait_ge(chunk_pe, pe + PE_N[f"D{u}"])
                    h = u % 2
                    sg.done(f"D{u}", eng.activation(kd_w[:, u, 1], X_BANK[u][:, h * HS:(h + 1) * HS], ACT.Copy))
                for lv in range(1, LEVELS):
                    for u in range(4):
                        eng.wait_ge(chunk_pe, pe + PE_N[f"X{lv}_{u}"])
                        sg.done(f"X{lv}_{u}", eng.activation(x_w[:, u], X_BANK[u][:, 0:CH], ACT.Copy))
                    if more and lv == LV_NEXT - 1:
                        exps(i + 1)
                for u in range(4):
                    eng.wait_ge(chunk_pe, pe + PE_N[f"WU{u}"])
                    sg.done(f"WU{u}", eng.activation(wu_w[:, u].rearrange("p k c -> p (k c)"), T_BANK[u][:, 0:2 * HS], ACT.Copy))
                for d in range(2):
                    eng.wait_ge(fin_sum, 2 * it + d + 1)
                    scale = e_cen[:, d, ds(i, 1)]
                    eng.activation(m_all[:, d, ds(i * HS, HS)], mr_w[:, d, 0:HS], ACT.Copy, scale=scale)
                    sg.done(f"FIN{d}", eng.activation(r_all[:, d, cols], mr_w[:, d, HS:HS + CH], ACT.Copy, scale=scale))
                eng.wait_ge(chunk_pe, pe + PE_N["Y0"])
                sg.done("Y0", eng.activation(y[:, cols], Y_BANK[:, 0:CH], ACT.Copy))

            chunks(eng, chunk)
            gs = Signals(gn_act, GN_ACT)
            eng.wait_ge(mean_off, 3 * t + 3)
            gs.done("sq", eng.activation(m_all[:, 0], y[:], ACT.Square))
            eng.wait_ge(gn_pe, t * len(GN_PE) + GN_PE["var"])
            for c in range(3):
                ins = eng.activation(pieces(m_all[:, 0])[c], SET_A[c], ACT.Sqrt, bias=eps[:, 0:1], scale=1.0 / HS)
            gs.done("root", ins)
            if following:
                lora(t + 1, "w0")
            eng.wait_ge(gn_pe, t * len(GN_PE) + GN_PE["gate"])
            for c in range(3):
                ins = eng.activation(pieces(m_all[:, 1])[c], SET_A[c], ACT.Copy)
            gs.done("gate", ins)
            if following:
                for name in LORA.names[1:]:
                    lora(t + 1, name)

        pairs_of_heads(eng, body)

    @block.vector
    def _(eng):
        eng.wait_ge(scan_in, 32)
        eng.wait_ge(kr_zero, 2)
        eng.sem_inc(chunk_dve, DV0)

        def body(t, following):
            pa = t * len(PRE_ACT)
            ch = Chain(eng, chain_v, t * V_ALL)
            ktile = z[:, ds(T_K + t, 1)].rearrange("p a c -> p (a c)")
            vtile = z[:, ds(T_V + t, 1)].rearrange("p a c -> p (a c)")
            ch(eng.tensor_copy(hp[:], par[:, ds(PCOLS["head"][0] + t * 10, 10)]))
            col = lambda n: hp[:, HP[n]:HP[n] + 1]
            ch(eng.tensor_scalar(kk[:], ktile, col("k_k"), None, ALU.mult))
            ch(eng.tensor_scalar(ka1[:], col("k_a"), -1.0, 1.0, ALU.mult, ALU.add))
            eng.wait_ge(lora_act, t * len(LORA) + LORA["w1"])
            eng.tensor_tensor_scan(l_in[:, 0], reset[:], l_ex[:, 0], 0.0, ALU.mult, ALU.add)
            ch(eng.tensor_tensor_scan(l_in[:, 1], reset[:], l_ex[:, 1], 0.0, ALU.mult, ALU.add))
            sums = l_in[:].rearrange("p d (n c) -> p d n c", c=CH)
            eng.tensor_copy(total[:], sums[:, 1, :, CH - 1])
            eng.tensor_scalar(ncen[:], sums[:, :, :, CH - 1], 0.5 * DECAY_C, None, ALU.mult)
            ch(eng.tensor_scalar(cen[:], sums[:, :, :, CH - 1], -0.5 * DECAY_C, None, ALU.mult))
            ch(eng.scalar_tensor_tensor(r_all[:, 1].rearrange("p (n c) -> p n c", c=CH),
                                        total[:].unsqueeze(2).to_broadcast([P, NCH, CH]), 1.0, sums[:, 1],
                                        ALU.mult, ALU.subtract))
            ch(eng.tensor_tensor(l_in[:, 1], r_all[:, 1], l_ex[:, 1], ALU.add))
            eng.tensor_copy(l_ex[:, 1], r_all[:, 1])
            ch(eng.tensor_tensor(l_ex[:, 0], l_in[:, 0], l_ex[:, 0], ALU.subtract))
            assert ch.n == V_PRE

            def keys(i, names):
                cols = ds(i * CH, CH)
                kc = Chain(eng, key_chain, (t * NCH + i) * len(KEY) + KEY[names[0]] - 1)
                for name in names:
                    if name == "max":
                        ins = eng.tensor_scalar(key_w[:, 0], kd[:, 0, cols], 1e-12, None, ALU.max)
                    if name == "inverse":
                        ins = eng.reciprocal(key_w[:, 1], key_w[:, 0])
                    if name == "kk":
                        ins = eng.tensor_tensor(kk[:, cols], kk[:, cols], key_w[:, 1], ALU.mult)
                    if name == "scale":
                        ins = eng.tensor_scalar(kd[:, :, cols], nb[:, :, cols], col("k_a"), ka1[:, 0:1], ALU.mult, ALU.add)
                    if name == "kd":
                        ins = eng.tensor_tensor(kd[:, :, cols], kd[:, :, cols], z[:, ds(T_K + t, 1), cols].to_broadcast([P, 2, CH]), ALU.mult)
                    if name == "nb":
                        ins = eng.scalar_tensor_tensor(nb[:, :, cols], nb[:, :, cols], -1.0,
                                                       kk[:, cols].unsqueeze(1).to_broadcast([P, 2, CH]), ALU.mult, ALU.mult)
                    kc(ins)

            def products(i, part):
                it = t * NCH + i
                cols = ds(i * CH, CH)
                if part == 0:
                    eng.wait_ge(ex_ready, it + 1)
                for h in range(2) if part == 0 else ():
                    eng.tensor_tensor(kr_w[H[h], :, h, 0], ex_w[H[h], 2], kk[H[h], cols].unsqueeze(1).to_broadcast([HS, 2, CH]), ALU.mult)
                    eng.tensor_tensor(kr_w[H[h], :, h, 1], ex_w[H[h], 0], z[H[h], ds(t, 1), cols].to_broadcast([HS, 2, CH]), ALU.mult)
                if part == 1:
                    eng.tensor_tensor(kh_w[:], kd[:, :, cols], ex_w[:, 1], ALU.mult)
                    eng.tensor_tensor(nb_w[:], nb[:, :, cols], ex_w[:, 1], ALU.mult).then_inc(prod_ready, 1)

            eng.wait_ge(lora_act, t * len(LORA) + LORA["a1"])
            eng.wait_ge(pre_act, pa + PRE_ACT["kroot"])
            keys(0, KEY.names)
            eng.wait_ge(pre_act, pa + PRE_ACT["e_cen"])
            products(0, 0)
            products(0, 1)

            def chunk(i, more):
                it = t * NCH + i
                pe, act = it * len(PE_N), it * len(ACT_N)
                sg = Signals(chunk_dve, DVE_N)
                cols = ds(i * CH, CH)
                for u in range(4):
                    eng.wait_ge(chunk_pe, pe + PE_N[f"AB{u}"])
                    eng.tensor_tensor(ab_w[:, u].rearrange("p k c -> p (k c)"), T_BANK[u][:, 0:384],
                                      mask[:, u // 2].rearrange("p k c -> p (k c)"), ALU.mult)
                    sg.done(f"AB{u}", eng.tensor_tensor(np_w[:, u, HS:HS + CH], T_BANK[u][:, 384:512], mask[:, u // 2, 1], ALU.mult))
                for u in range(4):
                    eng.wait_ge(chunk_pe, pe + PE_N[f"X0_{u}"])
                    sg.done(f"X0_{u}", eng.tensor_tensor(t_w[:, u, 0], X_BANK[u][:, 0:CH], ident, ALU.add))
                for lv in range(1, LEVELS):
                    for u in range(4):
                        eng.wait_ge(chunk_pe, pe + PE_N[f"T{lv}_{u}"])
                        if lv < LEVELS - 1:
                            tt = t_w[:, u].rearrange("p k c -> p (k c)")
                            sg.done(f"T{lv}_{u}", eng.tensor_tensor(tt, T_BANK[u][:, 0:2 * CH], tt, ALU.add))
                        else:
                            sg.done(f"T{lv}_{u}", eng.tensor_tensor(t_w[:, u, 1], T_BANK[u][:, CH:2 * CH], t_w[:, u, 1], ALU.add))
                    if more and lv < LV_NEXT:
                        keys(i + 1, KEY.names[2 * lv - 2:2 * lv])
                    if more and lv == LV_NEXT:
                        eng.wait_ge(chunk_act, act + ACT_N["RH"])
                        products(i + 1, 0)
                    if more and lv == LV_NEXT + 1:
                        keys(i + 1, KEY.names[4:])
                    if more and lv == LV_NEXT + 2:
                        products(i + 1, 1)
                for d in range(2):
                    eng.wait_ge(chunk_pe, pe + PE_N[f"FIN{d}"])
                    fin = FIN_BANK[d]
                    eng.tensor_tensor(mr_w[:, d, 0:HS], fin[:, 0:HS], eye, ALU.add)
                    eng.tensor_tensor(mr_w[:, d, HS:HS + CH], fin[:, HS:HS + CH], rh_w[:, d], ALU.add).then_inc(fin_sum, 1)
                    sg.done(f"FIN{d}", eng.tensor_scalar(n_all[:, d, ds(i * HS, HS)], fin[:, HS + CH:2 * HS + CH],
                                                         e_cen[:, d, ds(i, 1)], None, ALU.mult))

            chunks(eng, chunk)
            eng.wait_ge(chunk_act, (t + 1) * NCH * len(ACT_N))
            eng.wait_ge(chunk_dve, DV0 + (t + 1) * NCH * len(DVE_N))
            if not isinstance(t, int) or t > 0:
                eng.wait_ge(state_out, 32 * t)
            diag = lambda d, b: [zst[H[h], d, b, h * HS:(h + 1) * HS] for h in range(2)]
            for d in range(2):
                eng.memset(zst[:, d, 0], 0.0).then_inc(state_dve, 1)
            for s in range(NCH):
                for d, order in enumerate((FWD, BWD)):
                    c = order[s]
                    eng.wait_ge(state_pe, t * 2 * NCH + 2 * s + d + 1)
                    outs = diag(d, (s + 1) % 2) if s else [z_ctx[h, d] for h in H]
                    for h, out in enumerate(outs):
                        ins = eng.scalar_tensor_tensor(out, banks[4 + d][H[h], 0:HS], e_cen[H[h], d, c:c + 1],
                                                       n_all[H[h], d, c * HS:(c + 1) * HS], ALU.mult, ALU.add)
                    ins.then_inc(state_dve, 1)
                if s == 0:
                    for d in range(2):
                        for h, out in enumerate(diag(d, 1)):
                            ins = eng.tensor_copy(out, z0s[H[h], d, ds(t, 1)].rearrange("p a v -> p (a v)"))
                        ins.then_inc(state_dve, 1)
                for k, (lo, num) in enumerate(SPANS):
                    for d, order in enumerate((FWD, BWD)):
                        if s == max(order.index(c) for c in range(lo, lo + num)):
                            ch(eng.tensor_tensor(y[:, lo * CH:(lo + num) * CH], y[:, lo * CH:(lo + num) * CH],
                                                 banks[2 * d + k % 2][:, 0:num * CH], ALU.add))
            gp = t * len(GN_PE)
            ga = t * len(GN_ACT)
            eng.wait_ge(gn_pe, gp + GN_PE["mean"])
            for c in range(3):
                eng.scalar_tensor_tensor(pieces(y[:])[c], SET_A[c], -1.0 / HS, pieces(y[:])[c], ALU.mult, ALU.add).then_inc(mean_off, 1)
            eng.wait_ge(gn_pe, gp + GN_PE["bonus"])
            for c in range(3):
                eng.tensor_tensor(pieces(n_all[:, 1])[c], SET_B[c], pieces(vtile)[c], ALU.mult).then_inc(bonus_v, 1)
            eng.wait_ge(bonus_v, 3 * t + 3)
            eng.wait_ge(gn_act, ga + GN_ACT["root"])
            ch(eng.reciprocal(n_all[:, 0], m_all[:, 0]))
            eng.wait_ge(norm_par, t + 1)
            assert ch.n == V_ALL, ch.n

        pairs_of_heads(eng, body)

    @block.tensor
    def _(eng):
        def mm(out, a, b, start=True, stop=True):
            return eng.matmul(out, a, b, start=start, stop=stop, skip_group_check=True)

        def lora(t, name):
            w, src = {"w": (up_w, T_W), "a": (up_a, T_A)}[name[0]]
            if name == "w0":
                eng.wait_ge(up_in, 64 * t + 64)
            if name in ("w1", "a1"):
                eng.wait_ge(lora_act, t * len(LORA) + LORA["w0" if name == "w1" else "w1"])
            for c in range(3):
                ins = eng.matmul(LORA_SET[name][c], w[:, int(name[1])], pieces(z[:, src])[c], start=True, stop=True)
            ins.then_inc(lora_pe, 1)

        for name in LORA.names:
            lora(0, name)

        def body(t, following):
            sg = Signals(pre_pe, PRE_PE)
            pa = t * len(PRE_ACT)
            vc = t * V_ALL
            eng.wait_ge(pre_act, pa + PRE_ACT["ksq"])
            for c in range(3):
                ins = eng.matmul(three(0)[c], blk, pieces(kd[:, 0])[c], start=True, stop=True)
            sg.done("kk", ins)

            def chunk(i, more):
                it = t * NCH + i
                dv, ac, po = DV0 + it * len(DVE_N), it * len(ACT_N), it * len(POOL_N)
                sg = Signals(chunk_pe, PE_N)
                eng.wait_ge(pre_act, pa + PRE_ACT["kroot"])
                eng.wait_ge(prod_ready, it + 1)
                for u in range(4):
                    rhs = kr_w[:, u // 2, u % 2].rearrange("p k c -> p (k c)")
                    mm(T_BANK[u][:, 0:256], kh_w[:, u // 2], rhs)
                    ins = mm(T_BANK[u][:, 256:512], nb_w[:, u // 2], rhs)
                    sg.done(f"AB{u}", ins)
                eng.wait_ge(chunk_dve, dv)
                eng.wait_ge(chunk_act, ac + ACT_N["V"])
                for d in range(2):
                    for n, src in enumerate((kr_w[:, d, 0, 0], kr_w[:, d, 1, 0], kh_w[:, d], nb_w[:, d])):
                        ins = eng.transpose(TOK_BANK[d][:, n * P:(n + 1) * P], src, ident)
                    if d == 0:
                        ins = eng.transpose(V_BANK[:, 0:CH], v_w[:], ident)
                    sg.done(f"TOK{d}", ins)
                for u in range(4):
                    eng.wait_ge(chunk_dve, dv + DVE_N[f"AB{u}"])
                    eng.wait_ge(chunk_act, ac + ACT_N["TOK1" if u > 1 else "TOK0"])
                    sg.done(f"D{u}", mm(X_BANK[u][:, 0:CH], ab_w[:, u, 0], tokv_w[:]))
                for u in range(4):
                    eng.wait_ge(chunk_pool, po + POOL_N[f"L0_{u}"])
                    eng.wait_ge(chunk_act, ac + ACT_N[f"D{u}"])
                    sg.done(f"X0_{u}", mm(X_BANK[u][:, 0:CH], lm_w[:, u, 0], ident))
                for lv in range(1, LEVELS):
                    for u in range(4):
                        eng.wait_ge(chunk_pool, po + POOL_N[f"L{lv}_{u}"])
                        eng.wait_ge(chunk_dve, dv + DVE_N[f"T{lv - 1}_{u}" if lv > 1 else f"X0_{u}"])
                        sg.done(f"X{lv}_{u}", mm(X_BANK[u][:, 0:CH], lm_w[:, u, lv % 2], t_w[:, u, 0]))
                    for u in range(4):
                        if lv == 1:
                            eng.wait_ge(chunk_pool, po + POOL_N[f"TT{u}"])
                        eng.wait_ge(chunk_act, ac + ACT_N[f"X{lv}_{u}"])
                        if lv < LEVELS - 1:
                            mm(T_BANK[u][:, 0:CH], t_w[:, u, 1], x_w[:, u])
                        sg.done(f"T{lv}_{u}", mm(T_BANK[u][:, CH:2 * CH], x_w[:, u], t_w[:, u, 1]))
                for u in range(4):
                    eng.wait_ge(chunk_dve, dv + DVE_N[f"T{LEVELS - 1}_{u}"])
                    sg.done(f"WU{u}", mm(T_BANK[u][:, 0:2 * HS], t_w[:, u, 1], kd_w[:, u].rearrange("p k c -> p (k c)")))
                for d in range(2):
                    for h in range(2):
                        u = 2 * d + h
                        hc = slice(h * HS, (h + 1) * HS)
                        eng.wait_ge(chunk_act, ac + ACT_N[f"WU{u}"])
                        mm(FIN_BANK[d][H[h], 0:HS + CH], wu_w[:, u, 0], np_w[:, u])
                        out = FIN_BANK[d][H[h], HS + CH:2 * HS + CH]
                        mm(out, kt_w[:, d, hc], tokv_w[:, hc], stop=False)
                        ins = mm(out, np_w[:, u, 0:HS], wu_w[:, u, 1], start=False)
                    sg.done(f"FIN{d}", ins)
                for h in range(2):
                    for d in range(2):
                        u = 2 * d + h
                        mm(Y_BANK[H[h], 0:CH], tokv_w[:, h * HS:(h + 1) * HS], ab_w[:, u, 1], start=d == 0, stop=False)
                        ins = mm(Y_BANK[H[h], 0:CH], wu_w[:, u, 1], np_w[:, u, HS:HS + CH], start=False, stop=d == 1)
                sg.done("Y0", ins)

            chunks(eng, chunk)
            eng.wait_ge(chunk_dve, DV0 + (t + 1) * NCH * len(DVE_N))
            eng.wait_ge(chunk_act, (t + 1) * NCH * len(ACT_N))

            def carried():
                eng.sem_inc(pe_began, 1)

            s0 = t * S_ALL
            for s in range(NCH):
                for d, order in enumerate((FWD, BWD)):
                    c = order[s]
                    eng.wait_ge(state_dve, s0 + (1 + d if s == 0 else 2 * s + 3 + d))
                    carried()
                    k = [k for k, (lo, num) in enumerate(SPANS) if lo <= c < lo + num][0]
                    lo = SPANS[k][0]
                    if s == 1 and d == 0:
                        eng.wait_ge(chain_v, vc + V_PRE + 2)
                        carried()
                    mm(banks[2 * d + k % 2][:, (c - lo) * CH:(c - lo + 1) * CH], zst[:, d, s % 2], r_all[:, d, c * CH:(c + 1) * CH])
                    for h in range(2):
                        ins = mm(banks[4 + d][H[h], 0:HS], m_all[H[h], d, c * HS:(c + 1) * HS], zst[H[h], d, s % 2, h * HS:(h + 1) * HS])
                    ins.then_inc(state_pe, 1)
            gs = Signals(gn_pe, GN_PE)
            eng.wait_ge(chain_v, vc + V_PRE + NSPAN)
            eng.wait_ge(state_dve, s0 + S_ALL)
            for c in range(3):
                ins = eng.matmul(SET_A[c], blk, pieces(y[:])[c], start=True, stop=True)
            gs.done("mean", ins)
            eng.wait_ge(bonus_pool, 3 * t + 3)
            for c in range(3):
                ins = eng.matmul(SET_B[c], blk, pieces(l_in[:, 0])[c], start=True, stop=True)
            gs.done("bonus", ins)
            if following:
                eng.wait_ge(bonus_v, 3 * t + 3)
                lora(t + 1, "w0")
            eng.wait_ge(gn_act, t * len(GN_ACT) + GN_ACT["sq"])
            for c in range(3):
                ins = eng.matmul(SET_A[c], blk, pieces(m_all[:, 0])[c], start=True, stop=True)
            gs.done("var", ins)
            eng.wait_ge(gn_act, t * len(GN_ACT) + GN_ACT["root"])
            eng.wait_ge(upg_in, 16 * t + 16)
            for c in range(3):
                ins = eng.matmul(SET_A[c], up_g[:], pieces(z[:, T_G])[c], start=True, stop=True)
            gs.done("gate", ins)
            if following:
                lora(t + 1, "w1")
                eng.wait_ge(gn_act, t * len(GN_ACT) + GN_ACT["gate"])
                lora(t + 1, "a0")
                lora(t + 1, "a1")

        pairs_of_heads(eng, body)


def output_phase(nc, st, io, keep):
    sb = lambda n, s, dt=F32: st.enter_context(nc.sbuf_tensor(n, s, dt))
    ps = lambda n, s: st.enter_context(nc.psum_tensor(n, s, F32))
    sem = lambda n: st.enter_context(nc.semaphore(n))
    cst, z, probs = (keep[n] for n in ("cst", "z", "probs"))
    x1 = keep["wide"][:].rearrange("p (t c) -> p t c", t=NT)
    ident = cst[:, 0:P]
    NLATE = KT - len(WO_TILES)
    wo_late = sb("wo_late", [P, NLATE, D])
    wr = sb("wr", [P, KT, NE])
    gt1 = sb("gt1", [P, 2, D])
    gn2 = sb("gn2", [P, 2, D])
    sh2 = sb("sh2", [P, 2, D])
    nrm2 = sb("nrm2", [P, D])
    yT = sb("yT", [P, KT, P])
    tmp = sb("tmp", [P, D])
    h2 = sb("h2_sb", [P, D])
    h2T = sb("h2T", [P, KT, P])
    st8 = sb("st8", [P, 8])
    ex = sb("ex", [P, NE])
    prT = sb("prT", [NE + 1, NTOK])
    sm = sb("sm", [P, 8])

    ps_m = ps("ps_m", [P, 2, 512])
    ps_h = ps("ps_h", [P, 2, 512])
    ps_r = ps("ps_r", [P, 512])
    ps_pt = ps("ps_pt", [P, 512])

    y_in = sem("y_in")
    wo_in = sem("wo_in")
    res_in = sem("res_in")
    latent_in = sem("latent_in")
    norm_in = sem("norm_in")
    y_static = sem("y_static")
    m_half = sem("m_half")
    m_done = sem("m_done")
    norm_chain = sem("norm_chain")
    soft_chain = sem("soft_chain")
    x1_sq = sem("x1_sq")
    h2_out = sem("h2_out")
    h2_turned = sem("h2_turned")
    h2T_done = sem("h2T_done")
    logits = sem("logits")
    exps = sem("exps")
    pr_turned = sem("pr_turned")
    prT_done = sem("prT_done")
    prT_out = sem("prT_out")
    row_chain = sem("row_chain")
    pr_kept = sem("pr_kept")
    V_TAKEN, V_X1, V_MS, V_H2, V_NORM = 1, 2, 3, 6, 6
    V_MAX, V_SOFT = 1, 3
    HK = KT // 2
    block = st.enter_context(nc.Block())

    def tile_of(buf, t):
        return buf[:, t] if isinstance(t, int) else buf[:, ds(t, 1)].rearrange("p a d -> p (a d)")

    def columns(t):
        return slice(t * P, (t + 1) * P) if isinstance(t, int) else ds(t * P, P)

    @block.sync
    def _(eng):
        def bcast(dst, section, got):
            for s in range(2):
                src = io["modrow"][s, (section - 2) * D:(section - 1) * D].unsqueeze(0).to_broadcast([P, D])
                eng.dma_start(dst[:, s], src).then_inc(got, 16)

        eng.dma_start(z[:, CT:KT], io["ypool"]).then_inc(y_in, 16)
        eng.dma_start(wo_late[:], io["w_out"].rearrange("(k p) n -> p k n", p=P)[:, KT - NLATE:]).then_inc(wo_in, 16)
        bcast(gt1, 2, res_in)
        x_v = io["x_all"].rearrange("(t p) d -> p t d", p=P)
        eng.dma_start(x1[:, 0:1], x_v[:, 0:1]).then_inc(res_in, 16)
        bcast(gn2, 4, norm_in)
        eng.dma_start(nrm2[:], io["norm2"].unsqueeze(0).to_broadcast([P, D])).then_inc(norm_in, 16)
        bcast(sh2, 3, norm_in)
        eng.dma_start(wr[:], io["w_router"].rearrange("(k p) n -> p k n", p=P)).then_inc(norm_in, 16)
        eng.dma_start(x1[:, 1:NT], x_v[:, 1:NT]).then_inc(latent_in, 16)

        def store(t):
            eng.wait_ge(norm_chain, t * V_NORM + V_H2)
            dst = io["h2"][t * P:(t + 1) * P] if isinstance(t, int) else io["h2"][ds(t * P, P)]
            eng.dma_start(dst, h2[:]).then_inc(h2_out, 16)

        store(0)
        with eng.Fori(1, NT) as t:
            store(t)
        eng.wait_ge(prT_done, NT + 1)
        eng.dma_start(io["probsT"], prT[:]).then_inc(prT_out, 16)
        eng.wait_ge(prT_out, 16)
        eng.wait_ge(h2_out, 16 * NT)

    @block.gpsimd
    def _(eng):
        eng.memset(prT[:], 0.0).then_inc(prT_done, 1)

    @block.tensor
    def _(eng):
        def main(t):
            if not isinstance(t, int) or t > 0:
                eng.wait_ge(norm_chain, (t - 1) * V_NORM + V_TAKEN)
            for half in range(2):
                eng.wait_ge(y_static, 2 * t + half + 1)
                if isinstance(t, int) and t == 0 and half == 1:
                    eng.wait_ge(wo_in, 16)
                for k in range(half * HK, (half + 1) * HK):
                    wo = z[:, WO_TILES[k]] if k < KT - NLATE else wo_late[:, k - (KT - NLATE)]
                    for n in range(2):
                        ins = eng.matmul(ps_m[:, n], yT[:, k], wo[:, n * 512:(n + 1) * 512], start=(k == 0), stop=(k == KT - 1))
                ins.then_inc(m_half if half == 0 else m_done, 1)

        def turn(t):
            eng.wait_ge(norm_chain, t * V_NORM + V_H2)
            for k in range(KT):
                ins = eng.transpose(ps_h[:, k // 4, (k % 4) * P:(k % 4 + 1) * P], h2[:, k * P:(k + 1) * P], ident)
            ins.then_inc(h2_turned, 1)

        def route(t):
            eng.wait_ge(h2T_done, t + 1)
            for k in range(KT):
                ins = eng.matmul(ps_r[:, 0:NE], h2T[:, k], wr[:, k], start=(k == 0), stop=(k == KT - 1))
            ins.then_inc(logits, 1)

        def turn_probs(t):
            eng.wait_ge(soft_chain, t * V_SOFT + V_SOFT)
            eng.transpose(ps_pt[0:NE, 0:P], ex[:], ident).then_inc(pr_turned, 1)

        main(0)
        main(1)
        turn(0)
        eng.wait_ge(norm_in, 96)
        route(0)
        with eng.Fori(2, NT) as t:
            main(t)
            turn(t - 1)
            turn_probs(t - 2)
            route(t - 1)
        turn(NT - 1)
        turn_probs(NT - 2)
        route(NT - 1)
        turn_probs(NT - 1)

    @block.scalar
    def _(eng):
        def take_y(t, half):
            if not isinstance(t, int) or t > 0:
                eng.wait_ge(m_half if half == 0 else m_done, t)
            eng.activation(yT[:, half * HK:(half + 1) * HK], z[:, half * HK:(half + 1) * HK, columns(t)],
                           ACT.Copy).then_inc(y_static, 1)

        def squares(t):
            eng.wait_ge(norm_chain, t * V_NORM + V_X1)
            eng.activation(tmp[:], tile_of(x1, t), ACT.Square, accum_out=st8[:, 0:1]).then_inc(x1_sq, 1)

        def root(t):
            eng.wait_ge(norm_chain, t * V_NORM + V_MS)
            eng.activation(st8[:, 2:3], st8[:, 1:2], ACT.Sqrt).then_inc(x1_sq, 1)

        def take_h2T(t):
            eng.wait_ge(h2_turned, t + 1)
            eng.activation(h2T[:].rearrange("p (a k) c -> p a (k c)", a=2), ps_h[:], ACT.Copy).then_inc(h2T_done, 1)

        def exp(t):
            eng.wait_ge(soft_chain, t * V_SOFT + V_MAX)
            eng.activation(ex[:], ps_r[:, 0:NE], ACT.Exp, bias=sm[:, 0:1], accum_out=sm[:, 1:2]).then_inc(exps, 1)

        def take_probs(t):
            eng.wait_ge(pr_turned, t + 1)
            eng.activation(prT[0:NE, columns(t)], ps_pt[0:NE, 0:P], ACT.Copy).then_inc(prT_done, 1)

        take_y(0, 0)
        eng.wait_ge(y_in, 16)
        take_y(0, 1)
        eng.wait_ge(prT_done, 1)
        for half in range(2):
            take_y(1, half)
        squares(0)
        root(0)
        for half in range(2):
            take_y(2, half)
        take_h2T(0)
        squares(1)
        exp(0)
        root(1)
        with eng.Fori(2, NT - 1) as t:
            for half in range(2):
                take_y(t + 1, half)
            take_h2T(t - 1)
            take_probs(t - 2)
            squares(t)
            exp(t - 1)
            root(t)
        take_h2T(NT - 2)
        take_probs(NT - 3)
        squares(NT - 1)
        exp(NT - 2)
        root(NT - 1)
        take_h2T(NT - 1)
        take_probs(NT - 2)
        exp(NT - 1)
        take_probs(NT - 1)

    @block.vector
    def _(eng):
        def residual(t, s, ch):
            eng.wait_ge(m_done, t + 1)
            ch(eng.tensor_tensor(tmp[:], ps_m[:].rearrange("p a c -> p (a c)"), gt1[:, s], ALU.mult))
            ch(eng.tensor_tensor(tile_of(x1, t), tile_of(x1, t), tmp[:], ALU.add))

        def mean_square(t, ch):
            eng.wait_ge(x1_sq, 2 * t + 1)
            ch(eng.tensor_scalar(st8[:, 1:2], st8[:, 0:1], 1.0 / D, RMS_EPS, ALU.mult, ALU.add))

        def norm(t, s, ch):
            eng.wait_ge(x1_sq, 2 * t + 2)
            ch(eng.reciprocal(st8[:, 3:4], st8[:, 2:3]))
            if not isinstance(t, int) or t > 0:
                eng.wait_ge(h2_out, 16 * t)
                eng.wait_ge(h2_turned, t)
            ch(eng.scalar_tensor_tensor(h2[:], tile_of(x1, t), st8[:, 3:4], gn2[:, s], ALU.mult, ALU.mult))
            ch(eng.tensor_tensor(h2[:], h2[:], sh2[:, s], ALU.add))

        def highest(t, so):
            eng.wait_ge(logits, t + 1)
            so(eng.tensor_reduce(sm[:, 0:1], ps_r[:, 0:NE], AXX, ALU.max, negate=True))

        def softmax(t, so):
            eng.wait_ge(exps, t + 1)
            so(eng.reciprocal(sm[:, 2:3], sm[:, 1:2]))
            pt = probs[:, t, 0:NE] if isinstance(t, int) else probs[:, ds(t, 1), 0:NE].rearrange("p a e -> p (a e)")
            eng.tensor_scalar(pt, ex[:], sm[:, 2:3], None, ALU.mult).then_inc(pr_kept, 1)
            eng.wait_ge(pr_kept, t + 1)
            so(eng.tensor_scalar(ex[:], ex[:], sm[:, 2:3], None, ALU.mult))

        def step(t, s):
            ch = Chain(eng, norm_chain, t * V_NORM)
            so = Chain(eng, soft_chain, (t - 1) * V_SOFT)
            residual(t, s, ch)
            highest(t - 1, so)
            mean_square(t, ch)
            softmax(t - 1, so)
            norm(t, s, ch)

        eng.memset(probs[:], 0.0)
        eng.wait_ge(res_in, 48)
        ch = Chain(eng, norm_chain)
        residual(0, 0, ch)
        mean_square(0, ch)
        eng.wait_ge(norm_in, 96)
        rc = Chain(eng, row_chain)
        for s in range(2):
            rc(eng.scalar_tensor_tensor(gn2[:, s], gn2[:, s], 1.0, nrm2[:], ALU.add, ALU.mult))
        norm(0, 0, ch)
        eng.wait_ge(latent_in, 16)
        step(1, 1)
        with eng.Fori(2, NT) as t:
            step(t, 1)
        so = Chain(eng, soft_chain, (NT - 1) * V_SOFT)
        highest(NT - 1, so)
        softmax(NT - 1, so)


NCHUNK = 4
FC = DE // NCHUNK
FT = FC // P


def expert_phase(nc, st, io, keep):
    sb = lambda n, s, dt=F32: st.enter_context(nc.sbuf_tensor(n, s, dt))
    ps = lambda n, s: st.enter_context(nc.psum_tensor(n, s, F32))
    sem = lambda n: st.enter_context(nc.semaphore(n))
    cst, probs = keep["cst"], keep["probs"]
    ident = cst[:, 0:P]
    tie, slot, tokid = (cst[:, CCOLS[n][0]:CCOLS[n][1]] for n in ("tie", "slot", "tokid"))

    w1c = sb("w1c", [P, 2, KT, FC])
    w3c = sb("w3c", [P, 2, KT, FC])
    w2c = sb("w2c", [P, 2, FT, D])
    prow = sb("prow", [P, NTOK])
    pcol = sb("pcol", [P, NT])
    cnts = sb("cnts", [P, NT, 3])
    rank = sb("rank", [P, NT])
    before = sb("before", [P, DEC - P])
    after = sb("after", [P, DEC])
    same = sb("same", [P, P])
    hot = sb("hot", [P, NT, P])
    pick = sb("pick", [P, NT, 2])
    gate_s = sb("gate_s", [P, 2, 1])
    gate_p = sb("gate_p", [CAP_P, 2, 1])
    idx_s = sb("idx_s", [P, 2, 1], U32)
    idx_p = sb("idx_p", [CAP_P, 2, 1], U32)
    xs = sb("xs", [P, D])
    xp = sb("xp", [CAP_P, D])
    xT = sb("xT", [P, KT, SLOTS])
    sig = sb("sig", [P, 2, SLOTS])
    u = sb("u", [P, 2, SLOTS])
    he = sb("he", [P, 2, FT, SLOTS])
    yT = sb("yeT", [P, KT, SLOTS])
    ys = sb("ys", [P, D])
    yp = sb("ye_p", [CAP_P, D])

    ps_y = ps("ps_ye", [P, 3, 512])
    ps_h = [ps(f"ps_h{i}", [P, 512]) for i in range(2)]
    ps_t = ps("ps_te", [P, 2, 512])
    ps_i = ps("ps_i", [P, 512])

    w13_in = [sem(f"w13_in{b}") for b in range(2)]
    w2_in = [sem(f"w2_in{b}") for b in range(2)]
    down_done = sem("down_done")
    prow_in = sem("prow_in")
    route_v = sem("route_v")
    route_pe = sem("route_pe")
    ids_done = sem("ids_done")
    gathered = sem("gathered")
    x_turned = sem("x_turned_e")
    xT_done = sem("xT_done")
    up_ps = sem("up_ps")
    sig_done = sem("sig_done")
    u_done = sem("u_done")
    he_done = sem("he_done")
    yT_done = sem("yT_done")
    y_turned = sem("y_turned")
    y_scaled = sem("y_scaled")
    scattered = sem("scattered")

    kept = sem("kept")
    acc_free = sem("acc_free")
    last_in = sem("last_in")
    sync_began = sem("sync_began")
    rank_done = sem("rank_done")
    pool_began = sem("pool_began")
    V_RANK = 3
    w1v = io["w1"].rearrange("e (k p) f -> e p k f", p=P)
    w3v = io["w3"].rearrange("e (k p) f -> e p k f", p=P)
    w2v = io["w2"].rearrange("e (t p) d -> e p t d", p=P)
    yps = lambda k: ps_y[:, k // 3, (k % 3) * SLOTS:(k % 3 + 1) * SLOTS]

    block = st.enter_context(nc.Block())

    @block.sync
    def _(eng):
        sl = lambda v, e: v[ds(e, 1)].rearrange("o p k f -> (o p) k f")

        def load_up(e, c, which=(0, 1)):
            new, c0 = c // NCHUNK, c % NCHUNK
            b = c % 2
            if not isinstance(e, int) or e > 0 or c >= 2:
                eng.wait_ge(up_ps, (e * NCHUNK + c - 1) * FT)
            for n in which:
                dst, src = ((w1c, w1v), (w3c, w3v))[n]
                eng.dma_start(dst[:, b], sl(src[new:], e)[:, :, c0 * FC:(c0 + 1) * FC]).then_inc(w13_in[b], 16)

        def load_down(e, c):
            if not isinstance(e, int) or e > 0 or c >= 2:
                eng.wait_ge(down_done, e * NCHUNK + c - 1)
                eng.sem_inc(sync_began, 1)
            eng.dma_start(w2c[:, c % 2], sl(w2v, e)[:, c * FT:(c + 1) * FT]).then_inc(w2_in[c % 2], 16)

        def expert(e, more):
            for c in range(NCHUNK):
                if c < NCHUNK - 1 or more:
                    load_up(e, c + 1, (1,) if isinstance(e, int) and e + c == 0 else (0, 1))
                load_down(e, c)

        eng.wait_ge(prow_in, 16)
        load_up(0, 0)
        load_up(0, 1, (0,))
        eng.wait_ge(gathered, 32)
        expert(0, True)
        for s in range(2):
            eng.dma_start(keep["gt2"][:, s], io["modrow"][s, 3 * D:4 * D].unsqueeze(0).to_broadcast([P, D])).then_inc(last_in, 16)
        eng.dma_start(keep["nf"][:], io["norm_f"].unsqueeze(0).to_broadcast([P, D])).then_inc(last_in, 16)
        with eng.Fori(1, NE - 1) as e:
            expert(e, True)
        expert(NE - 1, False)
        eng.wait_ge(last_in, 48)

    @block.scalar
    def _(eng):
        def row(e):
            src = io["probsT"][e:e + 1] if isinstance(e, int) else io["probsT"][ds(e, 1)]
            eng.dma_start(prow[:], src.to_broadcast([P, NTOK])).then_inc(prow_in, 16)

        def take_x(e):
            eng.wait_ge(x_turned, e + 1)
            eng.activation(xT[:, :, 0:CAP_S].rearrange("p (a k) c -> p a k c", a=2),
                           ps_t[:].rearrange("p a (k c) -> p a k c", c=P), ACT.Copy)
            eng.activation(xT[:, :, CAP_S:SLOTS], ps_i[:, 0:KT * CAP_P].rearrange("p (k c) -> p k c", c=CAP_P),
                           ACT.Copy).then_inc(xT_done, 1)

        def take_y(e):
            eng.wait_ge(down_done, (e + 1) * NCHUNK)
            for j in range(3):
                k0, k1 = 3 * j, min(3 * j + 3, KT)
                ins = eng.activation(yT[:, k0:k1], ps_y[:, j, 0:(k1 - k0) * SLOTS].rearrange("p (k c) -> p k c", c=SLOTS), ACT.Copy)
            ins.then_inc(yT_done, 1)

        def scale(e, part):
            dst, g, n = ((ys, gate_s, P), (yp, gate_p, CAP_P))[part]
            eng.wait_ge(y_turned, 2 * e + part + 1)
            if part == 0:
                eng.wait_ge(kept, e + 1)
            eng.activation(dst[:].rearrange("p (a c) -> p a c", a=2), ps_t[0:n], ACT.Copy,
                           scale=g[:, 0]).then_inc(y_scaled, 1)

        def expert(e, more):
            eng.wait_ge(rank_done, e * NT + NT)
            row(e + 1)
            if more:
                take_y(e - 1)
            for f in range(NCHUNK * FT):
                n = e * (NCHUNK * FT) + f + 1
                eng.wait_ge(up_ps, n)
                eng.activation(sig[:, f % 2], ps_h[f % 2][:, 0:SLOTS], ACT.Sigmoid).then_inc(sig_done, 1)
                if more and f in (FT - 1, 2 * FT - 1):
                    scale(e - 1, f // FT)
            take_x(e + 1)

        row(0)
        take_x(0)
        expert(0, False)
        with eng.Fori(1, NE) as e:
            expert(e, True)
        take_y(NE - 1)
        for part in range(2):
            scale(NE - 1, part)

    @block.gpsimd
    def _(eng):
        eng.sem_inc(acc_free, 1)

        def gather(e):
            eng.wait_ge(ids_done, e + 1)
            if not isinstance(e, int) or e > 0:
                eng.wait_ge(x_turned, e)
                eng.sem_inc(pool_began, 1)
            eng.indirect_dma_start(xs[:], None, io["h2"], bass.IndirectOffsetOnAxis(ap=idx_s[:, 0], axis=0)).then_inc(gathered, 16)
            eng.indirect_dma_start(xp[:], None, io["h2"], bass.IndirectOffsetOnAxis(ap=idx_p[:, 0], axis=0)).then_inc(gathered, 16)

        def scatter(e):
            eng.wait_ge(y_scaled, 2 * e + 2)
            eng.sem_inc(pool_began, 1)
            eng.indirect_dma_start(io["acc"], bass.IndirectOffsetOnAxis(ap=idx_s[:, 1], axis=0), ys[:], None,
                                   compute_op=ALU.add).then_inc(scattered, 16)
            eng.indirect_dma_start(io["acc"], bass.IndirectOffsetOnAxis(ap=idx_p[:, 1], axis=0), yp[:], None,
                                   compute_op=ALU.add).then_inc(scattered, 16)
            eng.wait_ge(scattered, 32 * e + 32)
            eng.sem_inc(acc_free, 1)

        gather(0)
        gather(1)
        with eng.Fori(1, NE) as e:
            scatter(e - 1)
            gather(e + 1)
        scatter(NE - 1)
        eng.wait_ge(gathered, 32 * NE + 32)

    @block.vector
    def _(eng):
        def route_begin(e):
            eng.wait_ge(prow_in, 16 * e + 16)
            column = probs[:, :, e] if isinstance(e, int) else probs[:, :, ds(e, 1)].rearrange("p t o -> p (t o)")
            eng.tensor_copy(pcol[:], column)
            eng.tensor_copy(pick[:, :, 1], column)
            eng.memset(cnts[:], 0.0).then_inc(route_v, 1)
            eng.wait_ge(route_v, e * V_RANK + 1)

        def route_rank(e, t):
            if isinstance(e, int) and t == 0:
                pass
            else:
                eng.wait_ge(rank_done, e * NT + t)
            lo, hi = (0, SEQ) if t == 0 else (SEQ, NTOK)
            me = t * P
            p = pcol[:, t:t + 1]
            if me > lo:
                eng.tensor_scalar(before[:, 0:me - lo], prow[:, lo:me], p, None, ALU.is_ge, ALU.add, accum_out=cnts[:, t, 0:1])
            eng.tensor_scalar(after[:, 0:hi - me], prow[:, me:hi], p, None, ALU.is_gt, ALU.add, accum_out=cnts[:, t, 1:2])
            ins = eng.scalar_tensor_tensor(same[:], prow[:, me:me + P], p, tie, ALU.is_equal, ALU.mult,
                                           accum_out=cnts[:, t, 2:3])
            ins.then_inc(rank_done, 1)

        def route_end(e):
            eng.wait_ge(rank_done, e * NT + NT)
            eng.tensor_reduce(rank[:], cnts[:], AXX, ALU.add).then_inc(route_v, 1)
            eng.wait_ge(route_v, e * V_RANK + 2)
            for t in range(NT):
                ins = eng.tensor_scalar(hot[:, t], slot, rank[:, t:t + 1], None, ALU.is_equal)
            ins.then_inc(route_v, 1)

        def ids(e):
            eng.wait_ge(route_pe, e + 1)
            eng.tensor_copy(gate_s[:, 1], ps_i[:, 257:258])
            eng.tensor_copy(gate_p[:, 1], ps_i[0:CAP_P, 259:260])
            eng.tensor_copy(idx_s[:, 0], ps_i[:, 256:257])
            eng.tensor_copy(idx_p[:, 0], ps_i[0:CAP_P, 258:259]).then_inc(ids_done, 1)

        eng.tensor_copy(pick[:, :, 0], tokid)
        eng.sem_inc(he_done, 2)
        route_begin(0)
        for t in range(NT):
            route_rank(0, t)
        route_end(0)
        ids(0)

        def keep_ids(e):
            eng.wait_ge(acc_free, e + 1)
            eng.wait_ge(gathered, 32 * e + 32)
            eng.tensor_copy(gate_s[:, 0], gate_s[:, 1])
            eng.tensor_copy(gate_p[:, 0], gate_p[:, 1])
            eng.tensor_copy(idx_s[:, 1], idx_s[:, 0])
            eng.tensor_copy(idx_p[:, 1], idx_p[:, 0]).then_inc(kept, 1)
            eng.wait_ge(kept, e + 1)
            ids(e + 1)

        with eng.Fori(0, NE) as e:
            for f in range(NCHUNK * FT):
                if f == 0:
                    route_begin(e + 1)
                n = e * (NCHUNK * FT) + f + 1
                b = (f // FT) % 2
                eng.wait_ge(sig_done, n)
                eng.tensor_tensor(u[:, f % 2], ps_h[f % 2][:, 0:SLOTS], sig[:, f % 2], ALU.mult).then_inc(u_done, 1)
                eng.wait_ge(u_done, n)
                eng.tensor_tensor(he[:, b, f % FT], ps_h[f % 2][:, SLOTS:2 * SLOTS], u[:, f % 2], ALU.mult).then_inc(he_done, 1)
                if f < NT:
                    route_rank(e + 1, f)
                if f == NT:
                    route_end(e + 1)
                if f == 3 * FT:
                    keep_ids(e)

    @block.tensor
    def _(eng):
        def pick_ids(e):
            eng.wait_ge(route_v, e * V_RANK + V_RANK)
            for t in range(1, NT):
                eng.matmul(ps_i[:, 256:258], hot[:, t], pick[:, t], start=(t == 1), stop=(t == NT - 1))
            eng.matmul(ps_i[0:CAP_P, 258:260], hot[:, 0, 0:CAP_P], pick[:, 0], start=True, stop=True).then_inc(route_pe, 1)

        def turn_x(e):
            eng.wait_ge(gathered, 32 * e + 32)
            eng.wait_ge(ids_done, e + 1)
            for k in range(KT):
                eng.transpose(ps_t[:, k // 4, (k % 4) * P:(k % 4 + 1) * P], xs[:, k * P:(k + 1) * P], ident)
            for k in range(KT):
                ins = eng.transpose(ps_i[:, k * CAP_P:(k + 1) * CAP_P], xp[:, k * P:(k + 1) * P], ident[0:CAP_P, 0:CAP_P])
            ins.then_inc(x_turned, 1)

        def turn_y(e, part):
            eng.wait_ge(yT_done, e + 1)
            if part == 1:
                eng.wait_ge(y_scaled, 2 * e + 1)
            lo, hi = ((0, CAP_S), (CAP_S, SLOTS))[part]
            for k in range(KT):
                ins = eng.transpose(ps_t[0:hi - lo, k // 4, (k % 4) * P:(k % 4 + 1) * P], yT[:, k, lo:hi], ident)
            ins.then_inc(y_turned, 1)

        def up(e, c):
            b = c % 2
            eng.wait_ge(w13_in[b], 64 * e + 32 * (c // 2) + 32)
            for f in range(FT):
                g = c * FT + f
                eng.wait_ge(he_done, e * (NCHUNK * FT) + g + 1)
                for w, off in ((w1c, 0), (w3c, SLOTS)):
                    for k in range(KT):
                        ins = eng.matmul(ps_h[g % 2][:, off:off + SLOTS], w[:, b, k, f * P:(f + 1) * P], xT[:, k],
                                         start=(k == 0), stop=(k == KT - 1))
                ins.then_inc(up_ps, 1)

        def down(e, c):
            b = c % 2
            eng.wait_ge(w2_in[b], 32 * e + 16 * (c // 2) + 16)
            eng.wait_ge(he_done, 2 + e * (NCHUNK * FT) + (c + 1) * FT)
            for f in range(FT):
                for k in range(KT):
                    ins = eng.matmul(yps(k), w2c[:, b, f, k * P:(k + 1) * P], he[:, b, f],
                                     start=(c == 0 and f == 0 and k % 3 == 0), stop=(c == NCHUNK - 1 and f == FT - 1),
                                     skip_group_check=True)
            ins.then_inc(down_done, 1)

        def expert(e, more):
            eng.wait_ge(xT_done, e + 1)
            up(e, 0)
            if more:
                turn_y(e - 1, 0)
            for c in range(1, NCHUNK):
                if c == NCHUNK - 1:
                    pick_ids(e + 1)
                up(e, c)
                down(e, c - 1)
                if more and c == 1:
                    turn_y(e - 1, 1)
            if more:
                eng.wait_ge(y_scaled, 2 * e)
            turn_x(e + 1)
            down(e, NCHUNK - 1)

        pick_ids(0)
        turn_x(0)
        expert(0, False)
        with eng.Fori(1, NE) as e:
            expert(e, True)
        turn_y(NE - 1, 0)
        turn_y(NE - 1, 1)


def final_phase(nc, st, io, keep):
    sb = lambda n, s, dt=F32: st.enter_context(nc.sbuf_tensor(n, s, dt))
    sem = lambda n: st.enter_context(nc.semaphore(n))
    x1 = keep["wide"][:].rearrange("p (t c) -> p t c", t=NT)
    gt2, nf = keep["gt2"], keep["nf"]
    acc = sb("acc_sb", [P, NT, D])
    tmp = sb("ftmp", [P, D])
    out = sb("fout", [P, 2, D])
    s4 = sb("fs4", [P, NT, 4])
    acc_in = [sem(f"acc_in{t}") for t in range(NT)]
    gated = sem("gated")
    summed = sem("summed")
    fin_chain = sem("fin_chain")
    fin_act = sem("fin_act")
    stored = [sem(f"stored{b}") for b in range(2)]
    V_MS, V_OUT, V_ALL = 1, 3, 3
    POOL_TILES = list(range(2, NT, 3))
    OWN_TILES = [t for t in range(NT) if t not in POOL_TILES]
    block = st.enter_context(nc.Block())

    @block.sync
    def _(eng):
        for t in range(NT):
            eng.dma_start(acc[:, t], io["acc"][t * P:(t + 1) * P]).then_inc(acc_in[t], 16)
        for t in range(NT):
            eng.wait_ge(fin_chain, t * V_ALL + V_OUT)
            eng.dma_start(io["y_out"][t * P:(t + 1) * P], out[:, t % 2]).then_inc(stored[t % 2], 16)
        for b in range(2):
            eng.wait_ge(stored[b], 16 * ((NT + 1 - b) // 2))

    @block.gpsimd
    def _(eng):
        for n, t in enumerate(POOL_TILES):
            eng.wait_ge(acc_in[t], 16)
            eng.tensor_tensor(acc[:, t], acc[:, t], gt2[:, 1], ALU.mult).then_inc(gated, 1)
            eng.wait_ge(gated, 2 * n + 1)
            eng.tensor_tensor(acc[:, t], acc[:, t], x1[:, t], ALU.add).then_inc(gated, 1)

    @block.vector
    def _(eng):
        def residual(t):
            if t in POOL_TILES:
                return
            eng.wait_ge(acc_in[t], 16)
            eng.tensor_tensor(acc[:, t], acc[:, t], gt2[:, min(t, 1)], ALU.mult).then_inc(summed, 1)
            eng.wait_ge(summed, 2 * OWN_TILES.index(t) + 1)
            eng.tensor_tensor(acc[:, t], acc[:, t], x1[:, t], ALU.add).then_inc(summed, 1)

        def norm(t):
            ch = Chain(eng, fin_chain, t * V_ALL)
            eng.wait_ge(fin_act, 2 * t + 1)
            ch(eng.tensor_scalar(s4[:, t, 1:2], s4[:, t, 0:1], 1.0 / D, RMS_EPS, ALU.mult, ALU.add))
            eng.wait_ge(fin_act, 2 * t + 2)
            ch(eng.reciprocal(s4[:, t, 3:4], s4[:, t, 2:3]))
            if t >= 2:
                eng.wait_ge(stored[t % 2], 16 * (t // 2))
            ch(eng.scalar_tensor_tensor(out[:, t % 2], acc[:, t], s4[:, t, 3:4], nf[:], ALU.mult, ALU.mult))

        residual(0)
        for t in range(1, NT):
            residual(t)
            norm(t - 1)
        norm(NT - 1)

    @block.scalar
    def _(eng):
        for t in range(NT):
            if t in POOL_TILES:
                eng.wait_ge(gated, 2 * POOL_TILES.index(t) + 2)
            else:
                eng.wait_ge(summed, 2 * OWN_TILES.index(t) + 2)
            eng.activation(tmp[:], acc[:, t], ACT.Square, accum_out=s4[:, t, 0:1]).then_inc(fin_act, 1)
            eng.wait_ge(fin_chain, t * V_ALL + V_MS)
            eng.activation(s4[:, t, 2:3], s4[:, t, 1:2], ACT.Sqrt).then_inc(fin_act, 1)


def build(nc, io):
    dram = lambda n, s: nc.dram_tensor(n, s, F32).ap()
    io["modrow"] = dram("modrow", [2, 4 * D])
    io["ypool"] = dram("ypool", [P, len(WINDOWS), NTOK])
    io["h2"] = dram("h2", [NTOK, D])
    io["probsT"] = dram("probsT", [NE + 1, NTOK])
    io["acc"] = dram("acc", [NTOK, D])
    with ExitStack() as st:
        sb = lambda s, n, shape: s.enter_context(nc.sbuf_tensor(n, shape, F32))
        keep = {"cst": sb(st, "cst", [P, NCONST]), "probs": sb(st, "probs", [P, NT, NE + 1])}
        assert KT * NTOK == NT * D and 4 * 2 * NTOK == NT * D
        keep["wide"] = sb(st, "wide", [P, NT * D])
        with ExitStack() as front:
            keep["par"] = sb(front, "par", [P, NPARAM])
            keep["z"] = sb(front, "z", [P, NZ, NTOK])
            with ExitStack() as early:
                keep["zpool"] = sb(early, "zpool", [P, 4, NTOK])
                with ExitStack() as s:
                    project_phase(nc, s, io, keep)
            with ExitStack() as s:
                scan_phase(nc, s, io, keep)
            with ExitStack() as s:
                output_phase(nc, s, io, keep)
        keep["gt2"] = sb(st, "gt2", [P, 2, D])
        keep["nf"] = sb(st, "nf", [P, D])
        with ExitStack() as s:
            expert_phase(nc, s, io, keep)
        with ExitStack() as s:
            final_phase(nc, s, io, keep)


def constants():
    c = np.zeros((P, NCONST), np.float32)

    def put(name, a):
        c[:, CCOLS[name][0]:CCOLS[name][1]] = a.reshape(P, -1)

    i = np.arange(P)
    put("ident", np.eye(P, dtype=np.float32))
    put("blk", (i[:, None] // HS == i[None] // HS).astype(np.float32))
    j = i[:, None]
    t = i[None]
    put("eye", (j % HS == t[:, :HS]).astype(np.float32))
    lvl = np.zeros((P, 2, LEVELS, CH), np.float32)
    mask = np.zeros((P, 2, 3, CH), np.float32)
    for d, (strict, incl) in enumerate(((j < t, j <= t), (j > t, j >= t))):
        for lv in range(LEVELS):
            s = 1 << lv
            lvl[:, d, lv] = strict & (j // (2 * s) == t // (2 * s)) & (j // s != t // s)
        for k in range(3):
            mask[:, d, k] = incl if k % 2 else strict
    put("lvl", lvl)
    put("mask", mask)
    put("tie", (i[None] < i[:, None]).astype(np.float32))
    put("slot", np.broadcast_to(i[None].astype(np.float32), (P, P)))
    put("tokid", (i[:, None] + P * np.arange(NT)[None]).astype(np.float32))
    reset = (np.arange(NTOK) % CH != 0).astype(np.float32)
    inv = np.zeros((len(WINDOWS), NTOK), np.float32)

    def count(n, win):
        pos = np.arange(n)
        return (np.clip(pos + win - win // 2, 0, n) - np.clip(pos - win // 2, 0, n)).astype(np.float64)

    for g, win in enumerate(WINDOWS):
        inv[g, :SEQ] = 1.0 / count(SEQ, win)
        inv[g, SEQ:] = (1.0 / (count(ROWS, win)[:, None] * count(GRID_W, win)[None])).reshape(-1)
    return c, reset, inv


def kernel(**inputs):
    import concourse.bacc as bacc
    from concourse.bass_utils import run_bass_kernel_spmd

    a = {n: np.asarray(v) for n, v in inputs.items()}
    cols = lambda v: np.ascontiguousarray(v.reshape(-1, P).T)
    par = np.zeros((P, NPARAM), np.float32)
    par[:, 0:16:2] = cols(a["c_ctx"])
    par[:, 1:16:2] = cols(a["c"][0])
    for name, v in (("norm1", a["norm1"][0]), ("mu", a["mu_shift"][0]), ("pool_scale", a["pool_scale"][0])):
        par[:, PCOLS[name][0]:PCOLS[name][1]] = cols(v)
    for name, v in (("w0f", a["w0"][0, 0]), ("w0b", a["w0"][0, 1]), ("a0f", a["a0"][0, 0]), ("a0b", a["a0"][0, 1]),
                    ("k_k", a["k_k"][0]), ("k_a", a["k_a"][0]), ("r_k", a["r_k"][0]), ("ln_w", a["ln_x_w"][0]), ("ln_b", a["ln_x_b"][0])):
        lo = PCOLS["head"][0] + HP[name]
        par[:, lo:lo + 40:10] = cols(v)
    consts, reset, inv = constants()
    state0 = np.ascontiguousarray(a["state_rwkv"][0, 0].transpose(0, 1, 3, 2)).reshape(2, CT, P, HS)
    arrays = {
        "consts": consts, "params": par, "reset": reset, "inv_cnt": inv, "state0": state0,
        "x_all": np.concatenate([a["x_prompt"][0], a["x_sample"][0]]),
        "ada_w": a["ada_w"][0], "ada_b": a["ada_b"][0], "w_in": a["w_in"][0], "pool_w": a["pool_w"][0],
        "w_up": a["w_up"][0].reshape(P, DR), "a_up": a["a_up"][0].reshape(P, DR), "g_up": a["g_up"][0],
        "w_out": a["w_out"][0], "norm2": a["norm2"][0], "norm_f": a["norm_f"], "w_router": a["w_router"][0],
        "w1": a["w1"][0], "w3": a["w3"][0], "w2": a["w2"][0],
    }
    arrays = {n: np.ascontiguousarray(v) for n, v in arrays.items()}
    nc = bacc.Bacc("TRN2", target_bir_lowering=False, num_devices=1)
    io = {n: nc.dram_tensor(f"in_{n}", v.shape, F32, kind="ExternalInput").ap() for n, v in arrays.items()}
    io["y_out"] = nc.dram_tensor("out_y", [NTOK, D], F32, kind="ExternalOutput").ap()
    io["state_out"] = nc.dram_tensor("out_state", [2, CT, P, HS], F32, kind="ExternalOutput").ap()
    build(nc, io)
    r = run_bass_kernel_spmd(nc, [{f"in_{n}": v for n, v in arrays.items()}], core_ids=[0]).results[0]
    y = r["out_y"]
    state = r["out_state"].reshape(2, 2 * CT, HS, HS).transpose(0, 1, 3, 2)
    return y[None, :SEQ], y[None, SEQ:], np.ascontiguousarray(state)[None, None]
```
